# Optimizing a Trainium2 kernel written in Bass

```python
import math
import jax
import jax.numpy as jnp
from jax import lax
import numpy as np

D_MODEL = 1024
BATCH = 1
SEQ = 256
DEPTH = 2

CTX_LEN = 256
GRID_W = 64
EPS = 1e-6
ROPE_BASE = 10000.0

RET_HEADS = 4
RET_DK = 128
RET_DV = 256
RET_CHUNK = 128
RET_QK = RET_HEADS * RET_DK
RET_V = RET_HEADS * RET_DV

HY_WIDTH = 512
HY_ORDER = 2
HY_BANDS = 16
HY_EMB = 2 * HY_BANDS + 1
HY_FFN = 64
HY_DECAY_TARGET = 1e-2
HY_FAST_DECAY = 0.3
HY_SLOW_DECAY = 1.5

AB_SPLITS = (RET_QK, 2 * RET_QK, 2 * RET_QK + RET_V, 2 * RET_QK + 2 * RET_V)
AB_IN = 2 * RET_QK + 2 * RET_V + (HY_ORDER + 1) * HY_WIDTH
AB_CAT = RET_V + HY_WIDTH

DA_HEADS = 8
DA_HEAD_DIM = 64
DA_WIDTH = DA_HEADS * 2 * DA_HEAD_DIM
Q_BLOCK = 128

N_EXPERTS = 64
TOP_K = 8
N_GROUPS = 8
TOPK_GROUPS = 4
EXPERT_DIM = 256
SHARED_DIM = 256
ROUTED_SCALE = 2.5
MOE_BLOCK = 128

kernel_name = "hybrid_retention_hyena_diffattn_moe_dit"

F32 = jnp.float32

def rmsnorm(x, g, eps=EPS):
    xf = x.astype(F32)
    y = xf * lax.rsqrt(jnp.mean(xf * xf, axis=-1, keepdims=True) + eps)
    return (y * g.astype(F32)).astype(x.dtype)

def head_norm(r, eps=EPS):
    mu = jnp.mean(r, axis=-1, keepdims=True)
    var = jnp.mean(jnp.square(r - mu), axis=-1, keepdims=True)
    return (r - mu) * lax.rsqrt(var + eps)

def swiglu(x, wg, wu, wd):
    return (jax.nn.silu(x @ wg) * (x @ wu)) @ wd

def axial_rope(rows, head_dim):
    n_freq = head_dim // 4
    inv = ROPE_BASE ** (-jnp.arange(n_freq, dtype=F32) / n_freq)
    row = jnp.repeat(jnp.arange(rows, dtype=F32), GRID_W)
    col = jnp.tile(jnp.arange(GRID_W, dtype=F32), rows)
    ang = jnp.concatenate([row[:, None] * inv, col[:, None] * inv], axis=-1)
    return jnp.cos(ang), jnp.sin(ang)

def apply_rope(x, cos, sin):
    shape = (1, x.shape[1]) + (1,) * (x.ndim - 3) + (cos.shape[-1],)
    cos = cos.reshape(shape).astype(x.dtype)
    sin = sin.reshape(shape).astype(x.dtype)
    x1, x2 = jnp.split(x, 2, axis=-1)
    return jnp.concatenate([x1 * cos - x2 * sin, x2 * cos + x1 * sin], axis=-1)

def retention_scan(q, k, v, log_g, s0):
    B, L, H, dk = q.shape
    dv = v.shape[-1]
    n = L // RET_CHUNK
    qc = q.reshape(B, n, RET_CHUNK, H, dk)
    kc = k.reshape(B, n, RET_CHUNK, H, dk)
    vc = v.reshape(B, n, RET_CHUNK, H, dv)
    i = jnp.arange(RET_CHUNK, dtype=F32)
    rel = i[:, None] - i[None, :]
    dec_in = jnp.where(rel[..., None] >= 0, jnp.exp(jnp.maximum(rel, 0.0)[..., None] * log_g), 0.0)
    s = jnp.einsum('bnihd,bnjhd->bnhij', qc, kc) * dec_in.transpose(2, 0, 1)
    inner = jnp.einsum('bnhij,bnjhe->bnihe', s, vc)
    q_dec = jnp.exp((i + 1.0)[:, None] * log_g)
    k_dec = jnp.exp((RET_CHUNK - 1.0 - i)[:, None] * log_g)
    upd = jnp.einsum('bnjhd,bnjhe->nbhde', kc * k_dec[:, :, None], vc)
    g_chunk = jnp.exp(RET_CHUNK * log_g)[None, :, None, None]

    def step(state, u):
        return g_chunk * state + u, state

    s_final, s_prev = lax.scan(step, s0, upd)
    cross = jnp.einsum('bnihd,nbhde->bnihe', qc * q_dec[:, :, None], s_prev)
    return (inner + cross).reshape(B, L, H, dv), s_final

def bidir_retention(qc, kc, vc, qx, kx, vx, log_g):
    B = qc.shape[0]
    z = jnp.zeros((B, RET_HEADS, RET_DK, RET_DV), F32)
    flip = lambda a: a[:, ::-1]
    yc_f, sc_f = retention_scan(qc, kc, vc, log_g[0], z)
    yx_f, _ = retention_scan(qx, kx, vx, log_g[0], sc_f)
    yc_b, sc_b = retention_scan(flip(qc), flip(kc), flip(vc), log_g[1], z)
    yx_b, _ = retention_scan(flip(qx), flip(kx), flip(vx), log_g[1], sc_b)
    return yc_f + flip(yc_b), yx_f + flip(yx_b)

def short_conv(u, w, b):
    up = jnp.pad(u, ((0, 0), (1, 1), (0, 0)))
    return up[:, :-2] * w[0] + up[:, 1:-1] * w[1] + up[:, 2:] * w[2] + b

def hyena_filters(L, w1, b1, f1, w2, b2, f2, w3):
    t = jnp.arange(L, dtype=F32)
    t_norm = t / max(L - 1, 1)
    bands = jnp.linspace(1e-4, HY_BANDS - 1, HY_BANDS, dtype=F32)
    ang = (2.0 * math.pi / L) * t[:, None] * bands[None, :]
    z = jnp.concatenate([t_norm[:, None], jnp.cos(ang), -jnp.sin(ang)], axis=-1)
    h = jnp.sin(f1 * (z @ w1 + b1))
    h = jnp.sin(f2 * (h @ w2 + b2))
    h = (h @ w3).astype(F32)
    deltas = jnp.abs(jnp.linspace(math.log(HY_DECAY_TARGET) / HY_SLOW_DECAY,
                                  math.log(HY_DECAY_TARGET) / HY_FAST_DECAY, HY_WIDTH, dtype=F32))
    window = jnp.exp(-t_norm[:, None] * deltas[None, :])
    return h.reshape(L, HY_ORDER, 2, HY_WIDTH) * window[:, None, None, :]

def bidir_long_conv(u, h_fwd, h_bwd, skip):
    L, C = h_fwd.shape
    hc = jnp.concatenate([h_fwd, jnp.zeros((1, C), F32), h_bwd[1:][::-1]], axis=0)
    uf = u.astype(F32)
    U = jnp.fft.rfft(uf, n=2 * L, axis=1)
    Hf = jnp.fft.rfft(hc, axis=0)
    y = jnp.fft.irfft(U * Hf[None], n=2 * L, axis=1)[:, :L]
    return (y + uf * skip.astype(F32)).astype(u.dtype)

def hyena(u3, conv_w, conv_b, filt, skip):
    u3 = short_conv(u3, conv_w, conv_b)
    v, x1, x2 = jnp.split(u3, 3, axis=-1)
    y = x1 * bidir_long_conv(v, filt[:, 0, 0], filt[:, 0, 1], skip[0])
    y = x2 * bidir_long_conv(y, filt[:, 1, 0], filt[:, 1, 1], skip[1])
    return y

def mixer_ab(hc, hx, w_in, w_out, decay_logit, conv_w, conv_b, w1, b1, f1, w2, b2, f2, w3, skip, rope, with_ctx):
    qc, kc, vc, gc, uc = jnp.split(hc @ w_in, AB_SPLITS, axis=-1)
    qx, kx, vx, gx, ux = jnp.split(hx @ w_in, AB_SPLITS, axis=-1)

    def heads(q, k, v):
        B, L, _ = q.shape
        return (q.reshape(B, L, RET_HEADS, RET_DK).astype(F32),
                k.reshape(B, L, RET_HEADS, RET_DK).astype(F32) * RET_DK ** -0.5,
                v.reshape(B, L, RET_HEADS, RET_DV).astype(F32))

    qc, kc, vc = heads(qc, kc, vc)
    qx, kx, vx = heads(qx, kx, vx)
    cos, sin = rope
    qx, kx = apply_rope(qx, cos, sin), apply_rope(kx, cos, sin)
    log_g = jax.nn.log_sigmoid(decay_logit.astype(F32))
    rc, rx = bidir_retention(qc, kc, vc, qx, kx, vx, log_g)

    def merge(r, g, u):
        B, L = r.shape[:2]
        ret = head_norm(r).reshape(B, L, RET_V).astype(g.dtype) * jax.nn.silu(g)
        hy = hyena(u, conv_w, conv_b, hyena_filters(L, w1, b1, f1, w2, b2, f2, w3), skip)
        return jnp.concatenate([ret, hy], axis=-1) @ w_out

    yx = merge(rx, gx, ux)
    yc = merge(rc, gc, uc) if with_ctx else None
    return yc, yx

def mixer_da(hc, hx, w_in, w_out, lam, subln, lambda_init, rope, with_ctx):
    def heads(p):
        B, L, _ = p.shape
        q, k, v = jnp.split(p, 3, axis=-1)
        return (q.reshape(B, L, DA_HEADS, 2, DA_HEAD_DIM), k.reshape(B, L, DA_HEADS, 2, DA_HEAD_DIM),
                v.reshape(B, L, DA_HEADS, 2 * DA_HEAD_DIM))

    qc, kc, vc = heads(hc @ w_in)
    qx, kx, vx = heads(hx @ w_in)
    cos, sin = rope
    qx, kx = apply_rope(qx, cos, sin), apply_rope(kx, cos, sin)
    lam_f = lam.astype(F32)
    lam_full = jnp.exp(jnp.sum(lam_f[0] * lam_f[1])) - jnp.exp(jnp.sum(lam_f[2] * lam_f[3])) + lambda_init
    k_all = jnp.concatenate([kc, kx], axis=1)
    v_all = jnp.concatenate([vc, vx], axis=1)

    def attend(q, k, v):
        s = jnp.einsum('bqhcd,bkhcd->bhcqk', q, k).astype(F32) * DA_HEAD_DIM ** -0.5
        p = jax.nn.softmax(s, axis=-1)
        a = p[:, :, 0] - lam_full * p[:, :, 1]
        return jnp.einsum('bhqk,bkhe->bqhe', a.astype(v.dtype), v)

    def finish(o):
        B, L = o.shape[:2]
        o = rmsnorm(o, subln, eps=1e-5) * (1.0 - lambda_init)
        return o.reshape(B, L, DA_WIDTH) @ w_out

    B, Lx = qx.shape[:2]
    nb = Lx // Q_BLOCK
    qb = qx.reshape(B, nb, Q_BLOCK, DA_HEADS, 2, DA_HEAD_DIM).transpose(1, 0, 2, 3, 4, 5)
    ox = lax.map(lambda qq: attend(qq, k_all, v_all), qb)
    ox = ox.transpose(1, 0, 2, 3, 4).reshape(B, Lx, DA_HEADS, 2 * DA_HEAD_DIM)
    yx = finish(ox)
    yc = finish(attend(qc, kc, vc)) if with_ctx else None
    return yc, yx

def route(xf, w_r, bias):
    N = xf.shape[0]
    scores = jax.nn.sigmoid((xf @ w_r).astype(F32))
    choice = scores + bias.astype(F32)
    grp = choice.reshape(N, N_GROUPS, N_EXPERTS // N_GROUPS)
    gscore = jnp.sum(lax.top_k(grp, 2)[0], axis=-1)
    _, gidx = lax.top_k(gscore, TOPK_GROUPS)
    gmask = jnp.any(gidx[:, :, None] == jnp.arange(N_GROUPS)[None, None, :], axis=1)
    emask = jnp.repeat(gmask, N_EXPERTS // N_GROUPS, axis=1)
    _, eidx = lax.top_k(jnp.where(emask, choice, -jnp.inf), TOP_K)
    w = jnp.take_along_axis(scores, eidx, axis=-1)
    w = w / (jnp.sum(w, axis=-1, keepdims=True) + 1e-20) * ROUTED_SCALE
    return eidx, w

def routed_experts(xf, eidx, w, wg, wu, wd):
    N, D = xf.shape
    A = N * TOP_K
    e_flat = eidx.reshape(A)
    tok_flat = jnp.repeat(jnp.arange(N, dtype=jnp.int32), TOP_K)
    w_flat = w.reshape(A)
    order = jnp.argsort(e_flat)
    e_sorted = e_flat[order]
    counts = jnp.bincount(e_flat, length=N_EXPERTS)
    padded = (counts + MOE_BLOCK - 1) // MOE_BLOCK * MOE_BLOCK
    pad_end = jnp.cumsum(padded)
    pad_start = pad_end - padded
    start = jnp.cumsum(counts) - counts
    dest = pad_start[e_sorted] + jnp.arange(A, dtype=jnp.int32) - start[e_sorted]
    n_blocks = -(-(A + N_EXPERTS * (MOE_BLOCK - 1)) // MOE_BLOCK)
    P = n_blocks * MOE_BLOCK
    slot_tok = jnp.full((P,), N, jnp.int32).at[dest].set(tok_flat[order])
    slot_w = jnp.zeros((P,), F32).at[dest].set(w_flat[order])
    block_expert = jnp.minimum(jnp.searchsorted(pad_end, jnp.arange(n_blocks, dtype=jnp.int32) * MOE_BLOCK,
                                                side='right'), N_EXPERTS - 1)
    x_pad = jnp.concatenate([xf, jnp.zeros((1, D), xf.dtype)], axis=0)

    def step(acc, blk):
        toks, ws, e = blk
        yb = swiglu(x_pad[toks], wg[e], wu[e], wd[e]) * ws[:, None].astype(xf.dtype)
        return acc.at[toks].add(yb), None

    acc, _ = lax.scan(step, jnp.zeros((N + 1, D), xf.dtype),
                      (slot_tok.reshape(n_blocks, MOE_BLOCK), slot_w.reshape(n_blocks, MOE_BLOCK), block_expert))
    return acc[:N]

def moe(h, w_r, b_r, wg, wu, wd, swg, swu, swd):
    eidx, w = route(h, w_r, b_r)
    return swiglu(h, swg, swu, swd) + routed_experts(h, eidx, w, wg, wu, wd)

def setup_inputs(seed: int = 0) -> dict:
    key = jax.random.key(seed)
    ks = iter(jax.random.split(key, 40))
    nrm = lambda shape, scale: jax.random.normal(next(ks), shape, jnp.float32) * scale
    D = D_MODEL
    ne, no = (DEPTH + 1) // 2, DEPTH // 2
    ret_base = jnp.log(2.0 ** (5.0 + 2.0 * jnp.arange(RET_HEADS, dtype=jnp.float32)) - 1.0)
    return {
        "x": nrm((BATCH, SEQ, D), 1.0),
        "c": nrm((BATCH, D), 1.0),
        "ctx": nrm((BATCH, CTX_LEN, D), 1.0),
        "c_ctx": nrm((D,), 1.0),
        "w_ada": nrm((DEPTH, D, 6 * D), 0.5 * D ** -0.5),
        "b_ada": nrm((DEPTH, 6 * D), 0.02),
        "norm_mix": 1.0 + nrm((DEPTH, D), 0.05),
        "norm_ffn": 1.0 + nrm((DEPTH, D), 0.05),
        "ab_w_in": nrm((ne, D, AB_IN), D ** -0.5),
        "ab_w_out": nrm((ne, AB_CAT, D), AB_CAT ** -0.5),
        "ret_decay_logit": ret_base + nrm((ne, 2, RET_HEADS), 0.1),
        "hy_conv_w": nrm((ne, 3, (HY_ORDER + 1) * HY_WIDTH), 0.5),
        "hy_conv_b": nrm((ne, (HY_ORDER + 1) * HY_WIDTH), 0.02),
        "hy_w1": nrm((ne, HY_EMB, HY_FFN), HY_EMB ** -0.5),
        "hy_b1": nrm((ne, HY_FFN), 0.1),
        "hy_freq1": 1.0 + nrm((ne, HY_FFN), 0.1),
        "hy_w2": nrm((ne, HY_FFN, HY_FFN), HY_FFN ** -0.5),
        "hy_b2": nrm((ne, HY_FFN), 0.1),
        "hy_freq2": 1.0 + nrm((ne, HY_FFN), 0.1),
        "hy_w3": nrm((ne, HY_FFN, HY_ORDER * 2 * HY_WIDTH), 0.005),
        "hy_skip": nrm((ne, HY_ORDER, HY_WIDTH), 0.5),
        "da_w_in": nrm((no, D, 3 * DA_WIDTH), D ** -0.5),
        "da_w_out": nrm((no, DA_WIDTH, D), DA_WIDTH ** -0.5),
        "da_lambda": nrm((no, 4, DA_HEAD_DIM), 0.1),
        "da_subln": 1.0 + nrm((no, 2 * DA_HEAD_DIM), 0.05),
        "router_w": nrm((DEPTH, D, N_EXPERTS), D ** -0.5),
        "router_b": nrm((DEPTH, N_EXPERTS), 0.01),
        "exp_w_gate": nrm((DEPTH, N_EXPERTS, D, EXPERT_DIM), D ** -0.5),
        "exp_w_up": nrm((DEPTH, N_EXPERTS, D, EXPERT_DIM), D ** -0.5),
        "exp_w_down": nrm((DEPTH, N_EXPERTS, EXPERT_DIM, D), EXPERT_DIM ** -0.5),
        "sh_w_gate": nrm((DEPTH, D, SHARED_DIM), D ** -0.5),
        "sh_w_up": nrm((DEPTH, D, SHARED_DIM), D ** -0.5),
        "sh_w_down": nrm((DEPTH, SHARED_DIM, D), SHARED_DIM ** -0.5),
        "norm_final": 1.0 + nrm((D,), 0.05),
    }

def reference(x, c, ctx, c_ctx, w_ada, b_ada, norm_mix, norm_ffn, ab_w_in, ab_w_out, ret_decay_logit,
              hy_conv_w, hy_conv_b, hy_w1, hy_b1, hy_freq1, hy_w2, hy_b2, hy_freq2, hy_w3, hy_skip,
              da_w_in, da_w_out, da_lambda, da_subln, router_w, router_b, exp_w_gate, exp_w_up, exp_w_down,
              sh_w_gate, sh_w_up, sh_w_down, norm_final):
    B, L, D = x.shape
    Lc = ctx.shape[1]
    rows = L // GRID_W
    rope_ret = axial_rope(rows, RET_DK)
    rope_da = axial_rope(rows, DA_HEAD_DIM)
    for i in range(DEPTH):
        with_ctx = i < DEPTH - 1
        j = i // 2
        mod_x = jax.nn.silu(c) @ w_ada[i] + b_ada[i]
        mod_c = jax.nn.silu(c_ctx) @ w_ada[i] + b_ada[i]
        sx = jnp.split(mod_x[:, None, :], 6, axis=-1)
        sc = jnp.split(mod_c, 6, axis=-1)
        hx = rmsnorm(x, norm_mix[i]) * (1.0 + sx[1]) + sx[0]
        hc = rmsnorm(ctx, norm_mix[i]) * (1.0 + sc[1]) + sc[0]
        if i % 2 == 0:
            yc, yx = mixer_ab(hc, hx, ab_w_in[j], ab_w_out[j], ret_decay_logit[j], hy_conv_w[j], hy_conv_b[j],
                              hy_w1[j], hy_b1[j], hy_freq1[j], hy_w2[j], hy_b2[j], hy_freq2[j], hy_w3[j], hy_skip[j],
                              rope_ret, with_ctx)
        else:
            lambda_init = 0.8 - 0.6 * math.exp(-0.3 * i)
            yc, yx = mixer_da(hc, hx, da_w_in[j], da_w_out[j], da_lambda[j], da_subln[j], lambda_init,
                              rope_da, with_ctx)
        x = x + sx[2] * yx
        hx = rmsnorm(x, norm_ffn[i]) * (1.0 + sx[4]) + sx[3]
        moe_w = (router_w[i], router_b[i], exp_w_gate[i], exp_w_up[i], exp_w_down[i],
                 sh_w_gate[i], sh_w_up[i], sh_w_down[i])
        if with_ctx:
            ctx = ctx + sc[2] * yc
            hc = rmsnorm(ctx, norm_ffn[i]) * (1.0 + sc[4]) + sc[3]
            h_all = jnp.concatenate([hc.reshape(B * Lc, D), hx.reshape(B * L, D)], axis=0)
            y_all = moe(h_all, *moe_w)
            ctx = ctx + sc[5] * y_all[:B * Lc].reshape(B, Lc, D)
            x = x + sx[5] * y_all[B * Lc:].reshape(B, L, D)
        else:
            x = x + sx[5] * moe(hx.reshape(B * L, D), *moe_w).reshape(B, L, D)
    return rmsnorm(x, norm_final)


_drawn_inputs = setup_inputs


def setup_inputs(seed=0):
    import zlib

    import numpy as np

    out = dict(_drawn_inputs(seed))
    spreads = {}
    factors = {'hy_conv_b': 6.615,
     'hy_b1': 4.092,
     'hy_freq1': 5.239,
     'hy_freq2': 4.202,
     'da_subln': 2.765}
    for name, (base, spread) in spreads.items():
        noise = np.random.default_rng([zlib.crc32(name.encode()), seed]).standard_normal(out[name].shape)
        drawn = base * np.exp(spread * noise) if base else spread * noise
        out[name] = jnp.asarray(drawn.astype(out[name].dtype))
    for name, factor in factors.items():
        out[name] = (out[name] * factor).astype(out[name].dtype)
    return out
```

```python
import math
from contextlib import ExitStack, contextmanager

import numpy as np

import concourse.bass as bass
from concourse import mybir

F32 = mybir.dt.float32
I32 = mybir.dt.int32
U32 = mybir.dt.uint32
ALU = mybir.AluOpType
ACT = mybir.ActivationFunctionType
AX_X = mybir.AxisListType.X

P = 128
D = 1024
KC = D // P
SEQ = 256
CTX = 256
NTOK = CTX + SEQ
NT = NTOK // P
DEPTH = 2
EPS = 1e-6
GRID_W = 64
ROPE_BASE = 10000.0

RET_HEADS, RET_DK, RET_DV = 4, 128, 256
RET_V = RET_HEADS * RET_DV
HW = 512
HY_BANDS = 16
HY_EMB = 2 * HY_BANDS + 1
HY_FFN = 64
NFFT = 2 * SEQ

DA_HEADS, DA_HD = 8, 64
LAMBDA_INIT = 0.8 - 0.6 * math.exp(-0.3)

NE = 64
NG = 8
TOPG = 4
TOPK = 8
ED = 256
ROUTED_SCALE = 2.5

BANKS = 8
DENSE_SLOTS = 3
EXPERT_SLOTS = 4
BIG = 1e30

TWO_PI = 2.0 * math.pi
MAGIC = 12582912.0
PI_1 = 6.28125
PI_2 = float(np.float32(TWO_PI - PI_1))
PI_3 = float(np.float32(TWO_PI - PI_1 - PI_2))
PI_SAFE = 3.1415925


def shape_constants():
    f32 = np.float32
    k = {}
    k["ident"] = np.eye(P, dtype=f32)
    t = np.arange(SEQ, dtype=np.float64)
    tn = t / (SEQ - 1)
    bands = np.linspace(1e-4, HY_BANDS - 1, HY_BANDS)
    ang = (2.0 * math.pi / SEQ) * t[:, None] * bands[None, :]
    k["filter_features"] = np.concatenate([tn[:, None], np.cos(ang), -np.sin(ang)], axis=1).T.astype(f32)
    deltas = np.abs(np.linspace(math.log(1e-2) / 1.5, math.log(1e-2) / 0.3, HW))
    window = np.exp(-tn[:, None] * deltas[None, :])
    k["window"] = window.reshape(2, P, HW).transpose(1, 0, 2).astype(f32)
    f = np.arange(SEQ, dtype=np.float64)
    w = 2.0 * math.pi / NFFT
    re_f, im_f = np.cos(w * np.outer(t, f)), -np.sin(w * np.outer(t, f))
    nyquist = np.cos(math.pi * t)
    im_packed = im_f.copy()
    im_packed[:, 0] = nyquist
    re_nyq = re_f[:, 0:P].copy()
    re_nyq[:, 0] = nyquist
    fwd = np.concatenate([re_f, im_packed, im_f[:, 0:P], re_nyq], axis=1)
    k["dft_fwd"] = fwd.reshape(2, P, 6 * P).transpose(1, 0, 2).astype(f32)
    bwd = np.concatenate([re_f, -im_packed, -im_f[:, 0:P], re_nyq], axis=1)
    bwd[:, 2 * P * 1] = 0.0
    bwd[0, :] = 0.0
    k["dft_bwd"] = bwd.reshape(2, P, 6 * P).transpose(1, 0, 2).astype(f32)
    inv = np.zeros((NFFT, SEQ))
    inv[0:SEQ] = 2.0 * re_f.T
    inv[0] = 1.0
    inv[SEQ:] = 2.0 * im_f.T
    inv[SEQ] = nyquist
    inv /= NFFT
    k["dft_inv"] = inv.reshape(4, P, SEQ).transpose(1, 0, 2).astype(f32)
    for name, hd in (("rope_ret", RET_DK), ("rope_da", DA_HD)):
        nf = hd // 4
        fr = ROPE_BASE ** (-np.arange(nf, dtype=np.float64) / nf)
        row, col = np.repeat(np.arange(SEQ // GRID_W), GRID_W), np.tile(np.arange(GRID_W), SEQ // GRID_W)
        a = np.concatenate([row[:, None] * fr, col[:, None] * fr], axis=-1)
        cs = np.stack([np.cos(a), np.sin(a)], axis=0).reshape(2, 2, P, hd // 2)
        k[name] = cs.transpose(2, 0, 1, 3).reshape(P, 2 * 2 * (hd // 2)).astype(f32)
    i, j = np.arange(SEQ), np.arange(SEQ)
    k["distance"] = (i[None, :] - j[:, None]).reshape(2, P, SEQ).transpose(1, 0, 2).astype(f32)
    k["iota1"] = np.tile(np.arange(1, P + 1, dtype=f32), (P, 1))
    k["iota8"] = np.tile(np.arange(NG, dtype=f32), (P, TOPG)).reshape(P, TOPG * NG)
    k["earlier"] = (np.arange(P)[:, None] < np.arange(P)[None, :]).astype(f32)
    k["ones"] = np.ones((P, P), f32)
    k["token_id1"] = (np.arange(NT)[None, :] * P + np.arange(P)[:, None] + 1).astype(f32)
    k["spare_id1"] = (NTOK + 1 + np.arange(P)[:, None]).astype(f32)
    sel = np.zeros((2, 2, P), f32)
    sel[0, 0], sel[1, 1] = 1.0, 1.0
    k["stream_select"] = sel
    return k


class BankRing:

    def __init__(self, order, bank_full, bank_read):
        self.order, self.bank_full, self.bank_read = order, bank_full, bank_read
        self.at = {use: n for n, use in enumerate(order)}
        self.claimed = 0

    def bank(self, stage, k):
        return self.at[(stage, k)] % BANKS

    def claim(self, pe, stage, k):
        n = self.at[(stage, k)]
        assert n == self.claimed, (stage, k, self.order[self.claimed])
        self.claimed += 1
        if n >= BANKS:
            pe.wait_ge(self.bank_read[n % BANKS], n // BANKS)

    def full(self, stage, k):
        return self.bank_full[self.bank(stage, k)]

    def read(self, stage, k):
        return self.bank_read[self.bank(stage, k)]

    def wait_full(self, eng, stage, k):
        n = self.at[(stage, k)]
        eng.wait_ge(self.bank_full[n % BANKS], n // BANKS + 1)

    def wait_read(self, eng, stage, k):
        n = self.at[(stage, k)]
        eng.wait_ge(self.bank_read[n % BANKS], n // BANKS + 1)

    def fence(self, pe):
        for n in range(self.claimed - BANKS, self.claimed):
            pe.wait_ge(self.bank_read[n % BANKS], n // BANKS + 1)


class Chain:

    def __init__(self, eng, sem):
        self.eng, self.sem, self.n = eng, sem, 0

    def __call__(self, ins):
        self.n += 1
        ins.then_inc(self.sem, 1)
        self.eng.wait_ge(self.sem, self.n)


def psum_order():
    o = [("filter_a", 0), ("filter_b", 0)]
    o += [("filter_c", k) for k in range(8)]
    o += [("filter_dft", k) for k in range(10)]

    def ada(tag, streams):
        return [(f"mod_{tag}", k) for k in range(6)] + [(f"bcast_{tag}", k) for k in range(6 * streams)]

    def norm(tag, tiles):
        return [(f"norm_{tag}", k) for k in range(2 * tiles)]

    def moe(tag, tiles):
        r = [(f"route_{tag}", k) for k in range(tiles)]
        r += [(f"pos_{tag}", k) for k in range(tiles + 1)]
        for t in range(tiles):
            r += [(f"sh_gu_{tag}", t), (f"sh_t_{tag}", t), (f"sh_y_{tag}", 2 * t), (f"sh_y_{tag}", 2 * t + 1)]
        return r

    o += ada("0a", 2) + norm("0a", NT)
    for m in range(12):
        o.append(("u_proj", m))
        if 1 <= m <= 8:
            o.append(("u_turn", m - 1))
    for order in range(2):
        for s in range(2):
            o += [(f"dft_{order}", 4 * s + m) for m in range(4)]
            o += [(f"idft_{order}", (2, 4)[order] * s + m) for m in range((2, 4)[order])]
    for c in range(2):
        for t in range(NT):
            o.append(("qk_proj", c * NT + t))
            if c * NT + t:
                o.append(("qk_turn", c * NT + t - 1))
    o.append(("qk_turn", 2 * NT - 1))
    o += [("vg_proj", k) for k in range(4 * NT)]
    for h in range(RET_HEADS):
        o += [("ret_s", 4 * h + k) for k in range(4)]
        o += [("ret_o", NT * h + t) for t in range(NT)]
        o += [("ret_turn", NT * h + t) for t in range(NT)]
    o += [("out_0", k) for k in range(2 * NT)]
    o += ada("0b", 2) + norm("0b", NT) + moe("0", NT)
    o += ada("1a", 2) + norm("1a", NT)
    n = 0
    for c in range(4):
        for t in range(NT):
            if c < 2 and t < 2:
                continue
            o.append(("da_qk", n))
            if n:
                o.append(("da_turn", n - 1))
            n += 1
    o.append(("da_turn", n - 1))
    o += [("da_v", k) for k in range(2 * NT)]
    for n in range(2 * DA_HEADS + 1):
        if n < 2 * DA_HEADS:
            o += [("da_s", 2 * n), ("da_s", 2 * n + 1)]
        if n:
            o += [("da_at", n - 1), ("da_o", n - 1)]
    o += [("da_ot", k) for k in range(4)]
    o += [("out_1", k) for k in range(4)]
    o += ada("1b", 1) + norm("1b", 2) + moe("1", 2)
    return o


def build(nc, A, K, out):
    with ExitStack() as ctx:
        def sb(name, shape, dt=F32, scope=ctx):
            return scope.enter_context(nc.sbuf_tensor(name, shape, dt))

        sems = {}

        def sem(name):
            if name not in sems:
                sems[name] = ctx.enter_context(nc.semaphore(name))
            return sems[name]

        order = psum_order()
        ring = BankRing(order, [sem(f"bank_full_{b}") for b in range(BANKS)],
                        [sem(f"bank_read_{b}") for b in range(BANKS)])
        ps = ctx.enter_context(nc.psum_tensor("ps", [P, BANKS, 512], F32))

        def bank(stage, k):
            return ps[:, ring.bank(stage, k), :]

        h_rows = nc.dram_tensor("h_rows", (NTOK + P, D), F32, kind="Internal").ap()
        acc_rows = nc.dram_tensor("acc_rows", (NTOK + P, D), F32, kind="Internal").ap()


        WORDS = 53000
        arena = sb("arena", [P, WORDS])

        class Region:
            def __init__(self, at, end=WORDS):
                self.at, self.end = at, end

            def take(self, *shape, parts=P, dt=F32):
                n = math.prod(shape)
                assert self.at + n <= self.end, (self.at, n, self.end)
                v = arena[0:parts, self.at:self.at + n]
                if dt != F32:
                    v = v.bitcast(dt)
                self.at += n
                names = ["a", "b", "c", "d"][:len(shape)]
                if len(shape) > 1:
                    v = v.rearrange(f"p ({' '.join(names)}) -> p {' '.join(names)}", **dict(zip(names, shape)))
                return v

        top = Region(0)
        WS = top.take(EXPERT_SLOTS, KC * 512)
        spare_at = top.at - KC * 512
        X = top.take(NT, D)
        bc = top.take(2, 3, D)
        hT = top.take(KC, NTOK)
        ident = top.take(P)
        select = top.take(2, P, parts=2)
        cvec = top.take(2, KC)
        csilu = top.take(2, KC)
        ssq = top.take(NT)
        rstd = top.take(NT)
        flags = top.take(DEPTH, dt=I32)
        scratch_at = top.at
        modrow = top.take(3 * D, parts=2)
        normrow = top.take(D, parts=2)
        phase_at = top.at

        r = Region(scratch_at, phase_at)
        router_w = r.take(KC, NE)
        router_b = r.take(NE)
        scores = r.take(NT, NE)
        picked = r.take(NT, NE)
        pos1 = r.take(NT, NE)
        idw = r.take(NT, NE, 2)
        choice = r.take(NE)
        replaced = r.take(NE)
        best = r.take(NG, 8)
        gsum = r.take(NG)
        gtop = r.take(8)
        gidx = r.take(8, dt=U32)
        gidxf = r.take(8)
        geq = r.take(TOPG, NG)
        gmask = r.take(NG)
        gneg = r.take(NG)
        wsum = r.take(1)
        counts_max = r.take(1)
        slot_id = r.take(NE)
        slot_w = r.take(NE)
        slot_empty = r.take(NE)
        slot_u = r.take(NE, dt=U32)
        gather_idx = r.take(EXPERT_SLOTS, 1, dt=U32)
        scatter_idx = r.take(EXPERT_SLOTS, 1, dt=U32)
        r = Region(phase_at)
        DN = r.take(EXPERT_SLOTS, 2 * D)
        xg = r.take(2, D)
        xgT = r.take(2, D)
        yb = r.take(2, D)
        gsil = r.take(2, ED)
        act = r.take(2, ED)
        actT = r.take(2, 2 * P)
        iota1 = r.take(P)
        iota8 = r.take(TOPG, NG)
        earlier = r.take(P)
        ones = r.take(P)
        token_id1 = r.take(NT)
        spare_id1 = r.take(1)
        one_hot = yb.rearrange("p a (t s) -> p a t s", s=P)
        accb = xg.rearrange("p a n -> p (a n)")

        r = Region(phase_at)
        H = r.take(2, 5, HW)
        dftf = r.take(2, 6 * P)
        dfti = r.take(4, SEQ)
        sub_at = r.at
        r = Region(WORDS - 4 * NTOK)
        catH = r.take(4, NTOK)
        r = Region(sub_at, WORDS - 4 * NTOK)
        window = r.take(2, HW)
        dftb = r.take(2, 6 * P)
        fz = r.take(SEQ, parts=HY_EMB)
        fw1 = r.take(HY_FFN, parts=HY_EMB)
        fw2 = r.take(HY_FFN, parts=HY_FFN)
        fw3 = r.take(4 * HW, parts=HY_FFN)
        fcol = r.take(4, parts=HY_FFN)
        farg = r.take(SEQ, parts=HY_FFN)
        fturn = r.take(SEQ, parts=HY_FFN)
        fh = r.take(2, SEQ, parts=HY_FFN)
        skiprow = r.take(2, HW, parts=1)
        r = Region(spare_at, spare_at + KC * 512)
        filt = r.take(2, 4, HW)
        r = Region(sub_at, WORDS - 4 * NTOK)
        vtok = r.take(NT, HW)
        x1tok = r.take(NT, HW)
        uconv = r.take(2, NTOK)
        specY = r.take(4, HW)
        r = Region(WORDS - 4 * NTOK)
        cw = r.take(3, 12)
        cb = r.take(12)
        r = Region(spare_at, spare_at + KC * 512)
        x2T = r.take(4, NTOK)
        upad = r.take(2, 2, SEQ + 2)
        spec_t = r.take(HW)
        r = Region(phase_at, WORDS - 4 * NTOK)
        v_tok = r.take(NT, RET_V)
        g_tok = r.take(NT, RET_V)
        qT = r.take(RET_HEADS, NTOK)
        kT = r.take(RET_HEADS, NTOK)
        qk_tok = r.take(2, 512)
        rope_r = r.take(2, 2, RET_DK // 2)
        rope_t = r.take(2, 256)
        dist = r.take(2, SEQ)
        r = Region(spare_at, spare_at + KC * 512)
        dist_f = r.take(2, SEQ)
        dist_b = r.take(2, SEQ)
        decay = r.take(2, 2, SEQ)
        decay_e = r.take(2, 2 * SEQ)
        r = Region(r.at, r.end)
        ret_row = r.take(2, RET_DV)
        ret_stat = r.take(NT, 6)
        ret_mv = r.take(NT, 2)
        lg = r.take(2 * RET_HEADS)
        lgt = r.take(4, 2 * RET_HEADS)
        lgs = r.take(3, 2 * RET_HEADS)
        r = Region(scratch_at, phase_at)
        sT0 = r.take(2, NTOK)
        sT2 = r.take(2, SEQ)
        catR = hT

        r = Region(phase_at)
        qTd = r.take(DA_HEADS, SEQ)
        kTd = r.take(DA_HEADS, NTOK)
        v_da = r.take(NT, D)
        qk_da = r.take(2, 512)
        rope_d = r.take(2, 2, DA_HD // 2)
        rope_dt = r.take(2, 256)
        o_tok = r.take(2, D)
        oT = r.take(DA_HEADS, SEQ)
        subln = r.take(P)
        lamv = r.take(4, DA_HD)
        lamt = r.take(8)
        r = Region(spare_at, spare_at + KC * 512)
        prob = r.take(2, 2, NTOK)
        adiff = r.take(2, NTOK)
        aT = r.take(1, NTOK)
        smax = r.take(2, 2)
        ssum = r.take(2, 2)
        sinv = r.take(2, 2)
        ohs = r.take(2, DA_HEADS)

        r = Region(WORDS - 4 * NTOK - 2 * D)
        hrow_mix = r.take(2, D)
        r = Region(phase_at + 4 * 2 * D)
        hrow_moe = r.take(2, D)
        final_g = Region(phase_at).take(D)
        assert hrow_moe.shape == xg.shape

        def spread(v):
            return v.unsqueeze(0).partition_broadcast(P) if False else v

        col = lambda v: v.rearrange("(p a) -> p a", a=1)
        row = lambda v: v.rearrange("(a n) -> a n", a=1)
        every = lambda v, n=P: row(v).broadcast_to([n, v.shape[0]])
        flat = lambda v, s: v.rearrange(s)
        start_loads = [
            (cvec[:, 0, :], A["c_ctx"].rearrange("(p c) -> p c", p=P)),
            (cvec[:, 1, :], A["c"].rearrange("a (p c) -> p (a c)", p=P)),
            (ident, K["ident"]),
            (select, K["stream_select"]),
        ]
        filter_loads = [
            (fz, K["filter_features"]),
            (fw1, A["hy_w1"][0]), (fw2, A["hy_w2"][0]), (fw3, A["hy_w3"][0]),
            (fcol[:, 0:1], col(A["hy_b1"][0])), (fcol[:, 1:2], col(A["hy_freq1"][0])),
            (fcol[:, 2:3], col(A["hy_b2"][0])), (fcol[:, 3:4], col(A["hy_freq2"][0])),
            (window, K["window"]), (dftf, K["dft_fwd"]), (dftb, K["dft_bwd"]), (dfti, K["dft_inv"]),
            (skiprow, A["hy_skip"][0:1]),
        ]
        token_loads = [(X[:, t, :], A["ctx"][0, t * P:(t + 1) * P, :]) for t in range(2)]
        token_loads += [(X[:, 2 + t, :], A["x"][0, t * P:(t + 1) * P, :]) for t in range(2)]
        conv_loads = [(cw[:, k, :].rearrange("p (i c) -> p i c", i=3), A["hy_conv_w"][0, k].rearrange("(i p c) -> p i c", p=P, c=4))
                      for k in range(3)]
        conv_loads += [(cb.rearrange("p (i c) -> p i c", i=3), A["hy_conv_b"][0].rearrange("(i p c) -> p i c", p=P, c=4))]
        ret_loads = [
            (rope_r, K["rope_ret"].rearrange("p (a b c) -> p a b c", a=2, b=2)),
            (dist, K["distance"]),
            (lgt[:, 0, :], every(A["ret_decay_logit"][0].rearrange("a h -> (a h)"))),
        ]
        da_loads = [
            (rope_d, K["rope_da"].rearrange("p (a b c) -> p a b c", a=2, b=2)),
            (subln, every(A["da_subln"][0])),
            (lamv, every(A["da_lambda"][0].rearrange("a h -> (a h)")).rearrange("p (a h) -> p a h", a=4)),
        ]

        def moe_loads(layer):
            return [
                (router_w, A["router_w"][layer].rearrange("(p c) n -> p c n", c=KC)),
                (router_b, every(A["router_b"][layer])),
                (iota1, K["iota1"]), (iota8, K["iota8"].rearrange("p (a b) -> p a b", a=TOPG)),
                (earlier, K["earlier"]), (ones, K["ones"]),
                (token_id1, K["token_id1"]), (spare_id1, K["spare_id1"]),
            ]

        def ada_loads(layer, half):
            g = A["norm_mix"] if half == 0 else A["norm_ffn"]
            return [
                (modrow, every(A["b_ada"][layer, half * 3 * D:(half + 1) * 3 * D], 2)),
                (normrow, every(g[layer], 2)),
            ]

        def columns(w, at):
            return w.rearrange("(p c) n -> p c n", c=KC)[:, :, at:at + 512]

        def row_chunks(w, at):
            return w.rearrange("(c p) n -> p c n", p=P)[:, at:at + 4, :]

        dense = []
        first = {}

        def stream(name, items, last_use):
            first[name] = len(dense)
            dense.extend((src, last_use(n)) for n, src in enumerate(items))

        U_AT = 2 * RET_HEADS * RET_DK + 2 * RET_V
        ab_in, da_in, w_ada = A["ab_w_in"][0], A["da_w_in"][0], A["w_ada"]
        stream("ada_0a", [columns(w_ada[0], 512 * n) for n in range(6)], lambda n: ("mod_0a", n))
        stream("u", [columns(ab_in, U_AT + 512 * n) for n in range(3)], lambda n: ("u_proj", 4 * n + 3))
        stream("qk", [columns(ab_in, 512 * n) for n in range(2)], lambda n: ("qk_proj", NT * n + NT - 1))
        stream("vg", [columns(ab_in, 512 * (2 + n)) for n in range(4)], lambda n: ("vg_proj", NT * n + NT - 1))
        stream("out_0", [row_chunks(A["ab_w_out"][0], 4 * n) for n in range(2)]
               + [A["ab_w_out"][0, RET_V:RET_V + HW, :].rearrange("(p c) n -> p c n", c=4)], lambda n: ("out_0", 2 * NT - 1))
        stream("ada_0b", [columns(w_ada[0], 512 * (6 + n)) for n in range(6)], lambda n: ("mod_0b", n))
        stream("ada_1a", [columns(w_ada[1], 512 * n) for n in range(6)], lambda n: ("mod_1a", n))
        stream("da_qk", [columns(da_in, 512 * n) for n in range(4)], lambda n: ("da_qk", (1, 3, 7, 11)[n]))
        stream("da_v", [columns(da_in, 512 * (4 + n)) for n in range(2)], lambda n: ("da_v", NT * n + NT - 1))
        stream("out_1", [row_chunks(A["da_w_out"][0], 4 * n) for n in range(2)], lambda n: ("out_1", 3))
        stream("ada_1b", [columns(w_ada[1], 512 * (6 + n)) for n in range(6)], lambda n: ("mod_1b", n))

        def dense_slot(n, width):
            return WS[:, n % DENSE_SLOTS, :].rearrange("p (c n) -> p c n", n=width)

        dense_in = [sem(f"dense_in_{i}") for i in range(DENSE_SLOTS)]

        def wait_dense(pe, n):
            pe.wait_ge(dense_in[n % DENSE_SLOTS], 16 * (n // DENSE_SLOTS + 1))

        LT = {0: (0, NT), 1: (2, 2)}

        start_in, filter_in, token_in = sem("start_in"), sem("filter_in"), sem("token_in")
        conv_in, ret_in, da_in_sem, moe_in, ada_in = (sem(x) for x in ("conv_in", "ret_in", "da_in", "moe_in", "ada_in"))
        final_in = sem("final_in")
        dve_step = sem("dve_step")
        c_silu, filt_arg, filt_sin, filt_taps = sem("c_silu"), sem("filt_arg"), sem("filt_sin"), sem("filt_taps")
        mod_rows = sem("mod_rows")
        squares, variance, deviation, rows = sem("squares"), sem("variance"), sem("deviation"), sem("rows")
        conv_done, conv_edges, spec_done = sem("conv_done"), sem("conv_edges"), sem("spec_done")
        decay_arg, decay_exp, decay_used = sem("decay_arg"), sem("decay_exp"), sem("decay_used")
        ret_var, ret_dev, ret_rows = sem("ret_var"), sem("ret_dev"), sem("ret_rows")
        residual = sem("residual")
        lam_sums, lam_exp = sem("lam_sums"), sem("lam_exp")
        score_max, probs, probs_mixed = sem("score_max"), sem("probs"), sem("probs_mixed")
        o_var, o_dev, o_rows = sem("o_var"), sem("o_dev"), sem("o_rows")
        spare_zero, spare_out = sem("spare_zero"), sem("spare_out")
        rows_out = [sem(f"rows_out_{i}") for i in range(2)]
        shared_out = [sem(f"shared_out_{i}") for i in range(2)]
        picks, id_weights, positions = sem("picks"), sem("id_weights"), sem("positions")
        hot, hot_used, flag_ready, slot_table = sem("hot"), sem("hot_used"), sem("flag_ready"), sem("slot_table")
        sh_silu, sh_act = sem("sh_silu"), sem("sh_act")
        acc_in, moe_done, result_out = sem("acc_in"), sem("moe_done"), sem("result_out")
        result = sem("result")
        E = {}
        for l in range(DEPTH):
            for nme in ("xg_in_0", "xg_in_1", "xT_full", "xT_read", "gu_full", "sg_done", "act_done", "aT_full",
                        "aT_read", "y_full", "y_read_a", "y_read_d", "scattered", "gidx", "sidx"):
                E[nme, l] = sem(f"{nme}_{l}")
            for i in range(EXPERT_SLOTS):
                E["gu_in", l, i] = sem(f"gu_in_{i}_{l}")
                E["dn_in", l, i] = sem(f"dn_in_{i}_{l}")

        def at_least(eng, s, v):
            if not isinstance(v, int) or v > 0:
                eng.wait_ge(s, v)

        block = ctx.enter_context(nc.Block())

        ROWS_BEFORE = {"0a": 0, "0b": NT, "1a": 2 * NT, "1b": 3 * NT, "final": 3 * NT + 2}
        NORM_NO = {"0a": 0, "0b": 1, "1a": 2, "1b": 3, "final": 4}
        NORM_TILES = {"0a": (0, NT), "0b": (0, NT), "1a": (0, NT), "1b": (2, 2), "final": (2, 2)}
        ADA_NO = {"0a": 0, "0b": 1, "1a": 2, "1b": 3}
        HROW = {"0a": hrow_mix, "0b": hrow_moe, "1a": hrow_mix, "1b": hrow_moe}
        ZERO = xgT[:, 0, :]
        ACC = Region(phase_at).take(NT, D)
        o_squares = qk_da.rearrange("p a (b c) -> p (a b) c", c=P)
        DA_USES = [(c, t) for c in range(4) for t in range(NT) if c >= 2 or t >= 2]

        M = {}
        for l in range(DEPTH):
            for nme in ("step", "in", "pe", "act", "dve", "xg", "out"):
                M[nme, l] = sem(f"more_{nme}_{l}")

        @contextmanager
        def overflow(eng, l):
            eng.wait_ge(flag_ready, l + 1)
            more = eng.value_load(flags[0:1, l:l + 1], min_val=0, max_val=1)
            with eng.If(more > 0):
                yield

        @block.sync
        def _(sp):
            def load_dense(name):
                n0 = first[name]
                n1 = min([first[x] for x in first if first[x] > n0], default=len(dense))
                for n in range(n0, n1):
                    if n >= DENSE_SLOTS:
                        ring.wait_full(sp, *dense[n - DENSE_SLOTS][1])
                    src = dense[n][0]
                    sp.dma_start(dense_slot(n, src.shape[2]), src).then_inc(dense_in[n % DENSE_SLOTS], 16)

            def expert_rows(w, l, e):
                v = w[l, e] if isinstance(e, int) else w[l, bass.ds(e, 1)].rearrange("a d n -> (a d) n")
                return v.rearrange("(p c) n -> p (c n)", p=P)

            def load_expert(l, u, gate, up, down):
                dst = WS[:, u, :].rearrange("p (a n) -> p a n", a=2)
                sp.dma_start(dst[:, 0, :], gate).then_inc(E["gu_in", l, u], 16)
                sp.dma_start(dst[:, 1, :], up).then_inc(E["gu_in", l, u], 16)
                sp.dma_start(DN[:, u, :], down).then_inc(E["dn_in", l, u], 16)

            def routed(l, item, u):
                e = item - 1
                load_expert(l, u, expert_rows(A["exp_w_gate"], l, e), expert_rows(A["exp_w_up"], l, e),
                            expert_rows(A["exp_w_down"], l, e))

            def load_experts(l):
                whole = lambda w: w[l].rearrange("(p c) n -> p (c n)", p=P)
                load_expert(l, 0, whole(A["sh_w_gate"]), whole(A["sh_w_up"]), whole(A["sh_w_down"]))
                for item in range(1, EXPERT_SLOTS):
                    routed(l, item, item)
                ring.wait_full(sp, f"sh_y_{l}", 2 * LT[l][1] - 1)
                for u in range(EXPERT_SLOTS):
                    if u:
                        sp.wait_ge(E["y_full", l], u)
                    routed(l, EXPERT_SLOTS + u, u)
                with sp.Fori(2, NE // EXPERT_SLOTS) as i:
                    for u in range(EXPERT_SLOTS):
                        sp.wait_ge(E["y_full", l], i * EXPERT_SLOTS + (u - EXPERT_SLOTS))
                        routed(l, i * EXPERT_SLOTS + u, u)
                sp.wait_ge(E["y_full", l], NE - EXPERT_SLOTS)
                routed(l, NE, 0)

            def overflow_sp(l):
                def load_more(e):
                    dst = WS[:, 0, :].rearrange("p (a n) -> p a n", a=2)
                    sp.dma_start(dst[:, 0, :], expert_rows(A["exp_w_gate"], l, e)).then_inc(M["in", l], 16)
                    sp.dma_start(dst[:, 1, :], expert_rows(A["exp_w_up"], l, e)).then_inc(M["in", l], 16)
                    sp.dma_start(DN[:, 0, :], expert_rows(A["exp_w_down"], l, e)).then_inc(M["in", l], 16)

                with overflow(sp, l):
                    load_more(0)
                    with sp.Fori(1, NE) as e:
                        sp.wait_ge(M["pe", l], e * (5 * (LT[l][1] - 1)))
                        load_more(e)

            for name in ("ada_0a", "u", "qk", "vg", "out_0", "ada_0b"):
                load_dense(name)
            ring.wait_full(sp, "mod_0b", 5)
            load_experts(0)
            sp.wait_ge(E["y_full", 0], NE)
            overflow_sp(0)
            for name in ("ada_1a", "da_qk", "da_v", "out_1", "ada_1b"):
                load_dense(name)
            ring.wait_full(sp, "mod_1b", 5)
            load_experts(1)
            sp.wait_ge(E["y_full", 1], NE)
            overflow_sp(1)
            for t in range(2):
                sp.wait_ge(result, t + 1)
                sp.dma_start(out[0, t * P:(t + 1) * P, :], hrow_mix[:, t, :]).then_inc(result_out, 16)
            sp.wait_ge(result_out, 32)

        @block.tensor
        def _(pe):
            def products(dst, pairs, signal):
                last = len(pairs) - 1
                for i, (l, r) in enumerate(pairs):
                    mm = nc.tensor.matmul(dst, l, r, start=(i == 0), stop=(i == last))
                if signal is not None:
                    mm.then_inc(signal, 1)

            def turns(dst, srcs, signal):
                for i, v in enumerate(srcs):
                    tr = nc.tensor.transpose(dst[:, i * P:(i + 1) * P], v, ident)
                tr.then_inc(signal, 1)

            def use(stage, k):
                ring.claim(pe, stage, k)
                return bank(stage, k), ring.full(stage, k)

            def ada(tag, streams):
                n0 = first[f"ada_{tag}"]
                for n in range(6):
                    wait_dense(pe, n0 + n)
                    w = dense_slot(n0 + n, 512)
                    b, full = use(f"mod_{tag}", n)
                    products(b[0:2, :], [(csilu[:, :, c], w[:, c, :]) for c in range(KC)], full)
                pe.wait_ge(mod_rows, ADA_NO[tag] + 1)
                for j in range(6):
                    for i, s in enumerate(streams):
                        b, full = use(f"bcast_{tag}", j * len(streams) + i)
                        products(b, [(select[:, s, :], modrow[:, j * 512:(j + 1) * 512])], full)

            def norm(tag):
                for j in range(NORM_TILES[tag][1]):
                    pe.wait_ge(rows, ROWS_BEFORE[tag] + j + 1)
                    v = HROW[tag][:, j % 2, :].rearrange("p (q c) -> p c q", c=KC)
                    for half in range(2):
                        b, full = use(f"norm_{tag}", 2 * j + half)
                        turns(b, [v[:, 4 * half + i, :] for i in range(4)], full)

            def all_norm_read(tag):
                for k in range(2 * NORM_TILES[tag][1]):
                    ring.wait_read(pe, f"norm_{tag}", k)

            def tile_cols(t):
                return slice(t * P, (t + 1) * P)

            def project(stage, k, n, t):
                w = dense_slot(n, 512)
                b, full = use(stage, k)
                products(b, [(hT[:, c, tile_cols(t)], w[:, c, :]) for c in range(KC)], full)

            def hyena_filters():
                pe.wait_ge(filter_in, 16 * len(filter_loads))
                b, full = use("filter_a", 0)
                products(b[0:HY_FFN, 0:SEQ], [(fw1, fz)], full)
                pe.wait_ge(filt_sin, 1)
                b, full = use("filter_b", 0)
                products(b[0:HY_FFN, 0:SEQ], [(fw2, fh[:, 0, :])], full)
                pe.wait_ge(filt_sin, 2)
                for t in range(2):
                    for n in range(4):
                        b, full = use("filter_c", 4 * t + n)
                        products(b, [(fh[:, 1, tile_cols(t)], fw3[:, n * HW:(n + 1) * HW])], full)
                pe.wait_ge(filt_taps, 1)
                for o in range(2):
                    for m in range(5):
                        g = (0, 1, 4, 3, 5)[m]
                        b, full = use("filter_dft", 5 * o + m)
                        products(b, [(tab[:, t, g * P:(g + 1) * P], filt[:, t, 2 * o + d, :])
                                     for t in range(2) for d, tab in enumerate((dftf, dftb))], full)

            def u_turn(m):
                pe.wait_ge(conv_done, m + 1)
                b, full = use("u_turn", m)
                turns(b, [uconv[:, m % 2, tile_cols(t)] for t in range(NT)], full)

            def hyena():
                for m in range(12):
                    n = first["u"] + m // 4
                    wait_dense(pe, n)
                    w = dense_slot(n, 512)
                    b, full = use("u_proj", m)
                    w = w.rearrange("p c (q m) -> p c q m", m=4)[:, :, :, m % 4]
                    products(b, [(w[:, c, :], hT[:, c, :]) for c in range(KC)], full)
                    if 1 <= m <= 8:
                        u_turn(m - 1)
                for k in range(8):
                    ring.wait_read(pe, "u_turn", k)
                for o in range(2):
                    for s in range(2):
                        if o:
                            for m in range(2):
                                ring.wait_read(pe, "idft_0", 2 * s + m)
                        for m in range(4):
                            b, full = use(f"dft_{o}", 4 * s + m)
                            products(b, [(dftf[:, t, m * P:(m + 1) * P], vtok[:, 2 * s + t, :])
                                         for t in range(2)], full)
                        pe.wait_ge(spec_done, 2 * o + s + 1)
                        for m in range((2, 4)[o]):
                            b, full = use(f"idft_{o}", (2, 4)[o] * s + m)
                            if o == 0:
                                products(b, [(dfti[:, f, m * P:(m + 1) * P], specY[:, f, :])
                                             for f in range(4)], full)
                            else:
                                by_chunk = specY.rearrange("p f (q m) -> p f q m", m=4)[:, :, :, m]
                                products(b[:, 0:SEQ], [(by_chunk[:, f, :], dfti[:, f, :])
                                                       for f in range(4)], full)

            def qk_turn(stage, source, n):
                ring.wait_read(pe, "qk_proj" if stage == "qk_turn" else "da_qk", n)
                b, full = use(stage, n)
                turns(b, [source[:, n % 2, i * P:(i + 1) * P] for i in range(4)], full)

            def retention():
                for n in range(2 * NT):
                    wait_dense(pe, first["qk"] + n // NT)
                    project("qk_proj", n, first["qk"] + n // NT, n % NT)
                    if n:
                        qk_turn("qk_turn", qk_tok, n - 1)
                qk_turn("qk_turn", qk_tok, 2 * NT - 1)
                for n in range(4 * NT):
                    wait_dense(pe, first["vg"] + n // NT)
                    project("vg_proj", n, first["vg"] + n // NT, n % NT)
                for n in range(2 * NT):
                    ring.wait_read(pe, "qk_turn", n)
                for n in range(4 * NT):
                    ring.wait_read(pe, "vg_proj", n)
                for h in range(RET_HEADS):
                    for kt in range(4):
                        b, full = use("ret_s", 4 * h + kt)
                        if kt < 2:
                            products(b, [(kT[:, h, tile_cols(kt)], qT[:, h, :])], full)
                        else:
                            products(b[:, 0:SEQ], [(kT[:, h, tile_cols(kt)], qT[:, h, CTX:])], full)
                    for kt in range(4):
                        ring.wait_read(pe, "ret_s", 4 * h + kt)
                    for t in range(NT):
                        b, full = use("ret_o", NT * h + t)
                        pairs = [(sT0[:, kt, tile_cols(t)], v_tok[:, kt, h * RET_DV:(h + 1) * RET_DV])
                                 for kt in range(2)]
                        if t >= 2:
                            pairs += [(sT2[:, kt, tile_cols(t - 2)], v_tok[:, 2 + kt, h * RET_DV:(h + 1) * RET_DV])
                                      for kt in range(2)]
                        products(b[:, 0:RET_DV], pairs, full)
                    for t in range(NT):
                        pe.wait_ge(ret_rows, NT * h + t + 1)
                        b, full = use("ret_turn", NT * h + t)
                        turns(b, [ret_row[:, t % 2, i * P:(i + 1) * P] for i in range(2)], full)

            def out_projection(layer):
                stage, n0 = f"out_{layer}", first[f"out_{layer}"]
                chunks = 12 if layer == 0 else KC
                for n in range(chunks // 4):
                    wait_dense(pe, n0 + n)
                for t in range(NT if layer == 0 else 2):
                    for half in range(2):
                        b, full = use(stage, 2 * t + half)
                        pairs = []
                        for c in range(chunks):
                            if layer == 0:
                                left = catR[:, c, tile_cols(t)] if c < 8 else catH[:, c - 8, tile_cols(t)]
                            else:
                                left = oT[:, c, tile_cols(t)]
                            w = dense_slot(n0 + c // 4, D)[:, c % 4, half * 512:(half + 1) * 512]
                            pairs.append((left, w))
                        products(b, pairs, full)

            def attention():
                for n, (c, t) in enumerate(DA_USES):
                    wait_dense(pe, first["da_qk"] + c)
                    project("da_qk", n, first["da_qk"] + c, t)
                    if n:
                        qk_turn("da_turn", qk_da, n - 1)
                qk_turn("da_turn", qk_da, len(DA_USES) - 1)
                for n in range(2 * NT):
                    wait_dense(pe, first["da_v"] + n // NT)
                    project("da_v", n, first["da_v"] + n // NT, n % NT)
                for n in range(len(DA_USES)):
                    ring.wait_read(pe, "da_turn", n)
                for n in range(2 * NT):
                    ring.wait_read(pe, "da_v", n)
                for n in range(2 * DA_HEADS + 1):
                    if n < 2 * DA_HEADS:
                        qt, h = n // DA_HEADS, n % DA_HEADS
                        for c in range(2):
                            b, full = use("da_s", 2 * n + c)
                            half = slice(c * DA_HD, (c + 1) * DA_HD)
                            products(b, [(qTd[half, h, tile_cols(qt)], kTd[half, h, :])], full)
                    if n:
                        m = n - 1
                        pe.wait_ge(probs_mixed, m + 1)
                        b, full = use("da_at", m)
                        turns(b, [adiff[:, m % 2, tile_cols(kt)] for kt in range(NT)], full)
                        ring.wait_read(pe, "da_at", m)
                        b, full = use("da_o", m)
                        h = m % DA_HEADS
                        products(b[:, 0:P], [(aT[:, 0, tile_cols(kt)], v_da[:, kt, h * P:(h + 1) * P])
                                             for kt in range(NT)], full)
                for qt in range(2):
                    pe.wait_ge(o_rows, qt + 1)
                    for half in range(2):
                        b, full = use("da_ot", 2 * qt + half)
                        turns(b, [o_tok[:, qt, (4 * half + i) * P:(4 * half + i + 1) * P] for i in range(4)], full)
                for k in range(4):
                    ring.wait_read(pe, "da_ot", k)

            def gate_up(dst, left, u, signal):
                w = WS[:, u, :].rearrange("p (a c n) -> p a c n", a=2, c=KC)
                products(dst, [(left(c), w[:, :, c, :]) for c in range(KC)], signal)

            def turn_act(dst, i, signal):
                v = act[:, i, :].rearrange("p (q c) -> p c q", c=2)
                turns(dst, [v[:, c, :] for c in range(2)], signal)

            def down(dst, half, i, u, signal):
                w = DN[:, u, :].rearrange("p (c n) -> p c n", c=2)
                products(dst, [(actT[:, i, c * P:(c + 1) * P], w[:, c, half * 512:(half + 1) * 512])
                               for c in range(2)], signal)

            def route(l):
                t0, tiles = LT[l]
                pe.wait_ge(moe_in, 16 * len(moe_loads(0)) * (l + 1))
                for k in range(tiles):
                    b, full = use(f"route_{l}", k)
                    products(b[:, 0:NE], [(hT[:, c, tile_cols(t0 + k)], router_w[:, c, :]) for c in range(KC)], full)
                pe.wait_ge(picks, (0, NT)[l] + tiles)
                for k in range(tiles + 1):
                    b, full = use(f"pos_{l}", k)
                    pairs = [(ones, picked[:, t0 + t, :]) for t in range(k)]
                    if k < tiles:
                        pairs.append((earlier, picked[:, t0 + k, :]))
                    products(b[:, 0:NE], pairs, full)

            def shared(l):
                t0, tiles = LT[l]
                pe.wait_ge(E["gu_in", l, 0], 32)
                pe.wait_ge(E["dn_in", l, 0], 16)
                before = (0, NT)[l]
                for t in range(tiles):
                    b, full = use(f"sh_gu_{l}", t)
                    gate_up(b, lambda c: hT[:, c, tile_cols(t0 + t)], 0, full)
                    ring.wait_read(pe, f"sh_gu_{l}", t)
                    b, full = use(f"sh_t_{l}", t)
                    turn_act(b, t % 2, full)
                    ring.wait_read(pe, f"sh_t_{l}", t)
                    for half in range(2):
                        b, full = use(f"sh_y_{l}", 2 * t + half)
                        down(b, half, t % 2, 0, full)

            def slots(l):
                t0, tiles = LT[l]
                pe.wait_ge(id_weights, (0, NT)[l] + tiles)
                with pe.Fori(0, NE // 2) as i:
                    for u in range(2):
                        pe.wait_ge(hot, i * 2 + (u + 1 + NE * l))
                        for t in range(tiles):
                            mm = nc.tensor.matmul(ps[:, 7, bass.ds(i * 4 + 2 * u, 2)], one_hot[:, u, t, :],
                                                  idw[:, t0 + t, bass.ds(i * 2 + u, 1), :].rearrange("p a b -> p (a b)"),
                                                  start=(t == 0), stop=(t == tiles - 1))
                        mm.then_inc(hot_used, 1)

            def experts(l):
                def turn_tokens(e, i, gathered):
                    pe.wait_ge(E[f"xg_in_{i}", l], gathered * 16)
                    at_least(pe, E["xT_read", l], e)
                    v = xg[:, i, :].rearrange("p (q c) -> p c q", c=KC)
                    for c in range(KC):
                        tr = nc.tensor.transpose(ps[:, c // 4, (c % 4) * P:(c % 4 + 1) * P], v[:, c, :], ident)
                    tr.then_inc(E["xT_full", l], 1)

                def down_of(e, i, u, item_count):
                    pe.wait_ge(E["aT_read", l], e + 1)
                    at_least(pe, E["y_read_a", l], e)
                    at_least(pe, E["y_read_d", l], e)
                    pe.wait_ge(E["dn_in", l, u], item_count * 16)
                    for half in range(2):
                        down(ps[:, 5 + half, :], half, i, u, E["y_full", l] if half else None)

                def step(e, r, i4, has_next=True):
                    u, i = r % 4, (r - 1) % 2
                    count = i4 + 1 + (1 if r == 4 else 0)
                    pe.wait_ge(E["xT_read", l], e + 1)
                    pe.wait_ge(E["gu_in", l, u], count * 32)
                    at_least(pe, E["act_done", l], e - 1)
                    gate_up(ps[:, 2 + i, :], lambda c: xgT[:, i, c * P:(c + 1) * P], u, E["gu_full", l])
                    if has_next:
                        turn_tokens(e + 1, 1 - i, i4 * 2 + (r // 2 + 1))
                    if not isinstance(e, int) or e > 0:
                        down_of(e - 1, 1 - i, (r - 1) % 4, i4 + 1)
                    pe.wait_ge(E["act_done", l], e + 1)
                    turn_act(ps[:, 4 if i == 0 else 7, :], i, E["aT_full", l])

                pe.wait_ge(slot_table, l + 1)
                turn_tokens(0, 0, 1)
                for r in range(1, 5):
                    step(r - 1, r, 0)
                with pe.Fori(1, NE // 4 - 1) as i4:
                    for r in range(1, 5):
                        step(i4 * 4 + (r - 1), r, i4)
                i4 = NE // 4 - 1
                for r in range(1, 5):
                    step(i4 * 4 + r - 1, r, i4, has_next=(r < 4))
                down_of(NE - 1, 1, 0, NE // 4 + 1)
                pe.wait_ge(E["y_read_a", l], NE)
                pe.wait_ge(E["y_read_d", l], NE)

            def overflow_pe(l):
                t0, tiles = LT[l]
                nb = tiles - 1
                with overflow(pe, l), pe.Fori(0, NE) as e:
                    for b in range(nb):
                        n = e * nb + b
                        pe.wait_ge(M["dve", l], n * 4 + 1)
                        for t in range(tiles):
                            mm = nc.tensor.matmul(ps[:, 7, 0:2], one_hot[:, 0, t, :],
                                                  idw[:, t0 + t, bass.ds(e, 1), :].rearrange("p a b -> p (a b)"),
                                                  start=(t == 0), stop=(t == tiles - 1))
                        mm.then_inc(M["pe", l], 1)
                        pe.wait_ge(M["xg", l], n * 16 + 16)
                        v = xg[:, 0, :].rearrange("p (q c) -> p c q", c=KC)
                        for c in range(KC):
                            tr = nc.tensor.transpose(ps[:, c // 4, (c % 4) * P:(c % 4 + 1) * P], v[:, c, :], ident)
                        tr.then_inc(M["pe", l], 1)
                        pe.wait_ge(M["act", l], n * 4 + 1)
                        pe.wait_ge(M["in", l], e * 48 + 48)
                        gate_up(ps[:, 2, :], lambda c: xgT[:, 0, c * P:(c + 1) * P], 0, M["pe", l])
                        pe.wait_ge(M["dve", l], n * 4 + 3)
                        turn_act(ps[:, 4, :], 0, M["pe", l])
                        pe.wait_ge(M["act", l], n * 4 + 3)
                        for half in range(2):
                            down(ps[:, 5 + half, :], half, 0, 0, M["pe", l] if half else None)
                with overflow(pe, l):
                    pe.wait_ge(M["act", l], NE * nb * 4)
                    pe.wait_ge(M["dve", l], NE * nb * 4)

            def layer_moe(l):
                route(l)
                shared(l)
                ring.fence(pe)
                slots(l)
                experts(l)
                overflow_pe(l)

            pe.wait_ge(start_in, 16 * len(start_loads))
            hyena_filters()
            pe.wait_ge(c_silu, 1)
            ada("0a", (0, 1))
            norm("0a")
            all_norm_read("0a")
            hyena()
            retention()
            for n in range(4 * RET_HEADS):
                ring.wait_read(pe, "ret_turn", n)
            out_projection(0)
            ada("0b", (0, 1))
            norm("0b")
            all_norm_read("0b")
            layer_moe(0)
            ada("1a", (0, 1))
            norm("1a")
            all_norm_read("1a")
            attention()
            out_projection(1)
            ada("1b", (1,))
            norm("1b")
            all_norm_read("1b")
            layer_moe(1)
            assert ring.claimed == len(ring.order)

        @block.scalar
        def _(act_e):
            A_ = nc.scalar.activation

            def load(items, s):
                for dst, src in items:
                    act_e.dma_start(dst, src).then_inc(s, 16)

            def norm_scale(tag):
                t0, tiles = NORM_TILES[tag]
                for j in range(tiles):
                    if j >= 2:
                        act_e.wait_ge(squares, ROWS_BEFORE[tag] + j - 1)
                    A_(HROW.get(tag, hrow_mix)[:, j % 2, :], X[:, t0 + j, :], ACT.Square,
                       accum_out=ssq[:, t0 + j:t0 + j + 1]).then_inc(squares, 1)
                act_e.wait_ge(variance, NORM_NO[tag] + 1)
                A_(rstd[:, t0:t0 + tiles], rstd[:, t0:t0 + tiles], ACT.Sqrt).then_inc(deviation, 1)

            def norm_turns(tag):
                t0, tiles = NORM_TILES[tag]
                for j in range(tiles):
                    t = t0 + j
                    for half in range(2):
                        k = 2 * j + half
                        ring.wait_full(act_e, f"norm_{tag}", k)
                        A_(hT[:, 4 * half:4 * half + 4, t * P:(t + 1) * P],
                           bank(f"norm_{tag}", k).rearrange("p (c q) -> p c q", c=4),
                           ACT.Copy).then_inc(ring.read(f"norm_{tag}", k), 1)

            def spread_mods(tag, streams):
                for j in range(6):
                    for i, s in enumerate(streams):
                        k = j * len(streams) + i
                        ring.wait_full(act_e, f"bcast_{tag}", k)
                        A_(bc[:, s, j // 2, (j % 2) * 512:(j % 2 + 1) * 512], bank(f"bcast_{tag}", k),
                           ACT.Copy).then_inc(ring.read(f"bcast_{tag}", k), 1)

            def evacuate(stage, k, dst, width=512, func=ACT.Copy, shape=None):
                ring.wait_full(act_e, stage, k)
                src = bank(stage, k)[:, 0:width]
                if shape:
                    src = src.rearrange("p (a b) -> p a b", a=shape)
                A_(dst, src, func).then_inc(ring.read(stage, k), 1)

            load(start_loads, start_in)
            load(ada_loads(0, 0), ada_in)
            load(filter_loads, filter_in)
            load(token_loads, token_in)
            act_e.wait_ge(start_in, 16 * len(start_loads))
            A_(csilu, cvec, ACT.Silu).then_inc(c_silu, 1)
            for n in range(2):
                act_e.wait_ge(filt_arg, n + 1)
                A_(fh[:, n, :], farg, ACT.Sin).then_inc(filt_sin, 1)
            for k in range(10):
                evacuate("filter_dft", k, H[:, k // 5, k % 5, :])
            load(conv_loads, conv_in)
            act_e.wait_ge(token_in, 16 * len(token_loads))
            norm_scale("0a")
            spread_mods("0a", (0, 1))
            norm_turns("0a")

            act_e.wait_ge(conv_edges, 1)
            for m in range(12):
                if m >= 2:
                    act_e.wait_ge(conv_done, m - 1)
                evacuate("u_proj", m, upad[:, m % 2, :, 1:SEQ + 1], shape=2)
                if 1 <= m <= 8:
                    n = m - 1
                    dst = (vtok, x1tok)[n // 4].rearrange("p t (q m) -> p t q m", m=4)[:, :, :, n % 4]
                    evacuate("u_turn", n, dst, shape=NT)
            for k in range(8):
                ring.wait_read(act_e, "idft_1", k)
            load(ret_loads, ret_in)
            for c in range(2):
                for t in range(NT):
                    n = c * NT + t
                    evacuate("qk_turn", n, (qT, kT)[c][:, :, t * P:(t + 1) * P], shape=RET_HEADS)
            for n in range(4 * NT):
                i, t = n // NT, n % NT
                dst = (v_tok, g_tok)[i // 2][:, t, (i % 2) * 512:(i % 2 + 1) * 512]
                evacuate("vg_proj", n, dst, func=ACT.Copy if i < 2 else ACT.Silu)
            act_e.wait_ge(decay_arg, 1)
            A_(lgt[:, 1, :], lgt[:, 1, :], ACT.Exp).then_inc(decay_exp, 1)
            act_e.wait_ge(decay_arg, 2)
            for h in range(RET_HEADS):
                f, b = slice(h, h + 1), slice(RET_HEADS + h, RET_HEADS + h + 1)
                at_least(act_e, decay_used, 2 * h)
                flat_ = lambda v: v.rearrange("p a n -> p (a n)")
                A_(decay_e[:, 0, :], flat_(dist_f), ACT.Exp, scale=lg[:, f])
                A_(decay_e[:, 1, :], flat_(dist_b), ACT.Exp, scale=lg[:, b]).then_inc(decay_exp, 1)
                act_e.wait_ge(decay_used, 2 * h + 1)
                A_(decay_e[:, 0, :], flat_(dist), ACT.Exp, scale=lg[:, f], bias=lgs[:, 0, f])
                A_(decay_e[:, 1, :], flat_(dist), ACT.Exp, scale=lgs[:, 2, b], bias=lgs[:, 0, b]).then_inc(decay_exp, 1)
                for t in range(NT):
                    n = NT * h + t
                    act_e.wait_ge(ret_var, n + 1)
                    A_(ret_mv[:, t, 1:2], ret_mv[:, t, 1:2], ACT.Sqrt).then_inc(ret_dev, 1)
                for t in range(NT):
                    evacuate("ret_turn", NT * h + t, catR[:, 2 * h:2 * h + 2, t * P:(t + 1) * P], width=2 * P, shape=2)
            load(ada_loads(0, 1), ada_in)
            act_e.wait_ge(residual, NT)
            norm_scale("0b")
            spread_mods("0b", (0, 1))

            def overflow_act(l):
                nb = LT[l][1] - 1
                with overflow(act_e, l), act_e.Fori(0, NE) as e:
                    for b in range(nb):
                        n = e * nb + b
                        act_e.wait_ge(M["pe", l], n * 5 + 2)
                        A_(xgT[:, 0, 0:512], ps[:, 0, :], ACT.Copy)
                        A_(xgT[:, 0, 512:], ps[:, 1, :], ACT.Copy).then_inc(M["act", l], 1)
                        act_e.wait_ge(M["pe", l], n * 5 + 3)
                        A_(gsil[:, 0, :], ps[:, 2, 0:ED], ACT.Silu).then_inc(M["act", l], 1)
                        act_e.wait_ge(M["pe", l], n * 5 + 4)
                        A_(actT[:, 0, :], ps[:, 4, 0:2 * P], ACT.Copy).then_inc(M["act", l], 1)
                        act_e.wait_ge(M["pe", l], n * 5 + 5)
                        A_(yb[:, 1, 0:512], ps[:, 5, :], ACT.Copy).then_inc(M["act", l], 1)
                        act_e.wait_ge(M["out", l], n * 16 + 16)

            def experts_phase(l):
                t0, tiles = LT[l]
                load(moe_loads(l), moe_in)
                norm_turns(f"{l}b")
                for k in range(tiles):
                    evacuate(f"route_{l}", k, scores[:, t0 + k, :], width=NE, func=ACT.Sigmoid)
                before = (0, NT)[l]
                for t in range(tiles):
                    ring.wait_full(act_e, f"sh_gu_{l}", t)
                    if t >= 2:
                        ring.wait_read(act_e, f"sh_gu_{l}", t - 2)
                    A_(gsil[:, t % 2, :], bank(f"sh_gu_{l}", t)[:, 0:ED], ACT.Silu).then_inc(sh_silu, 1)
                    evacuate(f"sh_t_{l}", t, actT[:, t % 2, :], width=2 * P)
                    if t >= 2:
                        act_e.wait_ge(shared_out[t % 2], 16)
                    evacuate(f"sh_y_{l}", 2 * t, yb[:, t % 2, 0:512])

                def tokens_in(e, i):
                    act_e.wait_ge(E["xT_full", l], e + 1)
                    for half in range(2):
                        a = A_(xgT[:, i, half * 512:(half + 1) * 512], ps[:, half, :], ACT.Copy)
                    a.then_inc(E["xT_read", l], 1)

                def rows_out_half(e, i):
                    act_e.wait_ge(E["y_full", l], e + 1)
                    at_least(act_e, E["scattered", l], 16 * (e - 1) if isinstance(e, int) else e * 16 - 16)
                    A_(yb[:, i, 0:512], ps[:, 5, :], ACT.Copy).then_inc(E["y_read_a", l], 1)

                def step(e, i, has_next=True):
                    act_e.wait_ge(E["gu_full", l], e + 1)
                    at_least(act_e, E["act_done", l], e - 1)
                    A_(gsil[:, i, :], ps[:, 2 + i, 0:ED], ACT.Silu).then_inc(E["sg_done", l], 1)
                    if has_next:
                        tokens_in(e + 1, 1 - i)
                    if not isinstance(e, int) or e > 0:
                        rows_out_half(e - 1, 1 - i)
                    act_e.wait_ge(E["aT_full", l], e + 1)
                    A_(actT[:, i, :], ps[:, 4 if i == 0 else 7, 0:2 * P], ACT.Copy).then_inc(E["aT_read", l], 1)

                tokens_in(0, 0)
                for e in range(4):
                    step(e, e % 2)
                with act_e.Fori(1, NE // 4 - 1) as i4:
                    for r in range(4):
                        step(i4 * 4 + r, r % 2)
                for e in range(NE - 4, NE):
                    step(e, e % 2, has_next=(e < NE - 1))
                rows_out_half(NE - 1, 1)
                overflow_act(l)

            experts_phase(0)
            act_e.wait_ge(moe_done, 1)
            load(ada_loads(1, 0), ada_in)
            norm_scale("1a")
            spread_mods("1a", (0, 1))
            load(da_loads, da_in_sem)
            load(ada_loads(1, 1), ada_in)
            norm_turns("1a")
            for n, (c, t) in enumerate(DA_USES):
                hs = slice((c % 2) * 4, (c % 2) * 4 + 4)
                dst = qTd[:, hs, (t - 2) * P:(t - 1) * P] if c < 2 else kTd[:, hs, t * P:(t + 1) * P]
                evacuate("da_turn", n, dst, shape=4)
            for n in range(2 * NT):
                i, t = n // NT, n % NT
                evacuate("da_v", n, v_da[:, t, i * 512:(i + 1) * 512])
            act_e.wait_ge(lam_sums, 1)
            A_(lamt[:, 0:2], lamt[:, 0:2], ACT.Exp).then_inc(lam_exp, 1)
            for n in range(2 * DA_HEADS + 1):
                if n < 2 * DA_HEADS:
                    act_e.wait_ge(score_max, n + 1)
                    if n >= 2:
                        act_e.wait_ge(probs_mixed, n - 1)
                    for c in range(2):
                        ring.wait_full(act_e, "da_s", 2 * n + c)
                        A_(prob[:, n % 2, c, :], bank("da_s", 2 * n + c), ACT.Exp, scale=DA_HD ** -0.5,
                           bias=smax[:, n % 2, c:c + 1], accum_out=ssum[:, n % 2, c:c + 1])\
                            .then_inc(ring.read("da_s", 2 * n + c), 1)
                if n:
                    m = n - 1
                    if m:
                        ring.wait_full(act_e, "da_o", m - 1)
                    evacuate("da_at", m, aT[:, 0, :])
                    evacuate("da_o", m, o_tok[:, m // DA_HEADS, (m % DA_HEADS) * P:(m % DA_HEADS + 1) * P], width=P)
            for qt in range(2):
                act_e.wait_ge(o_var, qt + 1)
                A_(ohs[:, qt, :], ohs[:, qt, :], ACT.Sqrt).then_inc(o_dev, 1)
            for k in range(4):
                qt, half = k // 2, k % 2
                evacuate("da_ot", k, oT[:, 4 * half:4 * half + 4, qt * P:(qt + 1) * P], shape=4)
            act_e.wait_ge(residual, 2 * NT - 1 + 2)
            norm_scale("1b")
            spread_mods("1b", (1,))
            experts_phase(1)
            act_e.wait_ge(moe_done, 2)
            act_e.dma_start(final_g, every(A["norm_final"])).then_inc(final_in, 16)
            norm_scale("final")

        @block.vector
        def _(dve):
            V = nc.vector
            link = Chain(dve, dve_step)

            def filter_arg(stage, i):
                ring.wait_full(dve, stage, 0)
                V.tensor_scalar(farg, bank(stage, 0)[0:HY_FFN, 0:SEQ], fcol[:, 2 * i:2 * i + 1],
                                fcol[:, 2 * i + 1:2 * i + 2], ALU.add, ALU.mult).then_inc(ring.read(stage, 0), 1)
                ring.wait_read(dve, stage, 0)
                link(V.tensor_scalar(fturn, farg, 1.0 / TWO_PI, MAGIC, ALU.mult, ALU.add))
                link(V.tensor_scalar(fturn, fturn, MAGIC, None, ALU.subtract))
                for part in (PI_1, PI_2, PI_3):
                    link(V.scalar_tensor_tensor(out=farg, in0=fturn, scalar=-part, in1=farg, op0=ALU.mult, op1=ALU.add))
                V.tensor_scalar(farg, farg, PI_SAFE, -PI_SAFE, ALU.min, ALU.max).then_inc(filt_arg, 1)

            def mods(tag):
                dve.wait_ge(ada_in, 32 * (ADA_NO[tag] + 1))
                for n in range(6):
                    stage = f"mod_{tag}"
                    ring.wait_full(dve, stage, n)
                    part = modrow[:, n * 512:(n + 1) * 512]
                    V.tensor_tensor(part, bank(stage, n)[0:2, :], part, ALU.add).then_inc(ring.read(stage, n), 1)
                for n in range(6):
                    ring.wait_read(dve, f"mod_{tag}", n)
                sc = modrow[:, D:2 * D]
                V.scalar_tensor_tensor(out=sc, in0=sc, scalar=1.0, in1=normrow, op0=ALU.add,
                                       op1=ALU.mult).then_inc(mod_rows, 1)

            def norm_inverse(tag):
                t0, tiles = NORM_TILES[tag]
                dve.wait_ge(squares, ROWS_BEFORE[tag] + tiles)
                V.tensor_scalar(rstd[:, t0:t0 + tiles], ssq[:, t0:t0 + tiles], 1.0 / D, EPS, ALU.mult,
                                ALU.add).then_inc(variance, 1)
                dve.wait_ge(deviation, NORM_NO[tag] + 1)
                link(V.reciprocal(rstd[:, t0:t0 + tiles], rstd[:, t0:t0 + tiles]))

            def norm_rows(tag, streams):
                t0, tiles = NORM_TILES[tag]
                norm_inverse(tag)
                for j in range(4 * len(streams)):
                    ring.wait_read(dve, f"bcast_{tag}", j)
                for j in range(tiles):
                    t = t0 + j
                    h = HROW[tag][:, j % 2, :]
                    if j >= 2:
                        ring.wait_full(dve, f"norm_{tag}", 2 * (j - 2) + 1)
                        if tag[1] == "b":
                            dve.wait_ge(rows_out[j % 2], 16)
                    link(V.scalar_tensor_tensor(out=h, in0=X[:, t, :], scalar=rstd[:, t:t + 1], in1=bc[:, t // 2, 1, :],
                                                op0=ALU.mult, op1=ALU.mult))
                    V.tensor_tensor(h, h, bc[:, t // 2, 0, :], ALU.add).then_inc(rows, 1)

            def rotate(dst, src, tab, tmp, t, groups, half, signal):
                v = src.rearrange("p (g a d) -> p g a d", g=groups, a=2)
                w = dst.rearrange("p (g a d) -> p g a d", g=groups, a=2)
                tmp = tmp.rearrange("p (g d) -> p g d", g=groups)
                cos, sin = (tab[:, i, t, :].unsqueeze(1).broadcast_to([P, groups, half]) for i in range(2))
                V.tensor_tensor(w[:, :, 0, :], v[:, :, 0, :], cos, ALU.mult)
                link(V.tensor_tensor(tmp, v[:, :, 1, :], sin, ALU.mult))
                link(V.tensor_tensor(w[:, :, 0, :], w[:, :, 0, :], tmp, ALU.subtract))
                V.tensor_tensor(w[:, :, 1, :], v[:, :, 1, :], cos, ALU.mult)
                link(V.tensor_tensor(tmp, v[:, :, 0, :], sin, ALU.mult))
                V.tensor_tensor(w[:, :, 1, :], w[:, :, 1, :], tmp, ALU.add).then_inc(signal, 1)

            def add_residual(stage, k, t, half):
                ring.wait_full(dve, stage, k)
                cols = slice(half * 512, (half + 1) * 512)
                b = bank(stage, k)
                V.tensor_tensor((qk_tok if stage == 'out_0' else qk_da)[:, k % 2, :], b, bc[:, t // 2, 2, cols], ALU.mult).then_inc(ring.read(stage, k), 1)
                ring.wait_read(dve, stage, k)
                return V.tensor_tensor(X[:, t, cols], X[:, t, cols], (qk_tok if stage == 'out_0' else qk_da)[:, k % 2, :], ALU.add)

            dve.wait_ge(filter_in, 16 * len(filter_loads))
            filter_arg("filter_a", 0)
            dve.wait_ge(filt_sin, 1)
            filter_arg("filter_b", 1)
            for k in range(8):
                t, n = k // 4, k % 4
                ring.wait_full(dve, "filter_c", k)
                V.tensor_tensor(filt[:, t, n, :], bank("filter_c", k), window[:, t, :], ALU.mult)\
                    .then_inc(ring.read("filter_c", k), 1)
            for k in range(8):
                ring.wait_read(dve, "filter_c", k)
            for o in range(2):
                ins = V.tensor_tensor(filt[0:1, 0, 2 * o, :], filt[0:1, 0, 2 * o, :], skiprow[:, o, :], ALU.add)
            ins.then_inc(filt_taps, 1)

            mods("0a")
            norm_rows("0a", (0, 1))

            for k in range(10):
                ring.wait_full(dve, "filter_dft", k)
            V.memset(upad[:, :, :, 0:1], 0.0)
            V.memset(upad[:, :, :, SEQ + 1:SEQ + 2], 0.0).then_inc(conv_edges, 1)
            dve.wait_ge(conv_in, 16 * len(conv_loads))
            dve.wait_ge(conv_edges, 1)
            for m in range(12):
                ring.wait_read(dve, "u_proj", m)
                if 2 <= m < 8:
                    ring.wait_full(dve, "u_turn", m - 2)
                dst = (uconv[:, m % 2, :] if m < 8 else x2T[:, m - 8, :]).rearrange("p (a n) -> p a n", a=2)
                u = upad[:, m % 2]
                link(V.tensor_scalar(dst, u[:, :, 0:SEQ], cw[:, 0, m:m + 1], cb[:, m:m + 1], ALU.mult, ALU.add))
                link(V.scalar_tensor_tensor(out=dst, in0=u[:, :, 1:SEQ + 1], scalar=cw[:, 1, m:m + 1], in1=dst,
                                            op0=ALU.mult, op1=ALU.add))
                V.scalar_tensor_tensor(out=dst, in0=u[:, :, 2:SEQ + 2], scalar=cw[:, 2, m:m + 1], in1=dst,
                                       op0=ALU.mult, op1=ALU.add).then_inc(conv_done, 1)
            for k in range(8):
                ring.wait_read(dve, "u_turn", k)
            for k in range(10):
                ring.wait_read(dve, "filter_dft", k)
            dve.wait_ge(conv_done, 12)
            for o in range(2):
                for s in range(2):
                    if o or s:
                        for m in range((2, 4)[(2 * o + s - 1) // 2]):
                            oo, sp_ = (2 * o + s - 1) // 2, (2 * o + s - 1) % 2
                            ring.wait_full(dve, f"idft_{oo}", (2, 4)[oo] * sp_ + m)
                    st = f"dft_{o}"
                    for m in range(4):
                        ring.wait_full(dve, st, 4 * s + m)
                    for m in range(2):
                        ur, ui = bank(st, 4 * s + m), bank(st, 4 * s + 2 + m)
                        hr, hi = H[:, o, m, :], H[:, o, 2 + m, :]
                        hr_i = H[:, o, 4, :] if m == 0 else hr
                        V.tensor_tensor(specY[:, m, :], ur, hr, ALU.mult)
                        link(V.tensor_tensor(spec_t, ui, hi, ALU.mult))
                        link(V.tensor_tensor(specY[:, m, :], specY[:, m, :], spec_t, ALU.subtract))
                        V.tensor_tensor(specY[:, 2 + m, :], ur, hi, ALU.mult).then_inc(ring.read(st, 4 * s + m), 1)
                        V.tensor_tensor(spec_t, ui, hr_i, ALU.mult).then_inc(ring.read(st, 4 * s + 2 + m), 1)
                        ring.wait_read(dve, st, 4 * s + 2 + m)
                        ins = V.tensor_tensor(specY[:, 2 + m, :], specY[:, 2 + m, :], spec_t, ALU.add)
                        if m == 0:
                            link(ins)
                    ins.then_inc(spec_done, 1)
                    for m in range((2, 4)[o]):
                        k = (2, 4)[o] * s + m
                        ring.wait_full(dve, f"idft_{o}", k)
                        if o == 0:
                            V.tensor_tensor(vtok[:, 2 * s + m, :], bank("idft_0", k), x1tok[:, 2 * s + m, :],
                                            ALU.mult).then_inc(ring.read("idft_0", k), 1)
                        else:
                            cols = slice(s * SEQ, (s + 1) * SEQ)
                            V.tensor_tensor(catH[:, m, cols], bank("idft_1", k)[:, 0:SEQ], x2T[:, m, cols],
                                            ALU.mult).then_inc(ring.read("idft_1", k), 1)

            dve.wait_ge(ret_in, 16 * len(ret_loads))
            for n in range(2 * NT):
                t = n % NT
                ring.wait_full(dve, "qk_proj", n)
                if n >= 2:
                    ring.wait_full(dve, "qk_turn", n - 2)
                    ring.wait_read(dve, "qk_proj", n - 2)
                dst, src = qk_tok[:, n % 2, :], bank("qk_proj", n)
                if t < 2:
                    V.tensor_copy(dst, src).then_inc(ring.read("qk_proj", n), 1)
                else:
                    rotate(dst, src, rope_r, rope_t[:, n % 2, :], t - 2, RET_HEADS, RET_DK // 2, ring.read("qk_proj", n))
            x_, e_, z_, p_ = (lgt[:, i, :] for i in range(4))
            link(V.tensor_scalar(e_, x_, -1.0, None, ALU.mult))
            V.tensor_tensor(e_, e_, x_, ALU.min).then_inc(decay_arg, 1)
            dve.wait_ge(decay_exp, 1)
            link(V.tensor_scalar(z_, e_, 2.0, None, ALU.add))
            link(V.reciprocal(z_, z_))
            link(V.tensor_tensor(z_, z_, e_, ALU.mult))
            link(V.tensor_tensor(e_, z_, z_, ALU.mult))
            link(V.tensor_scalar(p_, e_, 1.0 / 17.0, 1.0 / 15.0, ALU.mult, ALU.add))
            for k in (13, 11, 9, 7, 5, 3, 1):
                link(V.tensor_tensor(p_, p_, e_, ALU.mult))
                link(V.tensor_scalar(p_, p_, 1.0 / k, None, ALU.add))
            link(V.tensor_tensor(p_, p_, z_, ALU.mult))
            link(V.tensor_scalar(lg, x_, 0.0, None, ALU.min))
            link(V.scalar_tensor_tensor(out=lg, in0=p_, scalar=-2.0, in1=lg, op0=ALU.mult, op1=ALU.add))
            link(V.tensor_scalar(lgs[:, 0, :], lg, float(CTX), None, ALU.mult))
            link(V.tensor_scalar(lgs[:, 2, :], lg, -1.0, None, ALU.mult))
            link(V.tensor_scalar(dist_f, dist, 0.0, None, ALU.max))
            V.tensor_scalar(dist_b, dist, -1.0, 0.0, ALU.mult, ALU.max).then_inc(decay_arg, 1)
            flat2 = lambda v: v.rearrange("p a n -> p (a n)")
            KS = RET_DK ** -0.5
            for h in range(RET_HEADS):
                dve.wait_ge(decay_exp, 2 * h + 2)
                e0, e1 = (decay_e[:, i, :].rearrange("p (a n) -> p a n", a=2) for i in range(2))
                link(V.scalar_tensor_tensor(out=e0, in0=dist, scalar=0.0, in1=e0, op0=ALU.is_ge, op1=ALU.mult))
                link(V.scalar_tensor_tensor(out=e1, in0=dist, scalar=0.0, in1=e1, op0=ALU.is_le, op1=ALU.mult))
                link(V.tensor_tensor(e0, e0, e1, ALU.add))
                V.tensor_scalar(decay[:, :, 0, :], e0, KS, None, ALU.mult).then_inc(decay_used, 1)
                dve.wait_ge(decay_exp, 2 * h + 3)
                link(V.tensor_tensor(e0, e0, e1, ALU.add))
                V.tensor_scalar(decay[:, :, 1, :], e0, KS, None, ALU.mult).then_inc(decay_used, 1)
                dve.wait_ge(decay_used, 2 * h + 2)
                if h:
                    for t in range(NT):
                        ring.wait_full(dve, "ret_o", NT * (h - 1) + t)
                for kt in range(4):
                    ring.wait_full(dve, "ret_s", 4 * h + kt)
                    if kt < 2:
                        V.tensor_tensor(sT0[:, kt, :], bank("ret_s", 4 * h + kt),
                                        decay[:, kt].rearrange("p a n -> p (a n)"), ALU.mult)\
                            .then_inc(ring.read("ret_s", 4 * h + kt), 1)
                    else:
                        V.tensor_tensor(sT2[:, kt - 2, :], bank("ret_s", 4 * h + kt)[:, 0:SEQ], decay[:, kt - 2, 0, :],
                                        ALU.mult).then_inc(ring.read("ret_s", 4 * h + kt), 1)
                for t in range(NT):
                    n = NT * h + t
                    ring.wait_full(dve, "ret_o", n)
                    link(V.bn_stats(ret_stat[:, t, :], bank("ret_o", n)[:, 0:RET_DV]))
                    link(V.bn_aggr(ret_mv[:, t, :], ret_stat[:, t, :]))
                    V.tensor_scalar(ret_mv[:, t, 1:2], ret_mv[:, t, 1:2], EPS, None, ALU.add).then_inc(ret_var, 1)
                for t in range(NT):
                    n = NT * h + t
                    dve.wait_ge(ret_dev, n + 1)
                    link(V.reciprocal(ret_mv[:, t, 1:2], ret_mv[:, t, 1:2]))
                    if n >= 2:
                        ring.wait_full(dve, "ret_turn", n - 2)
                    r_ = ret_row[:, t % 2, :]
                    V.tensor_scalar(r_, bank("ret_o", n)[:, 0:RET_DV], ret_mv[:, t, 0:1], ret_mv[:, t, 1:2],
                                    ALU.subtract, ALU.mult).then_inc(ring.read("ret_o", n), 1)
                    ring.wait_read(dve, "ret_o", n)
                    V.tensor_tensor(r_, r_, g_tok[:, t, h * RET_DV:(h + 1) * RET_DV], ALU.mult).then_inc(ret_rows, 1)
            for k in range(2 * NT):
                ins = add_residual("out_0", k, k // 2, k % 2)
                if k % 2:
                    ins.then_inc(residual, 1)
            dve.wait_ge(residual, NT)

            def top8_mask(t):
                link(V.tensor_tensor(choice, scores[:, t, :], router_b, ALU.add))
                for g in range(NG):
                    ins = V.max(best[:, g, :], choice[:, g * 8:(g + 1) * 8])
                link(ins)
                link(V.tensor_tensor(gsum, best[:, :, 0], best[:, :, 1], ALU.add))
                link(V.max(gtop, gsum))
                link(V.max_index(gidx, gtop, gsum))
                link(V.tensor_copy(gidxf, gidx))
                link(V.tensor_tensor(geq, iota8, gidxf[:, 0:TOPG].unsqueeze(2).broadcast_to([P, TOPG, NG]), ALU.is_equal))
                link(V.tensor_reduce(gmask, geq.rearrange("p k g -> p g k"), AX_X, ALU.add))
                link(V.tensor_scalar(gneg, gmask, 1.0, BIG, ALU.subtract, ALU.mult))
                c3 = choice.rearrange("p (g n) -> p g n", g=NG)
                link(V.tensor_tensor(c3, c3, gmask.unsqueeze(2).broadcast_to([P, NG, NE // NG]), ALU.mult))
                link(V.tensor_tensor(c3, c3, gneg.unsqueeze(2).broadcast_to([P, NG, NE // NG]), ALU.add))
                link(V.max(gtop, choice))
                link(V.match_replace(replaced, gtop, choice, -3e38))
                return V.tensor_tensor(picked[:, t, :], replaced, choice, ALU.not_equal)

            def slots_of(ids, weights, spare, where, out_u, signal):
                link(V.tensor_copy(ids, where[:, :, 0]))
                link(V.tensor_copy(weights, where[:, :, 1]))
                link(V.scalar_tensor_tensor(out=spare, in0=ids, scalar=0.0, in1=spare_id1.broadcast_to(list(ids.shape)),
                                            op0=ALU.is_equal, op1=ALU.mult))
                link(V.tensor_tensor(ids, ids, spare, ALU.add))
                V.tensor_scalar(out_u, ids, 1.0, None, ALU.subtract).then_inc(signal, 1)

            def overflow_dve(l):
                t0, tiles = LT[l]
                nb = tiles - 1
                step = M["step", l]
                with overflow(dve, l):
                    dve.wait_ge(E["scattered", l], 16 * NE)
                    with dve.Fori(0, NE) as e:
                        for b in range(nb):
                            n = e * nb + b
                            oh = one_hot[:, 0, 0:tiles, :]
                            V.tensor_scalar(oh, iota1.unsqueeze(1).broadcast_to([P, tiles, P]), float(P * (b + 1)),
                                            None, ALU.add).then_inc(step, 1)
                            dve.wait_ge(step, n * 5 + 1)
                            V.tensor_tensor(oh, pos1[:, t0:t0 + tiles, bass.ds(e, 1)].broadcast_to([P, tiles, P]), oh,
                                            ALU.is_equal).then_inc(M["dve", l], 1)
                            dve.wait_ge(M["pe", l], n * 5 + 1)
                            V.tensor_copy(slot_id[:, 0:1], ps[:, 7, 0:1]).then_inc(step, 1)
                            V.tensor_copy(slot_w[:, 0:1], ps[:, 7, 1:2]).then_inc(step, 1)
                            dve.wait_ge(step, n * 5 + 3)
                            V.scalar_tensor_tensor(out=slot_empty[:, 0:1], in0=slot_id[:, 0:1], scalar=0.0, in1=spare_id1,
                                                   op0=ALU.is_equal, op1=ALU.mult).then_inc(step, 1)
                            dve.wait_ge(step, n * 5 + 4)
                            V.tensor_tensor(slot_id[:, 0:1], slot_id[:, 0:1], slot_empty[:, 0:1], ALU.add).then_inc(step, 1)
                            dve.wait_ge(step, n * 5 + 5)
                            V.tensor_scalar(gather_idx[:, 0, :], slot_id[:, 0:1], 1.0, None, ALU.subtract)\
                                .then_inc(M["dve", l], 1)
                            dve.wait_ge(M["act", l], n * 4 + 2)
                            V.scalar_tensor_tensor(out=act[:, 0, :], in0=ps[:, 2, ED:2 * ED], scalar=slot_w[:, 0:1],
                                                   in1=gsil[:, 0, :], op0=ALU.mult, op1=ALU.mult).then_inc(M["dve", l], 1)
                            dve.wait_ge(M["pe", l], n * 5 + 5)
                            V.tensor_copy(yb[:, 1, 512:], ps[:, 6, :]).then_inc(M["dve", l], 1)
                            dve.wait_ge(M["out", l], n * 16 + 16)

            def experts_phase(l):
                t0, tiles = LT[l]
                before = (0, NT)[l]
                dve.wait_ge(moe_in, 16 * len(moe_loads(0)) * (l + 1))
                for k in range(tiles):
                    t = t0 + k
                    ring.wait_read(dve, f"route_{l}", k)
                    top8_mask(t).then_inc(picks, 1)
                    dve.wait_ge(picks, before + k + 1)
                    link(V.tensor_tensor_reduce(out=replaced, in0=scores[:, t, :], in1=picked[:, t, :], scale=1.0,
                                                scalar=0.0, op0=ALU.mult, op1=ALU.add, accum_out=wsum))
                    link(V.tensor_scalar(wsum, wsum, 1e-20, None, ALU.add))
                    link(V.reciprocal(wsum, wsum))
                    V.tensor_scalar(idw[:, t, :, 1], replaced, wsum, ROUTED_SCALE, ALU.mult, ALU.mult)
                    V.tensor_copy(idw[:, t, :, 0], token_id1[:, t:t + 1].broadcast_to([P, NE])).then_inc(id_weights, 1)
                for k in range(tiles + 1):
                    ring.wait_full(dve, f"pos_{l}", k)
                    b = bank(f"pos_{l}", k)[:, 0:NE]
                    if k < tiles:
                        V.scalar_tensor_tensor(out=pos1[:, t0 + k, :], in0=b, scalar=1.0, in1=picked[:, t0 + k, :],
                                               op0=ALU.add, op1=ALU.mult).then_inc(ring.read(f"pos_{l}", k), 1)
                        ring.wait_read(dve, f"pos_{l}", k)
                    else:
                        V.tensor_reduce(counts_max, b, AX_X, ALU.max).then_inc(ring.read(f"pos_{l}", k), 1)
                        ring.wait_read(dve, f"pos_{l}", k)
                        V.tensor_scalar(flags[:, l:l + 1], counts_max, P + 0.5, None, ALU.is_gt).then_inc(flag_ready, 1)
                for t in range(tiles):
                    dve.wait_ge(sh_silu, before + t + 1)
                    if t >= 2:
                        ring.wait_full(dve, f"sh_t_{l}", t - 2)
                    V.tensor_tensor(act[:, t % 2, :], bank(f"sh_gu_{l}", t)[:, ED:2 * ED], gsil[:, t % 2, :], ALU.mult)\
                        .then_inc(ring.read(f"sh_gu_{l}", t), 1)
                    ring.wait_full(dve, f"sh_y_{l}", 2 * t + 1)
                    if t >= 2:
                        dve.wait_ge(shared_out[t % 2], 16)
                    V.tensor_copy(yb[:, t % 2, 512:], bank(f"sh_y_{l}", 2 * t + 1)).then_inc(ring.read(f"sh_y_{l}", 2 * t + 1), 1)
                for i in range(2):
                    dve.wait_ge(shared_out[i], (32, 48)[l])

                def one_hot_of(e, u):
                    V.tensor_tensor(one_hot[:, u, 0:tiles, :],
                                    pos1[:, t0:t0 + tiles, bass.ds(e, 1)].broadcast_to([P, tiles, P]),
                                    iota1.unsqueeze(1).broadcast_to([P, tiles, P]), ALU.is_equal).then_inc(hot, 1)

                for u in range(2):
                    one_hot_of(u, u)
                with dve.Fori(1, NE // 2) as i:
                    for u in range(2):
                        dve.wait_ge(hot_used, i * 2 + (u - 1 + NE * l))
                        one_hot_of(i * 2 + u, u)
                dve.wait_ge(hot_used, NE * (l + 1))
                tab = ps[:, 7, 0:2 * NE].rearrange("p (e c) -> p e c", c=2)
                slots_of(slot_id, slot_w, slot_empty, tab, slot_u, slot_table)

                def rows_out_half(e, i):
                    dve.wait_ge(E["y_full", l], e + 1)
                    at_least(dve, E["scattered", l], 16 * (e - 1) if isinstance(e, int) else e * 16 - 16)
                    V.tensor_copy(yb[:, i, 512:], ps[:, 6, :]).then_inc(E["y_read_d", l], 1)

                def step(e, i):
                    dve.wait_ge(E["sg_done", l], e + 1)
                    at_least(dve, E["aT_full", l], e - 1)
                    w = slot_w[:, e:e + 1] if isinstance(e, int) else slot_w[:, bass.ds(e, 1)]
                    V.scalar_tensor_tensor(out=act[:, i, :], in0=ps[:, 2 + i, ED:2 * ED], scalar=w, in1=gsil[:, i, :],
                                           op0=ALU.mult, op1=ALU.mult).then_inc(E["act_done", l], 1)
                    if not isinstance(e, int) or e > 0:
                        rows_out_half(e - 1, 1 - i)

                for e in range(4):
                    step(e, e % 2)
                with dve.Fori(1, NE // 4 - 1) as i4:
                    for r in range(4):
                        step(i4 * 4 + r, r % 2)
                for e in range(NE - 4, NE):
                    step(e, e % 2)
                rows_out_half(NE - 1, 1)
                overflow_dve(l)
                dve.wait_ge(acc_in, 16 * (l + 1))
                for k in range(tiles):
                    t = t0 + k
                    a_ = ACC[:, k, :]
                    link(V.tensor_tensor(a_, a_, bc[:, t // 2, 2, :], ALU.mult))
                    ins = V.tensor_tensor(X[:, t, :], X[:, t, :], a_, ALU.add)
                    if k < tiles - 1:
                        ins.then_inc(residual, 1)
                    else:
                        ins.then_inc(moe_done, 1)

            mods("0b")
            norm_rows("0b", (0, 1))
            experts_phase(0)

            dve.wait_ge(residual, 2 * NT - 1)
            dve.wait_ge(moe_done, 1)
            mods("1a")
            norm_rows("1a", (0, 1))
            dve.wait_ge(da_in_sem, 16 * len(da_loads))
            for n, (c, t) in enumerate(DA_USES):
                ring.wait_full(dve, "da_qk", n)
                if n >= 2:
                    ring.wait_full(dve, "da_turn", n - 2)
                    ring.wait_read(dve, "da_qk", n - 2)
                dst, src = qk_da[:, n % 2, :], bank("da_qk", n)
                if t < 2:
                    V.tensor_copy(dst, src).then_inc(ring.read("da_qk", n), 1)
                else:
                    rotate(dst, src, rope_d, rope_dt[:, n % 2, :], t - 2, 8, DA_HD // 2, ring.read("da_qk", n))
            for i in range(2):
                ins = V.tensor_tensor_reduce(out=lamv[:, 2 * i, :], in0=lamv[:, 2 * i, :], in1=lamv[:, 2 * i + 1, :],
                                             scale=1.0, scalar=0.0, op0=ALU.mult, op1=ALU.add,
                                             accum_out=lamt[:, i:i + 1])
            ins.then_inc(lam_sums, 1)
            dve.wait_ge(lam_exp, 1)
            link(V.tensor_tensor(lamt[:, 2:3], lamt[:, 1:2], lamt[:, 0:1], ALU.subtract))
            link(V.tensor_scalar(lamt[:, 2:3], lamt[:, 2:3], LAMBDA_INIT, None, ALU.subtract))
            sc = DA_HD ** -0.5

            def mix(n):
                i = n % 2
                for c in range(2):
                    ring.wait_read(dve, "da_s", 2 * n + c)
                link(V.reciprocal(sinv[:, i, :], ssum[:, i, :]))
                link(V.tensor_tensor(sinv[:, i, 1:2], sinv[:, i, 1:2], lamt[:, 2:3], ALU.mult))
                if n >= 2:
                    ring.wait_full(dve, "da_at", n - 2)
                link(V.tensor_scalar(adiff[:, i, :], prob[:, i, 0, :], sinv[:, i, 0:1], None, ALU.mult))
                V.scalar_tensor_tensor(out=adiff[:, i, :], in0=prob[:, i, 1, :], scalar=sinv[:, i, 1:2],
                                       in1=adiff[:, i, :], op0=ALU.mult, op1=ALU.add).then_inc(probs_mixed, 1)

            for n in range(2 * DA_HEADS + 1):
                if n < 2 * DA_HEADS:
                    i = n % 2
                    if n >= 2:
                        for c in range(2):
                            ring.wait_read(dve, "da_s", 2 * (n - 2) + c)
                    for c in range(2):
                        ring.wait_full(dve, "da_s", 2 * n + c)
                        ins = V.tensor_reduce(smax[:, i, c:c + 1], bank("da_s", 2 * n + c), AX_X, ALU.max)
                    link(ins)
                    V.tensor_scalar(smax[:, i, :], smax[:, i, :], -sc, None, ALU.mult).then_inc(score_max, 1)
                if n:
                    mix(n - 1)
            for qt in range(2):
                for m in range(DA_HEADS):
                    ring.wait_read(dve, "da_o", qt * DA_HEADS + m)
                o3 = o_tok[:, qt, :].rearrange("p (h d) -> p h d", h=DA_HEADS)
                link(V.tensor_tensor(o_squares, o3, o3, ALU.mult))
                link(V.tensor_reduce(ohs[:, qt, :], o_squares, AX_X, ALU.add))
                V.tensor_scalar(ohs[:, qt, :], ohs[:, qt, :], 1.0 / P, 1e-5, ALU.mult, ALU.add).then_inc(o_var, 1)
            link(V.tensor_scalar(subln, subln, 1.0 - LAMBDA_INIT, None, ALU.mult))
            for qt in range(2):
                dve.wait_ge(o_dev, qt + 1)
                o3 = o_tok[:, qt, :].rearrange("p (h d) -> p h d", h=DA_HEADS)
                link(V.reciprocal(ohs[:, qt, :], ohs[:, qt, :]))
                link(V.tensor_tensor(o3, o3, ohs[:, qt, :].unsqueeze(2).broadcast_to([P, DA_HEADS, P]), ALU.mult))
                V.tensor_tensor(o3, o3, subln.unsqueeze(1).broadcast_to([P, DA_HEADS, P]), ALU.mult).then_inc(o_rows, 1)
            for k in range(4):
                ins = add_residual("out_1", k, 2 + k // 2, k % 2)
                if k % 2:
                    ins.then_inc(residual, 1)
                else:
                    link(ins)
            dve.wait_ge(residual, 2 * NT - 1 + 2)
            mods("1b")
            norm_rows("1b", (1,))
            experts_phase(1)
            dve.wait_ge(residual, 2 * NT - 1 + 3)
            dve.wait_ge(moe_done, 2)
            norm_inverse("final")
            dve.wait_ge(final_in, 16)
            for j in range(2):
                V.scalar_tensor_tensor(out=hrow_mix[:, j, :], in0=X[:, 2 + j, :], scalar=rstd[:, 2 + j:3 + j],
                                       in1=final_g, op0=ALU.mult, op1=ALU.mult).then_inc(result, 1)

        @block.gpsimd
        def _(pool):
            def overflow_pool(l):
                nb = LT[l][1] - 1
                last_row = pool.alloc_register(f"more_last_row_{l}")
                with overflow(pool, l), pool.Fori(0, NE) as e:
                    for b in range(nb):
                        n = e * nb + b
                        pool.wait_ge(M["dve", l], n * 4 + 2)
                        pool.reg_add(last_row, pool.zero_reg, NTOK + P - 1)
                        pool.indirect_dma_start(xg[:, 0, :], None, h_rows,
                                                bass.IndirectOffsetOnAxis(gather_idx[:, 0, :], 0),
                                                bounds_check=last_row).then_inc(M["xg", l], 16)
                        pool.wait_ge(M["dve", l], n * 4 + 4)
                        pool.wait_ge(M["act", l], n * 4 + 4)
                        pool.reg_add(last_row, pool.zero_reg, NTOK + P - 1)
                        pool.indirect_dma_start(acc_rows, bass.IndirectOffsetOnAxis(gather_idx[:, 0, :], 0),
                                                yb[:, 1, :], None, compute_op=ALU.add,
                                                bounds_check=last_row).then_inc(M["out", l], 16)
                        pool.wait_ge(M["out", l], n * 16 + 16)

            def experts_phase(l):
                t0, tiles = LT[l]
                if l == 0:
                    pool.wait_ge(residual, NT)
                    nc.gpsimd.memset(ZERO, 0.0).then_inc(spare_zero, 1)
                    pool.wait_ge(spare_zero, 1)
                    pool.dma_start(h_rows[NTOK:NTOK + P, :], ZERO).then_inc(spare_out, 16)
                    pool.dma_start(acc_rows[NTOK:NTOK + P, :], ZERO).then_inc(spare_out, 16)
                for j in range(tiles):
                    pool.wait_ge(rows, ROWS_BEFORE[f"{l}b"] + j + 1)
                    t = t0 + j
                    pool.dma_start(h_rows[t * P:(t + 1) * P, :], hrow_moe[:, j % 2, :]).then_inc(rows_out[j % 2], 16)
                for j in range(tiles):
                    for half in range(2):
                        ring.wait_read(pool, f"sh_y_{l}", 2 * j + half)
                    t = t0 + j
                    pool.dma_start(acc_rows[t * P:(t + 1) * P, :], yb[:, j % 2, :]).then_inc(shared_out[j % 2], 16)
                pool.wait_ge(spare_out, 32)
                for i in range(2):
                    pool.wait_ge(rows_out[i], (32, 48)[l])
                pool.wait_ge(slot_table, l + 1)

                last_row = pool.alloc_register(f"last_row_{l}")

                def gather(e, u):
                    col_ = slot_u[:, e:e + 1] if isinstance(e, int) else slot_u[:, bass.ds(e, 1)]
                    nc.gpsimd.tensor_copy(gather_idx[:, u, :], col_).then_inc(E["gidx", l], 1)
                    pool.wait_ge(E["gidx", l], e + 1)
                    at_least(pool, E["xT_full", l], e - 1)
                    pool.reg_add(last_row, pool.zero_reg, NTOK + P - 1)
                    pool.indirect_dma_start(xg[:, u % 2, :], None, h_rows,
                                            bass.IndirectOffsetOnAxis(gather_idx[:, u, :], 0),
                                            bounds_check=last_row).then_inc(E[f"xg_in_{u % 2}", l], 16)

                def scatter(e, u):
                    col_ = slot_u[:, e:e + 1] if isinstance(e, int) else slot_u[:, bass.ds(e, 1)]
                    nc.gpsimd.tensor_copy(scatter_idx[:, u, :], col_).then_inc(E["sidx", l], 1)
                    pool.wait_ge(E["sidx", l], e + 1)
                    at_least(pool, E["scattered", l], e * 16)
                    pool.wait_ge(E["y_read_a", l], e + 1)
                    pool.wait_ge(E["y_read_d", l], e + 1)
                    pool.reg_add(last_row, pool.zero_reg, NTOK + P - 1)
                    pool.indirect_dma_start(acc_rows, bass.IndirectOffsetOnAxis(scatter_idx[:, u, :], 0),
                                            yb[:, u % 2, :], None, compute_op=ALU.add,
                                            bounds_check=last_row).then_inc(E["scattered", l], 16)

                gather(0, 0)
                gather(1, 1)
                for i in range(2):
                    pool.wait_ge(shared_out[i], (32, 48)[l])
                for e in range(2):
                    gather(e + 2, e + 2)
                    scatter(e, e)
                with pool.Fori(0, NE // 4 - 1) as i4:
                    for r in range(4):
                        e = i4 * 4 + (r + 2)
                        gather(i4 * 4 + (r + 4), r)
                        scatter(e, (r + 2) % 4)
                for e in range(NE - 2, NE):
                    scatter(e, e % 4)
                pool.wait_ge(E["scattered", l], 16 * NE)
                overflow_pool(l)
                pool.dma_start(ACC[:, 0:tiles, :], acc_rows[t0 * P:(t0 + tiles) * P, :].rearrange("(t p) n -> p t n", p=P))\
                    .then_inc(acc_in, 16)

            experts_phase(0)
            experts_phase(1)
            pool.wait_ge(acc_in, 32)


_INS = ['x', 'c', 'ctx', 'c_ctx', 'w_ada', 'b_ada', 'norm_mix', 'norm_ffn', 'ab_w_in', 'ab_w_out', 'ret_decay_logit',
        'hy_conv_w', 'hy_conv_b', 'hy_w1', 'hy_b1', 'hy_freq1', 'hy_w2', 'hy_b2', 'hy_freq2', 'hy_w3', 'hy_skip',
        'da_w_in', 'da_w_out', 'da_lambda', 'da_subln', 'router_w', 'router_b', 'exp_w_gate', 'exp_w_up', 'exp_w_down',
        'sh_w_gate', 'sh_w_up', 'sh_w_down', 'norm_final']


def kernel(**inputs):
    import numpy as _np
    import concourse.bacc as _bacc
    from concourse import mybir as _mybir
    from concourse.bass_utils import run_bass_kernel_spmd as _run

    nc = _bacc.Bacc("TRN2", target_bir_lowering=False, num_devices=1)
    arrays, A, K = {}, {}, {}
    for name in _INS:
        a = _np.ascontiguousarray(inputs[name])
        arrays[f"in_{name}"] = a
        A[name] = nc.dram_tensor(f"in_{name}", a.shape, _mybir.dt.from_np(a.dtype), kind="ExternalInput").ap()
    for name, a in shape_constants().items():
        a = _np.ascontiguousarray(a)
        arrays[f"const_{name}"] = a
        K[name] = nc.dram_tensor(f"const_{name}", a.shape, _mybir.dt.from_np(a.dtype), kind="ExternalInput").ap()
    out = nc.dram_tensor("out_0", (1, SEQ, D), F32, kind="ExternalOutput").ap()
    build(nc, A, K, out)
    r = _run(nc, [arrays], core_ids=[0])
    return r.results[0]["out_0"]
```

```python
import math
from contextlib import ExitStack, contextmanager

import numpy as np

import concourse.bass as bass
from concourse import mybir

F32 = mybir.dt.float32
I32 = mybir.dt.int32
U32 = mybir.dt.uint32
ALU = mybir.AluOpType
ACT = mybir.ActivationFunctionType
AX_X = mybir.AxisListType.X

P = 128
D = 1024
KC = D // P
SEQ = 256
CTX = 256
NTOK = CTX + SEQ
NT = NTOK // P
DEPTH = 2
EPS = 1e-6
GRID_W = 64
ROPE_BASE = 10000.0

RET_HEADS, RET_DK, RET_DV = 4, 128, 256
RET_V = RET_HEADS * RET_DV
HW = 512
HY_BANDS = 16
HY_EMB = 2 * HY_BANDS + 1
HY_FFN = 64
NFFT = 2 * SEQ

DA_HEADS, DA_HD = 8, 64
LAMBDA_INIT = 0.8 - 0.6 * math.exp(-0.3)

NE = 64
NG = 8
TOPG = 4
TOPK = 8
ED = 256
ROUTED_SCALE = 2.5

BANKS = 8
DENSE_SLOTS = 3
EXPERT_SLOTS = 4
XG = 4
YB = 4
TABLES_FIRST = 5
BIG = 1e30

TWO_PI = 2.0 * math.pi
MAGIC = 12582912.0
PI_1 = 6.28125
PI_2 = float(np.float32(TWO_PI - PI_1))
PI_3 = float(np.float32(TWO_PI - PI_1 - PI_2))
PI_SAFE = 3.1415925


def shape_constants():
    f32 = np.float32
    k = {}
    k["ident"] = np.eye(P, dtype=f32)
    t = np.arange(SEQ, dtype=np.float64)
    tn = t / (SEQ - 1)
    bands = np.linspace(1e-4, HY_BANDS - 1, HY_BANDS)
    ang = (2.0 * math.pi / SEQ) * t[:, None] * bands[None, :]
    k["filter_features"] = np.concatenate([tn[:, None], np.cos(ang), -np.sin(ang)], axis=1).T.astype(f32)
    deltas = np.abs(np.linspace(math.log(1e-2) / 1.5, math.log(1e-2) / 0.3, HW))
    window = np.exp(-tn[:, None] * deltas[None, :])
    k["window"] = window.reshape(2, P, HW).transpose(1, 0, 2).astype(f32)
    f = np.arange(SEQ, dtype=np.float64)
    w = 2.0 * math.pi / NFFT
    re_f, im_f = np.cos(w * np.outer(t, f)), -np.sin(w * np.outer(t, f))
    nyquist = np.cos(math.pi * t)
    im_packed = im_f.copy()
    im_packed[:, 0] = nyquist
    re_nyq = re_f[:, 0:P].copy()
    re_nyq[:, 0] = nyquist
    fwd = np.concatenate([re_f, im_packed, im_f[:, 0:P], re_nyq], axis=1)
    k["dft_fwd"] = fwd.reshape(2, P, 6 * P).transpose(1, 0, 2).astype(f32)
    bwd = np.concatenate([re_f, -im_packed, -im_f[:, 0:P], re_nyq], axis=1)
    bwd[:, 2 * P * 1] = 0.0
    bwd[0, :] = 0.0
    k["dft_bwd"] = bwd.reshape(2, P, 6 * P).transpose(1, 0, 2).astype(f32)
    inv = np.zeros((NFFT, SEQ))
    inv[0:SEQ] = 2.0 * re_f.T
    inv[0] = 1.0
    inv[SEQ:] = 2.0 * im_f.T
    inv[SEQ] = nyquist
    inv /= NFFT
    k["dft_inv"] = inv.reshape(4, P, SEQ).transpose(1, 0, 2).astype(f32)
    for name, hd in (("rope_ret", RET_DK), ("rope_da", DA_HD)):
        nf = hd // 4
        fr = ROPE_BASE ** (-np.arange(nf, dtype=np.float64) / nf)
        row, col = np.repeat(np.arange(SEQ // GRID_W), GRID_W), np.tile(np.arange(GRID_W), SEQ // GRID_W)
        a = np.concatenate([row[:, None] * fr, col[:, None] * fr], axis=-1)
        cs = np.stack([np.cos(a), np.sin(a)], axis=0).reshape(2, 2, P, hd // 2)
        k[name] = cs.transpose(2, 0, 1, 3).reshape(P, 2 * 2 * (hd // 2)).astype(f32)
    i, j = np.arange(SEQ), np.arange(SEQ)
    k["distance"] = (i[None, :] - j[:, None]).reshape(2, P, SEQ).transpose(1, 0, 2).astype(f32)
    k["iota1"] = np.tile(np.arange(1, P + 1, dtype=f32), (P, 1))
    k["iota8"] = np.tile(np.arange(NG, dtype=f32), (P, TOPG)).reshape(P, TOPG * NG)
    k["earlier"] = (np.arange(P)[:, None] < np.arange(P)[None, :]).astype(f32)
    k["ones"] = np.ones((P, P), f32)
    k["token_id1"] = (np.arange(NT)[None, :] * P + np.arange(P)[:, None] + 1).astype(f32)
    k["spare_id1"] = (1 + np.arange(P)[:, None]).astype(f32)
    k["expert_no"] = np.tile(np.arange(NE, dtype=f32), (P, 1))
    sel = np.zeros((2, 2, P), f32)
    sel[0, 0], sel[1, 1] = 1.0, 1.0
    k["stream_select"] = sel
    return k


class BankRing:

    def __init__(self, order, bank_full, bank_read):
        self.order, self.bank_full, self.bank_read = order, bank_full, bank_read
        self.at = {use: n for n, use in enumerate(order)}
        self.claimed = 0

    def bank(self, stage, k):
        return self.at[(stage, k)] % BANKS

    def claim(self, pe, stage, k):
        n = self.at[(stage, k)]
        assert n == self.claimed, (stage, k, self.order[self.claimed])
        self.claimed += 1
        if n >= BANKS:
            pe.wait_ge(self.bank_read[n % BANKS], n // BANKS)

    def full(self, stage, k):
        return self.bank_full[self.bank(stage, k)]

    def read(self, stage, k):
        return self.bank_read[self.bank(stage, k)]

    def wait_full(self, eng, stage, k):
        n = self.at[(stage, k)]
        eng.wait_ge(self.bank_full[n % BANKS], n // BANKS + 1)

    def wait_read(self, eng, stage, k):
        n = self.at[(stage, k)]
        eng.wait_ge(self.bank_read[n % BANKS], n // BANKS + 1)

    def fence(self, pe):
        for n in range(self.claimed - BANKS, self.claimed):
            pe.wait_ge(self.bank_read[n % BANKS], n // BANKS + 1)


class Chain:

    def __init__(self, eng, sem):
        self.eng, self.sem, self.n = eng, sem, 0

    def __call__(self, ins):
        self.n += 1
        ins.then_inc(self.sem, 1)
        self.eng.wait_ge(self.sem, self.n)


def psum_order():
    o = [("filter_a", 0), ("filter_b", 0)]
    o += [("filter_c", k) for k in range(8)]
    o += [("filter_dft", k) for k in range(10)]

    def ada(tag, streams):
        return [(f"mod_{tag}", k) for k in range(6)] + [(f"bcast_{tag}", k) for k in range(6 * streams)]

    def norm(tag, tiles):
        return [(f"norm_{tag}", k) for k in range(2 * tiles)]

    def moe(tag, tiles):
        r = [(f"route_{tag}", k) for k in range(tiles)] + [(f"sh_gu_{tag}", 0)]
        r += [(f"pos_{tag}", k) for k in range(tiles + 1)] + [(f"sh_gu_{tag}", 1)]
        r += [(f"table_{tag}", e) for e in range(TABLES_FIRST)]
        for t in range(tiles):
            if t >= 2:
                r.append((f"sh_gu_{tag}", t))
            r += [(f"sh_t_{tag}", t), (f"sh_y_{tag}", 2 * t), (f"sh_y_{tag}", 2 * t + 1)]
        return r

    o += ada("0a", 2) + norm("0a", NT)
    for m in range(12):
        o.append(("u_proj", m))
        if 1 <= m <= 8:
            o.append(("u_turn", m - 1))
    for order in range(2):
        for s in range(2):
            o += [(f"dft_{order}", 4 * s + m) for m in range(4)]
            o += [(f"idft_{order}", (2, 4)[order] * s + m) for m in range((2, 4)[order])]
    for c in range(2):
        for t in range(NT):
            o.append(("qk_proj", c * NT + t))
            if c * NT + t:
                o.append(("qk_turn", c * NT + t - 1))
    o.append(("qk_turn", 2 * NT - 1))
    o += [("vg_proj", k) for k in range(4 * NT)]
    for h in range(RET_HEADS):
        o += [("ret_s", 4 * h + k) for k in range(4)]
        o += [("ret_o", NT * h + t) for t in range(NT)]
        o += [("ret_turn", NT * h + t) for t in range(NT)]
    o += [("out_0", k) for k in range(2 * NT)]
    o += ada("0b", 2) + norm("0b", NT) + moe("0", NT)
    o += ada("1a", 2) + norm("1a", NT)
    n = 0
    for c in range(4):
        for t in range(NT):
            if c < 2 and t < 2:
                continue
            o.append(("da_qk", n))
            if n:
                o.append(("da_turn", n - 1))
            n += 1
    o.append(("da_turn", n - 1))
    o += [("da_v", k) for k in range(2 * NT)]
    for n in range(2 * DA_HEADS + 1):
        if n < 2 * DA_HEADS:
            o += [("da_s", 2 * n), ("da_s", 2 * n + 1)]
        if n:
            o += [("da_at", n - 1), ("da_o", n - 1)]
    o += [("da_ot", k) for k in range(4)]
    o += [("out_1", k) for k in range(4)]
    o += ada("1b", 1) + norm("1b", 2) + moe("1", 2)
    return o


def build(nc, A, K, out):
    with ExitStack() as ctx:
        def sb(name, shape, dt=F32, scope=ctx):
            return scope.enter_context(nc.sbuf_tensor(name, shape, dt))

        sems = {}

        def sem(name):
            if name not in sems:
                sems[name] = ctx.enter_context(nc.semaphore(name))
            return sems[name]

        order = psum_order()
        ring = BankRing(order, [sem(f"bank_full_{b}") for b in range(BANKS)],
                        [sem(f"bank_read_{b}") for b in range(BANKS)])
        ps = ctx.enter_context(nc.psum_tensor("ps", [P, BANKS, 512], F32))

        def bank(stage, k):
            return ps[:, ring.bank(stage, k), :]

        h_rows = nc.dram_tensor("h_rows", (NTOK, D), F32, kind="Internal").ap()
        y_rows = nc.dram_tensor("y_rows", (NE * NTOK, D), F32, kind="Internal").ap()



        WORDS = 53000
        arena = sb("arena", [P, WORDS])

        class Region:
            def __init__(self, at, end=WORDS):
                self.at, self.end = at, end

            def take(self, *shape, parts=P, dt=F32):
                n = math.prod(shape)
                assert self.at + n <= self.end, (self.at, n, self.end)
                v = arena[0:parts, self.at:self.at + n]
                if dt != F32:
                    v = v.bitcast(dt)
                self.at += n
                names = ["a", "b", "c", "d"][:len(shape)]
                if len(shape) > 1:
                    v = v.rearrange(f"p ({' '.join(names)}) -> p {' '.join(names)}", **dict(zip(names, shape)))
                return v

        top = Region(0)
        WS = top.take(EXPERT_SLOTS, KC * 512)
        spare_at = top.at - KC * 512
        X = top.take(NT, D)
        bc = top.take(2, 3, D)
        hT = top.take(KC, NTOK)
        ident = top.take(P)
        select = top.take(2, P, parts=2)
        cvec = top.take(2, KC)
        csilu = top.take(2, KC)
        ssq = top.take(NT)
        rstd = top.take(NT)
        flags = top.take(DEPTH, dt=I32)
        scratch_at = top.at
        modrow = top.take(3 * D, parts=2)
        normrow = top.take(D, parts=2)
        phase_at = top.at

        r = Region(scratch_at, phase_at)
        router_w = r.take(KC, NE)
        router_b = r.take(NE)
        scores = r.take(NT, NE)
        picked = r.take(NT, NE)
        pos1 = r.take(NT, NE)
        idw = r.take(NT, NE, 2)
        choice = r.take(NE)
        replaced = r.take(NE)
        best = r.take(NG, 8)
        gsum = r.take(NG)
        gtop = r.take(8)
        gidx = r.take(8, dt=U32)
        gidxf = r.take(8)
        geq = r.take(TOPG, NG)
        gmask = r.take(NG)
        gneg = r.take(NG)
        wsum = r.take(1)
        counts_max = r.take(1)
        slot_w = r.take(NE)
        slot_empty = r.take(2)
        row_sum = r.take(NE)
        row_best = r.take(8)
        combine_idx = r.take(NT, TOPK, dt=U32)
        slot_u = r.take(NE, dt=U32)
        gather_idx = r.take(XG, 1, dt=U32)
        r = Region(phase_at)
        DN = r.take(EXPERT_SLOTS, 2 * D)
        xg = r.take(XG, D)
        xgT = r.take(2, D)
        gsil = r.take(2, ED)
        act = r.take(2, ED)
        actT = r.take(2, 2 * P)
        iota1 = r.take(P)
        iota8 = r.take(TOPG, NG)
        earlier = r.take(P)
        ones = r.take(P)
        token_id1 = r.take(NT)
        spare_id1 = r.take(1)
        expert_no = r.take(NE)
        one_hot = r.take(2, NT, P)
        yb = hT.rearrange("p a n -> p (a n)").rearrange("p (a n) -> p a n", a=YB)
        combined = Region(phase_at).take(2, 4, D)
        combine_sum = xgT[:, 0, :]

        r = Region(phase_at)
        H = r.take(2, 5, HW)
        dftf = r.take(2, 6 * P)
        dfti = r.take(4, SEQ)
        sub_at = r.at
        r = Region(WORDS - 4 * NTOK)
        catH = r.take(4, NTOK)
        r = Region(sub_at, WORDS - 4 * NTOK)
        window = r.take(2, HW)
        dftb = r.take(2, 6 * P)
        fz = r.take(SEQ, parts=HY_EMB)
        fw1 = r.take(HY_FFN, parts=HY_EMB)
        fw2 = r.take(HY_FFN, parts=HY_FFN)
        fw3 = r.take(4 * HW, parts=HY_FFN)
        fcol = r.take(4, parts=HY_FFN)
        farg = r.take(SEQ, parts=HY_FFN)
        fturn = r.take(SEQ, parts=HY_FFN)
        fh = r.take(2, SEQ, parts=HY_FFN)
        skiprow = r.take(2, HW, parts=1)
        r = Region(spare_at, spare_at + KC * 512)
        filt = r.take(2, 4, HW)
        r = Region(sub_at, WORDS - 4 * NTOK)
        vtok = r.take(NT, HW)
        x1tok = r.take(NT, HW)
        uconv = r.take(2, NTOK)
        specY = r.take(4, HW)
        r = Region(WORDS - 4 * NTOK)
        cw = r.take(3, 12)
        cb = r.take(12)
        r = Region(spare_at, spare_at + KC * 512)
        x2T = r.take(4, NTOK)
        upad = r.take(2, 2, SEQ + 2)
        spec_t = r.take(HW)
        r = Region(phase_at, WORDS - 4 * NTOK)
        v_tok = r.take(NT, RET_V)
        g_tok = r.take(NT, RET_V)
        qT = r.take(RET_HEADS, NTOK)
        kT = r.take(RET_HEADS, NTOK)
        qk_tok = r.take(2, 512)
        rope_r = r.take(2, 2, RET_DK // 2)
        rope_t = r.take(2, 256)
        dist = r.take(2, SEQ)
        r = Region(spare_at, spare_at + KC * 512)
        dist_f = r.take(2, SEQ)
        dist_b = r.take(2, SEQ)
        decay = r.take(2, 2, SEQ)
        decay_e = r.take(2, 2 * SEQ)
        r = Region(r.at, r.end)
        ret_row = r.take(2, RET_DV)
        ret_stat = r.take(NT, 6)
        ret_mv = r.take(NT, 2)
        lg = r.take(2 * RET_HEADS)
        lgt = r.take(4, 2 * RET_HEADS)
        lgs = r.take(3, 2 * RET_HEADS)
        r = Region(scratch_at, phase_at)
        sT0 = r.take(2, NTOK)
        sT2 = r.take(2, SEQ)
        catR = hT

        r = Region(phase_at)
        qTd = r.take(DA_HEADS, SEQ)
        kTd = r.take(DA_HEADS, NTOK)
        v_da = r.take(NT, D)
        qk_da = r.take(2, 512)
        rope_d = r.take(2, 2, DA_HD // 2)
        rope_dt = r.take(2, 256)
        o_tok = r.take(2, D)
        oT = r.take(DA_HEADS, SEQ)
        subln = r.take(P)
        lamv = r.take(4, DA_HD)
        lamt = r.take(8)
        r = Region(spare_at, spare_at + KC * 512)
        prob = r.take(2, 2, NTOK)
        adiff = r.take(2, NTOK)
        aT = r.take(1, NTOK)
        smax = r.take(2, 2)
        ssum = r.take(2, 2)
        sinv = r.take(2, 2)
        ohs = r.take(2, DA_HEADS)

        r = Region(WORDS - 4 * NTOK - 2 * D)
        hrow_mix = r.take(2, D)
        r = Region(phase_at + 4 * 2 * D)
        hrow_moe = r.take(2, D)
        final_g = Region(phase_at).take(D)

        def spread(v):
            return v.unsqueeze(0).partition_broadcast(P) if False else v

        col = lambda v: v.rearrange("(p a) -> p a", a=1)
        row = lambda v: v.rearrange("(a n) -> a n", a=1)
        every = lambda v, n=P: row(v).broadcast_to([n, v.shape[0]])
        flat = lambda v, s: v.rearrange(s)
        start_loads = [
            (cvec[:, 0, :], A["c_ctx"].rearrange("(p c) -> p c", p=P)),
            (cvec[:, 1, :], A["c"].rearrange("a (p c) -> p (a c)", p=P)),
            (ident, K["ident"]),
            (select, K["stream_select"]),
        ]
        filter_loads = [
            (fz, K["filter_features"]),
            (fw1, A["hy_w1"][0]), (fw2, A["hy_w2"][0]), (fw3, A["hy_w3"][0]),
            (fcol[:, 0:1], col(A["hy_b1"][0])), (fcol[:, 1:2], col(A["hy_freq1"][0])),
            (fcol[:, 2:3], col(A["hy_b2"][0])), (fcol[:, 3:4], col(A["hy_freq2"][0])),
            (window, K["window"]), (dftf, K["dft_fwd"]), (dftb, K["dft_bwd"]), (dfti, K["dft_inv"]),
            (skiprow, A["hy_skip"][0:1]),
        ]
        token_loads = [(X[:, t, :], A["ctx"][0, t * P:(t + 1) * P, :]) for t in range(2)]
        token_loads += [(X[:, 2 + t, :], A["x"][0, t * P:(t + 1) * P, :]) for t in range(2)]
        conv_loads = [(cw[:, k, :].rearrange("p (i c) -> p i c", i=3), A["hy_conv_w"][0, k].rearrange("(i p c) -> p i c", p=P, c=4))
                      for k in range(3)]
        conv_loads += [(cb.rearrange("p (i c) -> p i c", i=3), A["hy_conv_b"][0].rearrange("(i p c) -> p i c", p=P, c=4))]
        ret_loads = [
            (rope_r, K["rope_ret"].rearrange("p (a b c) -> p a b c", a=2, b=2)),
            (dist, K["distance"]),
            (lgt[:, 0, :], every(A["ret_decay_logit"][0].rearrange("a h -> (a h)"))),
        ]
        da_loads = [
            (rope_d, K["rope_da"].rearrange("p (a b c) -> p a b c", a=2, b=2)),
            (subln, every(A["da_subln"][0])),
            (lamv, every(A["da_lambda"][0].rearrange("a h -> (a h)")).rearrange("p (a h) -> p a h", a=4)),
        ]

        def moe_loads(layer):
            return [
                (router_w, A["router_w"][layer].rearrange("(p c) n -> p c n", c=KC)),
                (router_b, every(A["router_b"][layer])),
                (iota1, K["iota1"]), (iota8, K["iota8"].rearrange("p (a b) -> p a b", a=TOPG)),
                (earlier, K["earlier"]), (ones, K["ones"]),
                (token_id1, K["token_id1"]), (spare_id1, K["spare_id1"]), (expert_no, K["expert_no"]),
            ]

        def ada_loads(layer, half):
            g = A["norm_mix"] if half == 0 else A["norm_ffn"]
            return [
                (modrow, every(A["b_ada"][layer, half * 3 * D:(half + 1) * 3 * D], 2)),
                (normrow, every(g[layer], 2)),
            ]

        def columns(w, at):
            return w.rearrange("(p c) n -> p c n", c=KC)[:, :, at:at + 512]

        def row_chunks(w, at):
            return w.rearrange("(c p) n -> p c n", p=P)[:, at:at + 4, :]

        dense = []
        first = {}

        def stream(name, items, last_use):
            first[name] = len(dense)
            dense.extend((src, last_use(n)) for n, src in enumerate(items))

        U_AT = 2 * RET_HEADS * RET_DK + 2 * RET_V
        ab_in, da_in, w_ada = A["ab_w_in"][0], A["da_w_in"][0], A["w_ada"]
        stream("ada_0a", [columns(w_ada[0], 512 * n) for n in range(6)], lambda n: ("mod_0a", n))
        stream("u", [columns(ab_in, U_AT + 512 * n) for n in range(3)], lambda n: ("u_proj", 4 * n + 3))
        stream("qk", [columns(ab_in, 512 * n) for n in range(2)], lambda n: ("qk_proj", NT * n + NT - 1))
        stream("vg", [columns(ab_in, 512 * (2 + n)) for n in range(4)], lambda n: ("vg_proj", NT * n + NT - 1))
        stream("out_0", [row_chunks(A["ab_w_out"][0], 4 * n) for n in range(2)]
               + [A["ab_w_out"][0, RET_V:RET_V + HW, :].rearrange("(p c) n -> p c n", c=4)], lambda n: ("out_0", 2 * NT - 1))
        stream("ada_0b", [columns(w_ada[0], 512 * (6 + n)) for n in range(6)], lambda n: ("mod_0b", n))
        stream("ada_1a", [columns(w_ada[1], 512 * n) for n in range(6)], lambda n: ("mod_1a", n))
        stream("da_qk", [columns(da_in, 512 * n) for n in range(4)], lambda n: ("da_qk", (1, 3, 7, 11)[n]))
        stream("da_v", [columns(da_in, 512 * (4 + n)) for n in range(2)], lambda n: ("da_v", NT * n + NT - 1))
        stream("out_1", [row_chunks(A["da_w_out"][0], 4 * n) for n in range(2)], lambda n: ("out_1", 3))
        stream("ada_1b", [columns(w_ada[1], 512 * (6 + n)) for n in range(6)], lambda n: ("mod_1b", n))

        def dense_slot(n, width):
            return WS[:, n % DENSE_SLOTS, :].rearrange("p (c n) -> p c n", n=width)

        dense_in = [sem(f"dense_in_{i}") for i in range(DENSE_SLOTS)]

        def wait_dense(pe, n):
            pe.wait_ge(dense_in[n % DENSE_SLOTS], 16 * (n // DENSE_SLOTS + 1))

        LT = {0: (0, NT), 1: (2, 2)}

        start_in, filter_in, token_in = sem("start_in"), sem("filter_in"), sem("token_in")
        conv_in, ret_in, da_in_sem, moe_in, ada_in = (sem(x) for x in ("conv_in", "ret_in", "da_in", "moe_in", "ada_in"))
        final_in = sem("final_in")
        dve_step = sem("dve_step")
        c_silu, filt_arg, filt_sin, filt_taps = sem("c_silu"), sem("filt_arg"), sem("filt_sin"), sem("filt_taps")
        mod_rows = sem("mod_rows")
        squares, variance, deviation, rows = sem("squares"), sem("variance"), sem("deviation"), sem("rows")
        conv_done, conv_edges, spec_done = sem("conv_done"), sem("conv_edges"), sem("spec_done")
        decay_arg, decay_exp, decay_used = sem("decay_arg"), sem("decay_exp"), sem("decay_used")
        ret_var, ret_dev, ret_rows = sem("ret_var"), sem("ret_dev"), sem("ret_rows")
        residual = sem("residual")
        lam_sums, lam_exp = sem("lam_sums"), sem("lam_exp")
        score_max, probs, probs_mixed = sem("score_max"), sem("probs"), sem("probs_mixed")
        o_var, o_dev, o_rows = sem("o_var"), sem("o_dev"), sem("o_rows")
        rows_out = [sem(f"rows_out_{i}") for i in range(2)]
        picks, id_weights, positions = sem("picks"), sem("id_weights"), sem("positions")
        hot, hot_used, flag_ready, slot_table = sem("hot"), sem("hot_used"), sem("flag_ready"), sem("slot_table")
        sh_silu, sh_act = sem("sh_silu"), sem("sh_act")
        moe_done, result_out = sem("moe_done"), sem("result_out")
        combine_in = [sem(f"combine_in_{i}") for i in range(2)]
        combine_used = sem("combine_used")
        result = sem("result")
        E = {}
        for l in range(DEPTH):
            for nme in ("xT_full", "xT_read", "gu_full", "sg_done", "act_done", "aT_full",
                        "aT_read", "y_full", "y_read_a", "y_read_d", "gidx", "empty"):
                E[nme, l] = sem(f"{nme}_{l}")
            for i in range(XG):
                E["xg_in", l, i] = sem(f"xg_in_{i}_{l}")
            for i in range(YB):
                E["stored", l, i] = sem(f"stored_{i}_{l}")
            for i in range(EXPERT_SLOTS):
                E["gu_in", l, i] = sem(f"gu_in_{i}_{l}")
                E["dn_in", l, i] = sem(f"dn_in_{i}_{l}")

        def at_least(eng, s, v):
            if not isinstance(v, int) or v > 0:
                eng.wait_ge(s, v)

        block = ctx.enter_context(nc.Block())

        ROWS_BEFORE = {"0a": 0, "0b": NT, "1a": 2 * NT, "1b": 3 * NT, "final": 3 * NT + 2}
        NORM_NO = {"0a": 0, "0b": 1, "1a": 2, "1b": 3, "final": 4}
        NORM_TILES = {"0a": (0, NT), "0b": (0, NT), "1a": (0, NT), "1b": (2, 2), "final": (2, 2)}
        ADA_NO = {"0a": 0, "0b": 1, "1a": 2, "1b": 3}
        HROW = {"0a": hrow_mix, "0b": hrow_moe, "1a": hrow_mix, "1b": hrow_moe}

        def y_block(e, b=0):
            v = y_rows.rearrange("(n p) d -> n p d", p=P)
            if isinstance(e, int):
                return v[b * NE + e]
            return v[bass.ds(e + b * NE, 1)].rearrange("a p d -> (a p) d")

        o_squares = qk_da.rearrange("p a (b c) -> p (a b) c", c=P)
        DA_USES = [(c, t) for c in range(4) for t in range(NT) if c >= 2 or t >= 2]

        M = {}
        for l in range(DEPTH):
            for nme in ("step", "in", "pe", "act", "dve", "xg", "out"):
                M[nme, l] = sem(f"more_{nme}_{l}")

        @contextmanager
        def overflow(eng, l):
            eng.wait_ge(flag_ready, l + 1)
            more = eng.value_load(flags[0:1, l:l + 1], min_val=0, max_val=1)
            with eng.If(more > 0):
                yield

        @block.sync
        def _(sp):
            def load_dense(name):
                n0 = first[name]
                n1 = min([first[x] for x in first if first[x] > n0], default=len(dense))
                for n in range(n0, n1):
                    if n >= DENSE_SLOTS:
                        ring.wait_full(sp, *dense[n - DENSE_SLOTS][1])
                    src = dense[n][0]
                    sp.dma_start(dense_slot(n, src.shape[2]), src).then_inc(dense_in[n % DENSE_SLOTS], 16)

            def expert_rows(w, l, e):
                v = w[l, e] if isinstance(e, int) else w[l, bass.ds(e, 1)].rearrange("a d n -> (a d) n")
                return v.rearrange("(p c) n -> p (c n)", p=P)

            def load_expert(l, u, gate, up, down):
                dst = WS[:, u, :].rearrange("p (a n) -> p a n", a=2)
                sp.dma_start(dst[:, 0, :], gate).then_inc(E["gu_in", l, u], 16)
                sp.dma_start(dst[:, 1, :], up).then_inc(E["gu_in", l, u], 16)
                sp.dma_start(DN[:, u, :], down).then_inc(E["dn_in", l, u], 16)

            def routed(l, item, u):
                e = item - 1
                load_expert(l, u, expert_rows(A["exp_w_gate"], l, e), expert_rows(A["exp_w_up"], l, e),
                            expert_rows(A["exp_w_down"], l, e))

            def load_experts(l):
                whole = lambda w: w[l].rearrange("(p c) n -> p (c n)", p=P)
                load_expert(l, 0, whole(A["sh_w_gate"]), whole(A["sh_w_up"]), whole(A["sh_w_down"]))
                for item in range(1, EXPERT_SLOTS):
                    routed(l, item, item)
                ring.wait_full(sp, f"sh_y_{l}", 2 * LT[l][1] - 1)
                for u in range(EXPERT_SLOTS):
                    if u:
                        sp.wait_ge(E["y_full", l], u)
                    routed(l, EXPERT_SLOTS + u, u)
                with sp.Fori(2, NE // EXPERT_SLOTS) as i:
                    for u in range(EXPERT_SLOTS):
                        sp.wait_ge(E["y_full", l], i * EXPERT_SLOTS + (u - EXPERT_SLOTS))
                        routed(l, i * EXPERT_SLOTS + u, u)
                sp.wait_ge(E["y_full", l], NE - EXPERT_SLOTS)
                routed(l, NE, 0)

            def overflow_sp(l):
                def load_more(e):
                    dst = WS[:, 0, :].rearrange("p (a n) -> p a n", a=2)
                    sp.dma_start(dst[:, 0, :], expert_rows(A["exp_w_gate"], l, e)).then_inc(M["in", l], 16)
                    sp.dma_start(dst[:, 1, :], expert_rows(A["exp_w_up"], l, e)).then_inc(M["in", l], 16)
                    sp.dma_start(DN[:, 0, :], expert_rows(A["exp_w_down"], l, e)).then_inc(M["in", l], 16)

                with overflow(sp, l):
                    load_more(0)
                    with sp.Fori(1, NE) as e:
                        sp.wait_ge(M["pe", l], e * (5 * (LT[l][1] - 1)))
                        load_more(e)

            for name in ("ada_0a", "u", "qk", "vg", "out_0", "ada_0b"):
                load_dense(name)
            ring.wait_full(sp, "mod_0b", 5)
            load_experts(0)
            sp.wait_ge(E["y_full", 0], NE)
            overflow_sp(0)
            for name in ("ada_1a", "da_qk", "da_v", "out_1", "ada_1b"):
                load_dense(name)
            ring.wait_full(sp, "mod_1b", 5)
            load_experts(1)
            sp.wait_ge(E["y_full", 1], NE)
            overflow_sp(1)
            for t in range(2):
                sp.wait_ge(result, t + 1)
                sp.dma_start(out[0, t * P:(t + 1) * P, :], hrow_mix[:, t, :]).then_inc(result_out, 16)
            sp.wait_ge(result_out, 32)

        @block.tensor
        def _(pe):
            def products(dst, pairs, signal):
                last = len(pairs) - 1
                for i, (l, r) in enumerate(pairs):
                    mm = nc.tensor.matmul(dst, l, r, start=(i == 0), stop=(i == last))
                if signal is not None:
                    mm.then_inc(signal, 1)

            def turns(dst, srcs, signal):
                for i, v in enumerate(srcs):
                    tr = nc.tensor.transpose(dst[:, i * P:(i + 1) * P], v, ident)
                tr.then_inc(signal, 1)

            def use(stage, k):
                ring.claim(pe, stage, k)
                return bank(stage, k), ring.full(stage, k)

            def ada(tag, streams):
                n0 = first[f"ada_{tag}"]
                for n in range(6):
                    wait_dense(pe, n0 + n)
                    w = dense_slot(n0 + n, 512)
                    b, full = use(f"mod_{tag}", n)
                    products(b[0:2, :], [(csilu[:, :, c], w[:, c, :]) for c in range(KC)], full)
                pe.wait_ge(mod_rows, ADA_NO[tag] + 1)
                for j in range(6):
                    for i, s in enumerate(streams):
                        b, full = use(f"bcast_{tag}", j * len(streams) + i)
                        products(b, [(select[:, s, :], modrow[:, j * 512:(j + 1) * 512])], full)

            def norm(tag):
                for j in range(NORM_TILES[tag][1]):
                    pe.wait_ge(rows, ROWS_BEFORE[tag] + j + 1)
                    v = HROW[tag][:, j % 2, :].rearrange("p (c q) -> p c q", c=KC)
                    for half in range(2):
                        b, full = use(f"norm_{tag}", 2 * j + half)
                        turns(b, [v[:, 4 * half + i, :] for i in range(4)], full)

            def all_norm_read(tag):
                for k in range(2 * NORM_TILES[tag][1]):
                    ring.wait_read(pe, f"norm_{tag}", k)

            def tile_cols(t):
                return slice(t * P, (t + 1) * P)

            def project(stage, k, n, t):
                w = dense_slot(n, 512)
                b, full = use(stage, k)
                products(b, [(hT[:, c, tile_cols(t)], w[:, c, :]) for c in range(KC)], full)

            def hyena_filters():
                pe.wait_ge(filter_in, 16 * len(filter_loads))
                b, full = use("filter_a", 0)
                products(b[0:HY_FFN, 0:SEQ], [(fw1, fz)], full)
                pe.wait_ge(filt_sin, 1)
                b, full = use("filter_b", 0)
                products(b[0:HY_FFN, 0:SEQ], [(fw2, fh[:, 0, :])], full)
                pe.wait_ge(filt_sin, 2)
                for t in range(2):
                    for n in range(4):
                        b, full = use("filter_c", 4 * t + n)
                        products(b, [(fh[:, 1, tile_cols(t)], fw3[:, n * HW:(n + 1) * HW])], full)
                pe.wait_ge(filt_taps, 1)
                for o in range(2):
                    for m in range(5):
                        g = (0, 1, 4, 3, 5)[m]
                        b, full = use("filter_dft", 5 * o + m)
                        products(b, [(tab[:, t, g * P:(g + 1) * P], filt[:, t, 2 * o + d, :])
                                     for t in range(2) for d, tab in enumerate((dftf, dftb))], full)

            def u_turn(m):
                pe.wait_ge(conv_done, m + 1)
                b, full = use("u_turn", m)
                turns(b, [uconv[:, m % 2, tile_cols(t)] for t in range(NT)], full)

            def hyena():
                for m in range(12):
                    n = first["u"] + m // 4
                    wait_dense(pe, n)
                    w = dense_slot(n, 512)
                    b, full = use("u_proj", m)
                    w = w.rearrange("p c (q m) -> p c q m", m=4)[:, :, :, m % 4]
                    products(b, [(w[:, c, :], hT[:, c, :]) for c in range(KC)], full)
                    if 1 <= m <= 8:
                        u_turn(m - 1)
                for k in range(8):
                    ring.wait_read(pe, "u_turn", k)
                for o in range(2):
                    for s in range(2):
                        if o:
                            for m in range(2):
                                ring.wait_read(pe, "idft_0", 2 * s + m)
                        for m in range(4):
                            b, full = use(f"dft_{o}", 4 * s + m)
                            products(b, [(dftf[:, t, m * P:(m + 1) * P], vtok[:, 2 * s + t, :])
                                         for t in range(2)], full)
                        pe.wait_ge(spec_done, 2 * o + s + 1)
                        for m in range((2, 4)[o]):
                            b, full = use(f"idft_{o}", (2, 4)[o] * s + m)
                            if o == 0:
                                products(b, [(dfti[:, f, m * P:(m + 1) * P], specY[:, f, :])
                                             for f in range(4)], full)
                            else:
                                by_chunk = specY.rearrange("p f (q m) -> p f q m", m=4)[:, :, :, m]
                                products(b[:, 0:SEQ], [(by_chunk[:, f, :], dfti[:, f, :])
                                                       for f in range(4)], full)

            def qk_turn(stage, source, n):
                ring.wait_read(pe, "qk_proj" if stage == "qk_turn" else "da_qk", n)
                b, full = use(stage, n)
                turns(b, [source[:, n % 2, i * P:(i + 1) * P] for i in range(4)], full)

            def retention():
                for n in range(2 * NT):
                    wait_dense(pe, first["qk"] + n // NT)
                    project("qk_proj", n, first["qk"] + n // NT, n % NT)
                    if n:
                        qk_turn("qk_turn", qk_tok, n - 1)
                qk_turn("qk_turn", qk_tok, 2 * NT - 1)
                for n in range(4 * NT):
                    wait_dense(pe, first["vg"] + n // NT)
                    project("vg_proj", n, first["vg"] + n // NT, n % NT)
                for n in range(2 * NT):
                    ring.wait_read(pe, "qk_turn", n)
                for n in range(4 * NT):
                    ring.wait_read(pe, "vg_proj", n)
                for h in range(RET_HEADS):
                    for kt in range(4):
                        b, full = use("ret_s", 4 * h + kt)
                        if kt < 2:
                            products(b, [(kT[:, h, tile_cols(kt)], qT[:, h, :])], full)
                        else:
                            products(b[:, 0:SEQ], [(kT[:, h, tile_cols(kt)], qT[:, h, CTX:])], full)
                    for kt in range(4):
                        ring.wait_read(pe, "ret_s", 4 * h + kt)
                    for t in range(NT):
                        b, full = use("ret_o", NT * h + t)
                        pairs = [(sT0[:, kt, tile_cols(t)], v_tok[:, kt, h * RET_DV:(h + 1) * RET_DV])
                                 for kt in range(2)]
                        if t >= 2:
                            pairs += [(sT2[:, kt, tile_cols(t - 2)], v_tok[:, 2 + kt, h * RET_DV:(h + 1) * RET_DV])
                                      for kt in range(2)]
                        products(b[:, 0:RET_DV], pairs, full)
                    for t in range(NT):
                        pe.wait_ge(ret_rows, NT * h + t + 1)
                        b, full = use("ret_turn", NT * h + t)
                        turns(b, [ret_row[:, t % 2, i * P:(i + 1) * P] for i in range(2)], full)

            def out_projection(layer):
                stage, n0 = f"out_{layer}", first[f"out_{layer}"]
                chunks = 12 if layer == 0 else KC
                for n in range(chunks // 4):
                    wait_dense(pe, n0 + n)
                for t in range(NT if layer == 0 else 2):
                    for half in range(2):
                        b, full = use(stage, 2 * t + half)
                        pairs = []
                        for c in range(chunks):
                            if layer == 0:
                                left = catR[:, c, tile_cols(t)] if c < 8 else catH[:, c - 8, tile_cols(t)]
                            else:
                                left = oT[:, c, tile_cols(t)]
                            w = dense_slot(n0 + c // 4, D)[:, c % 4, half * 512:(half + 1) * 512]
                            pairs.append((left, w))
                        products(b, pairs, full)

            def attention():
                for n, (c, t) in enumerate(DA_USES):
                    wait_dense(pe, first["da_qk"] + c)
                    project("da_qk", n, first["da_qk"] + c, t)
                    if n:
                        qk_turn("da_turn", qk_da, n - 1)
                qk_turn("da_turn", qk_da, len(DA_USES) - 1)
                for n in range(2 * NT):
                    wait_dense(pe, first["da_v"] + n // NT)
                    project("da_v", n, first["da_v"] + n // NT, n % NT)
                for n in range(len(DA_USES)):
                    ring.wait_read(pe, "da_turn", n)
                for n in range(2 * NT):
                    ring.wait_read(pe, "da_v", n)
                for n in range(2 * DA_HEADS + 1):
                    if n < 2 * DA_HEADS:
                        qt, h = n // DA_HEADS, n % DA_HEADS
                        for c in range(2):
                            b, full = use("da_s", 2 * n + c)
                            half = slice(c * DA_HD, (c + 1) * DA_HD)
                            products(b, [(qTd[half, h, tile_cols(qt)], kTd[half, h, :])], full)
                    if n:
                        m = n - 1
                        pe.wait_ge(probs_mixed, m + 1)
                        b, full = use("da_at", m)
                        turns(b, [adiff[:, m % 2, tile_cols(kt)] for kt in range(NT)], full)
                        ring.wait_read(pe, "da_at", m)
                        b, full = use("da_o", m)
                        h = m % DA_HEADS
                        products(b[:, 0:P], [(aT[:, 0, tile_cols(kt)], v_da[:, kt, h * P:(h + 1) * P])
                                             for kt in range(NT)], full)
                for qt in range(2):
                    pe.wait_ge(o_rows, qt + 1)
                    for half in range(2):
                        b, full = use("da_ot", 2 * qt + half)
                        turns(b, [o_tok[:, qt, (4 * half + i) * P:(4 * half + i + 1) * P] for i in range(4)], full)
                for k in range(4):
                    ring.wait_read(pe, "da_ot", k)

            def gate_up(dst, left, u, signal):
                w = WS[:, u, :].rearrange("p (a c n) -> p a c n", a=2, c=KC)
                products(dst, [(left(c), w[:, :, c, :]) for c in range(KC)], signal)

            def turn_act(dst, i, signal):
                turns(dst, [act[:, i, c * P:(c + 1) * P] for c in range(2)], signal)

            def down(dst, half, i, u, signal):
                w = DN[:, u, :].rearrange("p (c n) -> p c n", c=2)
                products(dst, [(actT[:, i, c * P:(c + 1) * P], w[:, c, half * 512:(half + 1) * 512])
                               for c in range(2)], signal)

            def route(l):
                t0, tiles = LT[l]
                pe.wait_ge(moe_in, 16 * len(moe_loads(0)) * (l + 1))
                for k in range(tiles):
                    b, full = use(f"route_{l}", k)
                    products(b[:, 0:NE], [(hT[:, c, tile_cols(t0 + k)], router_w[:, c, :]) for c in range(KC)], full)
                shared(l, [("gu", 0)])
                pe.wait_ge(picks, (0, NT)[l] + tiles)
                for k in range(tiles + 1):
                    b, full = use(f"pos_{l}", k)
                    pairs = [(ones, picked[:, t0 + t, :]) for t in range(k)]
                    if k < tiles:
                        pairs.append((earlier, picked[:, t0 + k, :]))
                    products(b[:, 0:NE], pairs, full)

            def shared(l, steps):
                t0 = LT[l][0]
                for what, t in steps:
                    if what == "gu":
                        if t == 0:
                            pe.wait_ge(E["gu_in", l, 0], 32)
                        b, full = use(f"sh_gu_{l}", t)
                        gate_up(b, lambda c: hT[:, c, tile_cols(t0 + t)], 0, full)
                        continue
                    if t == 0:
                        pe.wait_ge(E["dn_in", l, 0], 16)
                    ring.wait_read(pe, f"sh_gu_{l}", t)
                    b, full = use(f"sh_t_{l}", t)
                    turn_act(b, t % 2, full)
                    ring.wait_read(pe, f"sh_t_{l}", t)
                    for half in range(2):
                        b, full = use(f"sh_y_{l}", 2 * t + half)
                        down(b, half, t % 2, 0, full)

            def slot_table_of(l, e, u, dst, signal):
                t0, tiles = LT[l]
                pe.wait_ge(hot, e + (1 + NE * l))
                for t in range(tiles):
                    one = slice(e, e + 1) if isinstance(e, int) else bass.ds(e, 1)
                    mm = nc.tensor.matmul(dst, one_hot[:, u, t, :],
                                          idw[:, t0 + t, one, :].rearrange("p a b -> p (a b)"),
                                          start=(t == 0), stop=(t == tiles - 1))
                mm.then_inc(signal, 1)

            def first_tables(l):
                t0, tiles = LT[l]
                pe.wait_ge(id_weights, (0, NT)[l] + tiles)
                for e in range(TABLES_FIRST):
                    b, full = use(f"table_{l}", e)
                    slot_table_of(l, e, e % 2, b[:, 0:2], full)

            def experts(l):
                def turn_tokens(e, u, gathered):
                    pe.wait_ge(E["xg_in", l, u], gathered * 16)
                    at_least(pe, E["xT_read", l], e)
                    for c in range(KC):
                        tr = nc.tensor.transpose(ps[:, c // 4, (c % 4) * P:(c % 4 + 1) * P],
                                                 xg[:, u, c * P:(c + 1) * P], ident)
                    tr.then_inc(E["xT_full", l], 1)

                def down_of(e, i, u, item_count):
                    pe.wait_ge(E["aT_read", l], e + 1)
                    at_least(pe, E["y_read_a", l], e)
                    at_least(pe, E["y_read_d", l], e)
                    pe.wait_ge(E["dn_in", l, u], item_count * 16)
                    for half in range(2):
                        down(ps[:, 5 + half, :], half, i, u, E["y_full", l] if half else None)

                def step(e, r, i4, has_next=True):
                    u, i = r % 4, (r - 1) % 2
                    count = i4 + 1 + (1 if r == 4 else 0)
                    pe.wait_ge(E["xT_read", l], e + 1)
                    pe.wait_ge(E["gu_in", l, u], count * 32)
                    at_least(pe, E["act_done", l], e - 1)
                    gate_up(ps[:, 2 + i, :], lambda c: xgT[:, i, c * P:(c + 1) * P], u, E["gu_full", l])
                    if has_next:
                        turn_tokens(e + 1, r % XG, i4 + (1 + r // XG))
                    if not isinstance(e, int) or e < NE - TABLES_FIRST:
                        x = e + TABLES_FIRST
                        pe.wait_ge(slot_table, x + NE * l)
                        slot_table_of(l, x, (r - 1 + TABLES_FIRST) % 2, ps[:, 7, 0:2], hot_used)
                    if not isinstance(e, int) or e > 0:
                        down_of(e - 1, 1 - i, (r - 1) % 4, i4 + 1)
                    pe.wait_ge(E["act_done", l], e + 1)
                    turn_act(ps[:, 4, :], i, E["aT_full", l])

                turn_tokens(0, 0, 1)
                for r in range(1, 5):
                    step(r - 1, r, 0)
                with pe.Fori(1, NE // 4 - 2) as i4:
                    for r in range(1, 5):
                        step(i4 * 4 + (r - 1), r, i4)
                for i4 in range(NE // 4 - 2, NE // 4):
                    for r in range(1, 5):
                        step(i4 * 4 + r - 1, r, i4, has_next=(i4 * 4 + r < NE))
                down_of(NE - 1, 1, 0, NE // 4 + 1)
                pe.wait_ge(E["y_read_a", l], NE)
                pe.wait_ge(E["y_read_d", l], NE)

            def overflow_pe(l):
                t0, tiles = LT[l]
                nb = tiles - 1
                with overflow(pe, l), pe.Fori(0, NE) as e:
                    for b in range(nb):
                        n = e * nb + b
                        pe.wait_ge(M["dve", l], n * 4 + 1)
                        for t in range(tiles):
                            mm = nc.tensor.matmul(ps[:, 7, 0:2], one_hot[:, 0, t, :],
                                                  idw[:, t0 + t, bass.ds(e, 1), :].rearrange("p a b -> p (a b)"),
                                                  start=(t == 0), stop=(t == tiles - 1))
                        mm.then_inc(M["pe", l], 1)
                        pe.wait_ge(M["xg", l], n * 16 + 16)
                        for c in range(KC):
                            tr = nc.tensor.transpose(ps[:, c // 4, (c % 4) * P:(c % 4 + 1) * P],
                                                     xg[:, 0, c * P:(c + 1) * P], ident)
                        tr.then_inc(M["pe", l], 1)
                        pe.wait_ge(M["act", l], n * 4 + 1)
                        pe.wait_ge(M["in", l], e * 48 + 48)
                        gate_up(ps[:, 2, :], lambda c: xgT[:, 0, c * P:(c + 1) * P], 0, M["pe", l])
                        pe.wait_ge(M["dve", l], n * 4 + 3)
                        turn_act(ps[:, 4, :], 0, M["pe", l])
                        pe.wait_ge(M["act", l], n * 4 + 3)
                        for half in range(2):
                            down(ps[:, 5 + half, :], half, 0, 0, M["pe", l] if half else None)
                with overflow(pe, l):
                    pe.wait_ge(M["act", l], NE * nb * 4)
                    pe.wait_ge(M["dve", l], NE * nb * 4)

            def layer_moe(l):
                route(l)
                shared(l, [("gu", 1)])
                first_tables(l)
                shared(l, [("y", 0), ("y", 1)] + [(w, t) for t in range(2, LT[l][1]) for w in ("gu", "y")])
                ring.fence(pe)
                experts(l)
                overflow_pe(l)

            pe.wait_ge(start_in, 16 * len(start_loads))
            hyena_filters()
            pe.wait_ge(c_silu, 1)
            ada("0a", (0, 1))
            norm("0a")
            all_norm_read("0a")
            hyena()
            retention()
            for n in range(4 * RET_HEADS):
                ring.wait_read(pe, "ret_turn", n)
            out_projection(0)
            ada("0b", (0, 1))
            norm("0b")
            all_norm_read("0b")
            layer_moe(0)
            ada("1a", (0, 1))
            norm("1a")
            all_norm_read("1a")
            attention()
            out_projection(1)
            ada("1b", (1,))
            norm("1b")
            all_norm_read("1b")
            layer_moe(1)
            assert ring.claimed == len(ring.order)

        @block.scalar
        def _(act_e):
            A_ = nc.scalar.activation

            def load(items, s):
                for dst, src in items:
                    act_e.dma_start(dst, src).then_inc(s, 16)

            def norm_scale(tag):
                t0, tiles = NORM_TILES[tag]
                for j in range(tiles):
                    if j >= 2:
                        act_e.wait_ge(squares, ROWS_BEFORE[tag] + j - 1)
                    A_(HROW.get(tag, hrow_mix)[:, j % 2, :], X[:, t0 + j, :], ACT.Square,
                       accum_out=ssq[:, t0 + j:t0 + j + 1]).then_inc(squares, 1)
                act_e.wait_ge(variance, NORM_NO[tag] + 1)
                A_(rstd[:, t0:t0 + tiles], rstd[:, t0:t0 + tiles], ACT.Sqrt).then_inc(deviation, 1)

            def norm_turns(tag):
                t0, tiles = NORM_TILES[tag]
                for j in range(tiles):
                    t = t0 + j
                    for half in range(2):
                        k = 2 * j + half
                        ring.wait_full(act_e, f"norm_{tag}", k)
                        A_(hT[:, 4 * half:4 * half + 4, t * P:(t + 1) * P],
                           bank(f"norm_{tag}", k).rearrange("p (c q) -> p c q", c=4),
                           ACT.Copy).then_inc(ring.read(f"norm_{tag}", k), 1)

            def spread_mods(tag, streams):
                for j in range(6):
                    for i, s in enumerate(streams):
                        k = j * len(streams) + i
                        ring.wait_full(act_e, f"bcast_{tag}", k)
                        A_(bc[:, s, j // 2, (j % 2) * 512:(j % 2 + 1) * 512], bank(f"bcast_{tag}", k),
                           ACT.Copy).then_inc(ring.read(f"bcast_{tag}", k), 1)

            def evacuate(stage, k, dst, width=512, func=ACT.Copy, shape=None):
                ring.wait_full(act_e, stage, k)
                src = bank(stage, k)[:, 0:width]
                if shape:
                    src = src.rearrange("p (a b) -> p a b", a=shape)
                A_(dst, src, func).then_inc(ring.read(stage, k), 1)

            load(start_loads, start_in)
            load(ada_loads(0, 0), ada_in)
            load(filter_loads, filter_in)
            load(token_loads, token_in)
            act_e.wait_ge(start_in, 16 * len(start_loads))
            A_(csilu, cvec, ACT.Silu).then_inc(c_silu, 1)
            for n in range(2):
                act_e.wait_ge(filt_arg, n + 1)
                A_(fh[:, n, :], farg, ACT.Sin).then_inc(filt_sin, 1)
            for k in range(10):
                evacuate("filter_dft", k, H[:, k // 5, k % 5, :])
            load(conv_loads, conv_in)
            act_e.wait_ge(token_in, 16 * len(token_loads))
            norm_scale("0a")
            spread_mods("0a", (0, 1))
            norm_turns("0a")

            act_e.wait_ge(conv_edges, 1)
            for m in range(12):
                if m >= 2:
                    act_e.wait_ge(conv_done, m - 1)
                evacuate("u_proj", m, upad[:, m % 2, :, 1:SEQ + 1], shape=2)
                if 1 <= m <= 8:
                    n = m - 1
                    dst = (vtok, x1tok)[n // 4].rearrange("p t (q m) -> p t q m", m=4)[:, :, :, n % 4]
                    evacuate("u_turn", n, dst, shape=NT)
            for k in range(8):
                ring.wait_read(act_e, "idft_1", k)
            load(ret_loads, ret_in)
            for c in range(2):
                for t in range(NT):
                    n = c * NT + t
                    evacuate("qk_turn", n, (qT, kT)[c][:, :, t * P:(t + 1) * P], shape=RET_HEADS)
            for n in range(4 * NT):
                i, t = n // NT, n % NT
                dst = (v_tok, g_tok)[i // 2][:, t, (i % 2) * 512:(i % 2 + 1) * 512]
                evacuate("vg_proj", n, dst, func=ACT.Copy if i < 2 else ACT.Silu)
            act_e.wait_ge(decay_arg, 1)
            A_(lgt[:, 1, :], lgt[:, 1, :], ACT.Exp).then_inc(decay_exp, 1)
            act_e.wait_ge(decay_arg, 2)
            for h in range(RET_HEADS):
                f, b = slice(h, h + 1), slice(RET_HEADS + h, RET_HEADS + h + 1)
                at_least(act_e, decay_used, 2 * h)
                flat_ = lambda v: v.rearrange("p a n -> p (a n)")
                A_(decay_e[:, 0, :], flat_(dist_f), ACT.Exp, scale=lg[:, f])
                A_(decay_e[:, 1, :], flat_(dist_b), ACT.Exp, scale=lg[:, b]).then_inc(decay_exp, 1)
                act_e.wait_ge(decay_used, 2 * h + 1)
                A_(decay_e[:, 0, :], flat_(dist), ACT.Exp, scale=lg[:, f], bias=lgs[:, 0, f])
                A_(decay_e[:, 1, :], flat_(dist), ACT.Exp, scale=lgs[:, 2, b], bias=lgs[:, 0, b]).then_inc(decay_exp, 1)
                for t in range(NT):
                    n = NT * h + t
                    act_e.wait_ge(ret_var, n + 1)
                    A_(ret_mv[:, t, 1:2], ret_mv[:, t, 1:2], ACT.Sqrt).then_inc(ret_dev, 1)
                for t in range(NT):
                    evacuate("ret_turn", NT * h + t, catR[:, 2 * h:2 * h + 2, t * P:(t + 1) * P], width=2 * P, shape=2)
            load(ada_loads(0, 1), ada_in)
            act_e.wait_ge(residual, NT)
            norm_scale("0b")
            spread_mods("0b", (0, 1))

            def overflow_act(l):
                nb = LT[l][1] - 1
                with overflow(act_e, l):
                  for i in range(YB):
                    act_e.wait_ge(E["stored", l, i], NE // YB * 16)
                  with act_e.Fori(0, NE) as e:
                    for b in range(nb):
                        n = e * nb + b
                        act_e.wait_ge(M["pe", l], n * 5 + 2)
                        A_(xgT[:, 0, 0:512], ps[:, 0, :], ACT.Copy)
                        A_(xgT[:, 0, 512:], ps[:, 1, :], ACT.Copy).then_inc(M["act", l], 1)
                        act_e.wait_ge(M["pe", l], n * 5 + 3)
                        A_(gsil[:, 0, :], ps[:, 2, 0:ED], ACT.Silu).then_inc(M["act", l], 1)
                        act_e.wait_ge(M["pe", l], n * 5 + 4)
                        A_(actT[:, 0, :], ps[:, 4, 0:2 * P], ACT.Copy).then_inc(M["act", l], 1)
                        act_e.wait_ge(M["pe", l], n * 5 + 5)
                        A_(yb[:, 0, 0:512], ps[:, 5, :], ACT.Copy).then_inc(M["act", l], 1)
                        act_e.wait_ge(M["act", l], n * 4 + 4)
                        act_e.wait_ge(M["dve", l], n * 4 + 4)
                        act_e.dma_start(y_block(e, b + 1), yb[:, 0, :]).then_inc(M["out", l], 16)
                        act_e.wait_ge(M["out", l], n * 16 + 16)

            def experts_phase(l):
                t0, tiles = LT[l]
                load(moe_loads(l), moe_in)
                norm_turns(f"{l}b")
                for k in range(tiles):
                    evacuate(f"route_{l}", k, scores[:, t0 + k, :], width=NE, func=ACT.Sigmoid)

                def shared_silu(t):
                    ring.wait_full(act_e, f"sh_gu_{l}", t)
                    if t >= 2:
                        ring.wait_read(act_e, f"sh_gu_{l}", t - 2)
                    A_(gsil[:, t % 2, :], bank(f"sh_gu_{l}", t)[:, 0:ED], ACT.Silu).then_inc(sh_silu, 1)

                shared_silu(0)
                shared_silu(1)
                for t in range(tiles):
                    if t >= 2:
                        shared_silu(t)
                    evacuate(f"sh_t_{l}", t, actT[:, t % 2, :], width=2 * P)

                def tokens_in(e, i):
                    act_e.wait_ge(E["xT_full", l], e + 1)
                    for half in range(2):
                        a = A_(xgT[:, i, half * 512:(half + 1) * 512], ps[:, half, :], ACT.Copy)
                    a.then_inc(E["xT_read", l], 1)

                def rows_out_half(e, u, stored):
                    act_e.wait_ge(E["y_full", l], e + 1)
                    at_least(act_e, E["stored", l, u], stored * 16)
                    A_(yb[:, u, 0:512], ps[:, 5, :], ACT.Copy).then_inc(E["y_read_a", l], 1)

                def store(e, u):
                    act_e.wait_ge(E["y_read_a", l], e + 1)
                    act_e.wait_ge(E["y_read_d", l], e + 1)
                    act_e.dma_start(y_block(e), yb[:, u, :]).then_inc(E["stored", l, u], 16)

                def step(e, i4, r, has_next=True):
                    i = r % 2
                    act_e.wait_ge(E["gu_full", l], e + 1)
                    at_least(act_e, E["act_done", l], e - 1)
                    A_(gsil[:, i, :], ps[:, 2 + i, 0:ED], ACT.Silu).then_inc(E["sg_done", l], 1)
                    if has_next:
                        tokens_in(e + 1, 1 - i)
                    behind = not isinstance(e, int) or e > 0
                    if behind:
                        rows_out_half(e - 1, (r - 1) % YB, i4)
                    act_e.wait_ge(E["aT_full", l], e + 1)
                    A_(actT[:, i, :], ps[:, 4, 0:2 * P], ACT.Copy).then_inc(E["aT_read", l], 1)
                    if behind:
                        store(e - 1, (r - 1) % YB)

                tokens_in(0, 0)
                step(0, -1, 4)
                for r in range(1, 5):
                    step(r, 0, r)
                with act_e.Fori(1, NE // 4 - 1) as i4:
                    for r in range(1, 5):
                        step(i4 * 4 + r, i4, r)
                for r in range(1, 4):
                    step(NE - 4 + r, NE // 4 - 1, r, has_next=(r < 3))
                rows_out_half(NE - 1, 3, NE // 4 - 1)
                store(NE - 1, 3)
                overflow_act(l)

            experts_phase(0)
            act_e.wait_ge(moe_done, 1)
            load(ada_loads(1, 0), ada_in)
            norm_scale("1a")
            spread_mods("1a", (0, 1))
            load(da_loads, da_in_sem)
            load(ada_loads(1, 1), ada_in)
            norm_turns("1a")
            for n, (c, t) in enumerate(DA_USES):
                hs = slice((c % 2) * 4, (c % 2) * 4 + 4)
                dst = qTd[:, hs, (t - 2) * P:(t - 1) * P] if c < 2 else kTd[:, hs, t * P:(t + 1) * P]
                evacuate("da_turn", n, dst, shape=4)
            for n in range(2 * NT):
                i, t = n // NT, n % NT
                evacuate("da_v", n, v_da[:, t, i * 512:(i + 1) * 512])
            act_e.wait_ge(lam_sums, 1)
            A_(lamt[:, 0:2], lamt[:, 0:2], ACT.Exp).then_inc(lam_exp, 1)
            for n in range(2 * DA_HEADS + 1):
                if n < 2 * DA_HEADS:
                    act_e.wait_ge(score_max, n + 1)
                    if n >= 2:
                        act_e.wait_ge(probs_mixed, n - 1)
                    for c in range(2):
                        ring.wait_full(act_e, "da_s", 2 * n + c)
                        A_(prob[:, n % 2, c, :], bank("da_s", 2 * n + c), ACT.Exp, scale=DA_HD ** -0.5,
                           bias=smax[:, n % 2, c:c + 1], accum_out=ssum[:, n % 2, c:c + 1])\
                            .then_inc(ring.read("da_s", 2 * n + c), 1)
                if n:
                    m = n - 1
                    if m:
                        ring.wait_full(act_e, "da_o", m - 1)
                    evacuate("da_at", m, aT[:, 0, :])
                    evacuate("da_o", m, o_tok[:, m // DA_HEADS, (m % DA_HEADS) * P:(m % DA_HEADS + 1) * P], width=P)
            for qt in range(2):
                act_e.wait_ge(o_var, qt + 1)
                A_(ohs[:, qt, :], ohs[:, qt, :], ACT.Sqrt).then_inc(o_dev, 1)
            for k in range(4):
                qt, half = k // 2, k % 2
                evacuate("da_ot", k, oT[:, 4 * half:4 * half + 4, qt * P:(qt + 1) * P], shape=4)
            act_e.wait_ge(residual, 2 * NT - 1 + 2)
            norm_scale("1b")
            spread_mods("1b", (1,))
            experts_phase(1)
            act_e.wait_ge(moe_done, 2)
            act_e.dma_start(final_g, every(A["norm_final"])).then_inc(final_in, 16)
            norm_scale("final")

        @block.vector
        def _(dve):
            V = nc.vector
            link = Chain(dve, dve_step)

            def filter_arg(stage, i):
                ring.wait_full(dve, stage, 0)
                V.tensor_scalar(farg, bank(stage, 0)[0:HY_FFN, 0:SEQ], fcol[:, 2 * i:2 * i + 1],
                                fcol[:, 2 * i + 1:2 * i + 2], ALU.add, ALU.mult).then_inc(ring.read(stage, 0), 1)
                ring.wait_read(dve, stage, 0)
                link(V.tensor_scalar(fturn, farg, 1.0 / TWO_PI, MAGIC, ALU.mult, ALU.add))
                link(V.tensor_scalar(fturn, fturn, MAGIC, None, ALU.subtract))
                for part in (PI_1, PI_2, PI_3):
                    link(V.scalar_tensor_tensor(out=farg, in0=fturn, scalar=-part, in1=farg, op0=ALU.mult, op1=ALU.add))
                V.tensor_scalar(farg, farg, PI_SAFE, -PI_SAFE, ALU.min, ALU.max).then_inc(filt_arg, 1)

            def mods(tag):
                dve.wait_ge(ada_in, 32 * (ADA_NO[tag] + 1))
                for n in range(6):
                    stage = f"mod_{tag}"
                    ring.wait_full(dve, stage, n)
                    part = modrow[:, n * 512:(n + 1) * 512]
                    V.tensor_tensor(part, bank(stage, n)[0:2, :], part, ALU.add).then_inc(ring.read(stage, n), 1)
                for n in range(6):
                    ring.wait_read(dve, f"mod_{tag}", n)
                sc = modrow[:, D:2 * D]
                V.scalar_tensor_tensor(out=sc, in0=sc, scalar=1.0, in1=normrow, op0=ALU.add,
                                       op1=ALU.mult).then_inc(mod_rows, 1)

            def norm_inverse(tag):
                t0, tiles = NORM_TILES[tag]
                dve.wait_ge(squares, ROWS_BEFORE[tag] + tiles)
                V.tensor_scalar(rstd[:, t0:t0 + tiles], ssq[:, t0:t0 + tiles], 1.0 / D, EPS, ALU.mult,
                                ALU.add).then_inc(variance, 1)
                dve.wait_ge(deviation, NORM_NO[tag] + 1)
                link(V.reciprocal(rstd[:, t0:t0 + tiles], rstd[:, t0:t0 + tiles]))

            def norm_rows(tag, streams):
                t0, tiles = NORM_TILES[tag]
                norm_inverse(tag)
                for j in range(4 * len(streams)):
                    ring.wait_read(dve, f"bcast_{tag}", j)
                for j in range(tiles):
                    t = t0 + j
                    h = HROW[tag][:, j % 2, :]
                    if j >= 2:
                        ring.wait_full(dve, f"norm_{tag}", 2 * (j - 2) + 1)
                        if tag[1] == "b":
                            dve.wait_ge(rows_out[j % 2], 16)
                    h = h.rearrange("p (c q) -> p q c", c=KC)
                    chunks = lambda v: v.rearrange("p (q c) -> p q c", c=KC)
                    link(V.scalar_tensor_tensor(out=h, in0=chunks(X[:, t, :]), scalar=rstd[:, t:t + 1],
                                                in1=chunks(bc[:, t // 2, 1, :]), op0=ALU.mult, op1=ALU.mult))
                    V.tensor_tensor(h, h, chunks(bc[:, t // 2, 0, :]), ALU.add).then_inc(rows, 1)

            def rotate(dst, src, tab, tmp, t, groups, half, signal):
                v = src.rearrange("p (g a d) -> p g a d", g=groups, a=2)
                w = dst.rearrange("p (g a d) -> p g a d", g=groups, a=2)
                tmp = tmp.rearrange("p (g d) -> p g d", g=groups)
                cos, sin = (tab[:, i, t, :].unsqueeze(1).broadcast_to([P, groups, half]) for i in range(2))
                V.tensor_tensor(w[:, :, 0, :], v[:, :, 0, :], cos, ALU.mult)
                link(V.tensor_tensor(tmp, v[:, :, 1, :], sin, ALU.mult))
                link(V.tensor_tensor(w[:, :, 0, :], w[:, :, 0, :], tmp, ALU.subtract))
                V.tensor_tensor(w[:, :, 1, :], v[:, :, 1, :], cos, ALU.mult)
                link(V.tensor_tensor(tmp, v[:, :, 0, :], sin, ALU.mult))
                V.tensor_tensor(w[:, :, 1, :], w[:, :, 1, :], tmp, ALU.add).then_inc(signal, 1)

            def add_residual(stage, k, t, half):
                ring.wait_full(dve, stage, k)
                cols = slice(half * 512, (half + 1) * 512)
                b = bank(stage, k)
                V.tensor_tensor((qk_tok if stage == 'out_0' else qk_da)[:, k % 2, :], b, bc[:, t // 2, 2, cols], ALU.mult).then_inc(ring.read(stage, k), 1)
                ring.wait_read(dve, stage, k)
                return V.tensor_tensor(X[:, t, cols], X[:, t, cols], (qk_tok if stage == 'out_0' else qk_da)[:, k % 2, :], ALU.add)

            dve.wait_ge(filter_in, 16 * len(filter_loads))
            filter_arg("filter_a", 0)
            dve.wait_ge(filt_sin, 1)
            filter_arg("filter_b", 1)
            for k in range(8):
                t, n = k // 4, k % 4
                ring.wait_full(dve, "filter_c", k)
                V.tensor_tensor(filt[:, t, n, :], bank("filter_c", k), window[:, t, :], ALU.mult)\
                    .then_inc(ring.read("filter_c", k), 1)
            for k in range(8):
                ring.wait_read(dve, "filter_c", k)
            for o in range(2):
                ins = V.tensor_tensor(filt[0:1, 0, 2 * o, :], filt[0:1, 0, 2 * o, :], skiprow[:, o, :], ALU.add)
            ins.then_inc(filt_taps, 1)

            mods("0a")
            norm_rows("0a", (0, 1))

            for k in range(10):
                ring.wait_full(dve, "filter_dft", k)
            V.memset(upad[:, :, :, 0:1], 0.0)
            V.memset(upad[:, :, :, SEQ + 1:SEQ + 2], 0.0).then_inc(conv_edges, 1)
            dve.wait_ge(conv_in, 16 * len(conv_loads))
            dve.wait_ge(conv_edges, 1)
            for m in range(12):
                ring.wait_read(dve, "u_proj", m)
                if 2 <= m < 8:
                    ring.wait_full(dve, "u_turn", m - 2)
                dst = (uconv[:, m % 2, :] if m < 8 else x2T[:, m - 8, :]).rearrange("p (a n) -> p a n", a=2)
                u = upad[:, m % 2]
                link(V.tensor_scalar(dst, u[:, :, 0:SEQ], cw[:, 0, m:m + 1], cb[:, m:m + 1], ALU.mult, ALU.add))
                link(V.scalar_tensor_tensor(out=dst, in0=u[:, :, 1:SEQ + 1], scalar=cw[:, 1, m:m + 1], in1=dst,
                                            op0=ALU.mult, op1=ALU.add))
                V.scalar_tensor_tensor(out=dst, in0=u[:, :, 2:SEQ + 2], scalar=cw[:, 2, m:m + 1], in1=dst,
                                       op0=ALU.mult, op1=ALU.add).then_inc(conv_done, 1)
            for k in range(8):
                ring.wait_read(dve, "u_turn", k)
            for k in range(10):
                ring.wait_read(dve, "filter_dft", k)
            dve.wait_ge(conv_done, 12)
            for o in range(2):
                for s in range(2):
                    if o or s:
                        for m in range((2, 4)[(2 * o + s - 1) // 2]):
                            oo, sp_ = (2 * o + s - 1) // 2, (2 * o + s - 1) % 2
                            ring.wait_full(dve, f"idft_{oo}", (2, 4)[oo] * sp_ + m)
                    st = f"dft_{o}"
                    for m in range(4):
                        ring.wait_full(dve, st, 4 * s + m)
                    for m in range(2):
                        ur, ui = bank(st, 4 * s + m), bank(st, 4 * s + 2 + m)
                        hr, hi = H[:, o, m, :], H[:, o, 2 + m, :]
                        hr_i = H[:, o, 4, :] if m == 0 else hr
                        V.tensor_tensor(specY[:, m, :], ur, hr, ALU.mult)
                        link(V.tensor_tensor(spec_t, ui, hi, ALU.mult))
                        link(V.tensor_tensor(specY[:, m, :], specY[:, m, :], spec_t, ALU.subtract))
                        V.tensor_tensor(specY[:, 2 + m, :], ur, hi, ALU.mult).then_inc(ring.read(st, 4 * s + m), 1)
                        V.tensor_tensor(spec_t, ui, hr_i, ALU.mult).then_inc(ring.read(st, 4 * s + 2 + m), 1)
                        ring.wait_read(dve, st, 4 * s + 2 + m)
                        ins = V.tensor_tensor(specY[:, 2 + m, :], specY[:, 2 + m, :], spec_t, ALU.add)
                        if m == 0:
                            link(ins)
                    ins.then_inc(spec_done, 1)
                    for m in range((2, 4)[o]):
                        k = (2, 4)[o] * s + m
                        ring.wait_full(dve, f"idft_{o}", k)
                        if o == 0:
                            V.tensor_tensor(vtok[:, 2 * s + m, :], bank("idft_0", k), x1tok[:, 2 * s + m, :],
                                            ALU.mult).then_inc(ring.read("idft_0", k), 1)
                        else:
                            cols = slice(s * SEQ, (s + 1) * SEQ)
                            V.tensor_tensor(catH[:, m, cols], bank("idft_1", k)[:, 0:SEQ], x2T[:, m, cols],
                                            ALU.mult).then_inc(ring.read("idft_1", k), 1)

            dve.wait_ge(ret_in, 16 * len(ret_loads))
            for n in range(2 * NT):
                t = n % NT
                ring.wait_full(dve, "qk_proj", n)
                if n >= 2:
                    ring.wait_full(dve, "qk_turn", n - 2)
                    ring.wait_read(dve, "qk_proj", n - 2)
                dst, src = qk_tok[:, n % 2, :], bank("qk_proj", n)
                if t < 2:
                    V.tensor_copy(dst, src).then_inc(ring.read("qk_proj", n), 1)
                else:
                    rotate(dst, src, rope_r, rope_t[:, n % 2, :], t - 2, RET_HEADS, RET_DK // 2, ring.read("qk_proj", n))
            x_, e_, z_, p_ = (lgt[:, i, :] for i in range(4))
            link(V.tensor_scalar(e_, x_, -1.0, None, ALU.mult))
            V.tensor_tensor(e_, e_, x_, ALU.min).then_inc(decay_arg, 1)
            dve.wait_ge(decay_exp, 1)
            link(V.tensor_scalar(z_, e_, 2.0, None, ALU.add))
            link(V.reciprocal(z_, z_))
            link(V.tensor_tensor(z_, z_, e_, ALU.mult))
            link(V.tensor_tensor(e_, z_, z_, ALU.mult))
            link(V.tensor_scalar(p_, e_, 1.0 / 17.0, 1.0 / 15.0, ALU.mult, ALU.add))
            for k in (13, 11, 9, 7, 5, 3, 1):
                link(V.tensor_tensor(p_, p_, e_, ALU.mult))
                link(V.tensor_scalar(p_, p_, 1.0 / k, None, ALU.add))
            link(V.tensor_tensor(p_, p_, z_, ALU.mult))
            link(V.tensor_scalar(lg, x_, 0.0, None, ALU.min))
            link(V.scalar_tensor_tensor(out=lg, in0=p_, scalar=-2.0, in1=lg, op0=ALU.mult, op1=ALU.add))
            link(V.tensor_scalar(lgs[:, 0, :], lg, float(CTX), None, ALU.mult))
            link(V.tensor_scalar(lgs[:, 2, :], lg, -1.0, None, ALU.mult))
            link(V.tensor_scalar(dist_f, dist, 0.0, None, ALU.max))
            V.tensor_scalar(dist_b, dist, -1.0, 0.0, ALU.mult, ALU.max).then_inc(decay_arg, 1)
            flat2 = lambda v: v.rearrange("p a n -> p (a n)")
            KS = RET_DK ** -0.5
            for h in range(RET_HEADS):
                dve.wait_ge(decay_exp, 2 * h + 2)
                e0, e1 = (decay_e[:, i, :].rearrange("p (a n) -> p a n", a=2) for i in range(2))
                link(V.scalar_tensor_tensor(out=e0, in0=dist, scalar=0.0, in1=e0, op0=ALU.is_ge, op1=ALU.mult))
                link(V.scalar_tensor_tensor(out=e1, in0=dist, scalar=0.0, in1=e1, op0=ALU.is_le, op1=ALU.mult))
                link(V.tensor_tensor(e0, e0, e1, ALU.add))
                V.tensor_scalar(decay[:, :, 0, :], e0, KS, None, ALU.mult).then_inc(decay_used, 1)
                dve.wait_ge(decay_exp, 2 * h + 3)
                link(V.tensor_tensor(e0, e0, e1, ALU.add))
                V.tensor_scalar(decay[:, :, 1, :], e0, KS, None, ALU.mult).then_inc(decay_used, 1)
                dve.wait_ge(decay_used, 2 * h + 2)
                if h:
                    for t in range(NT):
                        ring.wait_full(dve, "ret_o", NT * (h - 1) + t)
                for kt in range(4):
                    ring.wait_full(dve, "ret_s", 4 * h + kt)
                    if kt < 2:
                        V.tensor_tensor(sT0[:, kt, :], bank("ret_s", 4 * h + kt),
                                        decay[:, kt].rearrange("p a n -> p (a n)"), ALU.mult)\
                            .then_inc(ring.read("ret_s", 4 * h + kt), 1)
                    else:
                        V.tensor_tensor(sT2[:, kt - 2, :], bank("ret_s", 4 * h + kt)[:, 0:SEQ], decay[:, kt - 2, 0, :],
                                        ALU.mult).then_inc(ring.read("ret_s", 4 * h + kt), 1)
                for t in range(NT):
                    n = NT * h + t
                    ring.wait_full(dve, "ret_o", n)
                    link(V.bn_stats(ret_stat[:, t, :], bank("ret_o", n)[:, 0:RET_DV]))
                    link(V.bn_aggr(ret_mv[:, t, :], ret_stat[:, t, :]))
                    V.tensor_scalar(ret_mv[:, t, 1:2], ret_mv[:, t, 1:2], EPS, None, ALU.add).then_inc(ret_var, 1)
                for t in range(NT):
                    n = NT * h + t
                    dve.wait_ge(ret_dev, n + 1)
                    link(V.reciprocal(ret_mv[:, t, 1:2], ret_mv[:, t, 1:2]))
                    if n >= 2:
                        ring.wait_full(dve, "ret_turn", n - 2)
                    r_ = ret_row[:, t % 2, :]
                    V.tensor_scalar(r_, bank("ret_o", n)[:, 0:RET_DV], ret_mv[:, t, 0:1], ret_mv[:, t, 1:2],
                                    ALU.subtract, ALU.mult).then_inc(ring.read("ret_o", n), 1)
                    ring.wait_read(dve, "ret_o", n)
                    V.tensor_tensor(r_, r_, g_tok[:, t, h * RET_DV:(h + 1) * RET_DV], ALU.mult).then_inc(ret_rows, 1)
            for k in range(2 * NT):
                ins = add_residual("out_0", k, k // 2, k % 2)
                if k % 2:
                    ins.then_inc(residual, 1)
            dve.wait_ge(residual, NT)

            def top8_mask(t):
                link(V.tensor_tensor(choice, scores[:, t, :], router_b, ALU.add))
                for g in range(NG):
                    ins = V.max(best[:, g, :], choice[:, g * 8:(g + 1) * 8])
                link(ins)
                link(V.tensor_tensor(gsum, best[:, :, 0], best[:, :, 1], ALU.add))
                link(V.max(gtop, gsum))
                link(V.max_index(gidx, gtop, gsum))
                link(V.tensor_copy(gidxf, gidx))
                link(V.tensor_tensor(geq, iota8, gidxf[:, 0:TOPG].unsqueeze(2).broadcast_to([P, TOPG, NG]), ALU.is_equal))
                link(V.tensor_reduce(gmask, geq.rearrange("p k g -> p g k"), AX_X, ALU.add))
                link(V.tensor_scalar(gneg, gmask, 1.0, BIG, ALU.subtract, ALU.mult))
                c3 = choice.rearrange("p (g n) -> p g n", g=NG)
                link(V.tensor_tensor(c3, c3, gmask.unsqueeze(2).broadcast_to([P, NG, NE // NG]), ALU.mult))
                link(V.tensor_tensor(c3, c3, gneg.unsqueeze(2).broadcast_to([P, NG, NE // NG]), ALU.add))
                link(V.max(gtop, choice))
                link(V.match_replace(replaced, gtop, choice, -3e38))
                return V.tensor_tensor(picked[:, t, :], replaced, choice, ALU.not_equal)

            def act_chunks(v):
                return v.rearrange("p (c q) -> p q c", c=2)

            def pairs_of(v):
                return v.rearrange("p (q c) -> p q c", c=2)

            def overflow_dve(l):
                t0, tiles = LT[l]
                nb = tiles - 1
                step = M["step", l]
                with overflow(dve, l):
                    with dve.Fori(0, NE) as e:
                        for b in range(nb):
                            n = e * nb + b
                            oh = one_hot[:, 0, 0:tiles, :]
                            V.tensor_scalar(oh, iota1.unsqueeze(1).broadcast_to([P, tiles, P]), float(P * (b + 1)),
                                            None, ALU.add).then_inc(step, 1)
                            dve.wait_ge(step, n * 3 + 1)
                            V.tensor_tensor(oh, pos1[:, t0:t0 + tiles, bass.ds(e, 1)].broadcast_to([P, tiles, P]), oh,
                                            ALU.is_equal).then_inc(M["dve", l], 1)
                            dve.wait_ge(M["pe", l], n * 5 + 1)
                            V.tensor_copy(slot_w[:, 0:1], ps[:, 7, 1:2]).then_inc(step, 1)
                            V.scalar_tensor_tensor(out=slot_empty[:, 0:1], in0=ps[:, 7, 0:1], scalar=0.0,
                                                   in1=spare_id1, op0=ALU.is_equal, op1=ALU.mult).then_inc(step, 1)
                            dve.wait_ge(step, n * 3 + 3)
                            V.scalar_tensor_tensor(out=gather_idx[:, 0, :], in0=ps[:, 7, 0:1], scalar=-1.0,
                                                   in1=slot_empty[:, 0:1], op0=ALU.add, op1=ALU.add)\
                                .then_inc(M["dve", l], 1)
                            dve.wait_ge(M["act", l], n * 4 + 2)
                            V.scalar_tensor_tensor(out=act_chunks(act[:, 0, :]), in0=pairs_of(ps[:, 2, ED:2 * ED]),
                                                   scalar=slot_w[:, 0:1], in1=pairs_of(gsil[:, 0, :]), op0=ALU.mult,
                                                   op1=ALU.mult).then_inc(M["dve", l], 1)
                            dve.wait_ge(M["pe", l], n * 5 + 5)
                            V.tensor_copy(yb[:, 0, 512:], ps[:, 6, :]).then_inc(M["dve", l], 1)
                            dve.wait_ge(M["out", l], n * 16 + 16)

            def experts_phase(l):
                t0, tiles = LT[l]
                before = (0, NT)[l]
                dve.wait_ge(moe_in, 16 * len(moe_loads(0)) * (l + 1))
                for k in range(tiles):
                    t = t0 + k
                    ring.wait_read(dve, f"route_{l}", k)
                    top8_mask(t).then_inc(picks, 1)
                    dve.wait_ge(picks, before + k + 1)
                    link(V.tensor_tensor_reduce(out=replaced, in0=scores[:, t, :], in1=picked[:, t, :], scale=1.0,
                                                scalar=0.0, op0=ALU.mult, op1=ALU.add, accum_out=wsum))
                    link(V.tensor_scalar(wsum, wsum, 1e-20, None, ALU.add))
                    link(V.reciprocal(wsum, wsum))
                    V.tensor_scalar(idw[:, t, :, 1], replaced, wsum, ROUTED_SCALE, ALU.mult, ALU.mult)
                    V.tensor_copy(idw[:, t, :, 0], token_id1[:, t:t + 1].broadcast_to([P, NE])).then_inc(id_weights, 1)
                for k in range(tiles + 1):
                    ring.wait_full(dve, f"pos_{l}", k)
                    b = bank(f"pos_{l}", k)[:, 0:NE]
                    if k < tiles:
                        V.scalar_tensor_tensor(out=pos1[:, t0 + k, :], in0=b, scalar=1.0, in1=picked[:, t0 + k, :],
                                               op0=ALU.add, op1=ALU.mult).then_inc(ring.read(f"pos_{l}", k), 1)
                        ring.wait_read(dve, f"pos_{l}", k)
                    else:
                        V.tensor_reduce(counts_max, b, AX_X, ALU.max).then_inc(ring.read(f"pos_{l}", k), 1)
                        ring.wait_read(dve, f"pos_{l}", k)
                        V.tensor_scalar(flags[:, l:l + 1], counts_max, P + 0.5, None, ALU.is_gt).then_inc(flag_ready, 1)

                def one_hot_of(e, u):
                    one = slice(e, e + 1) if isinstance(e, int) else bass.ds(e, 1)
                    V.tensor_tensor(one_hot[:, u, 0:tiles, :], pos1[:, t0:t0 + tiles, one].broadcast_to([P, tiles, P]),
                                    iota1.unsqueeze(1).broadcast_to([P, tiles, P]), ALU.is_equal).then_inc(hot, 1)

                def slots_of(e, u, where, free=None):
                    one = slice(e, e + 1) if isinstance(e, int) else bass.ds(e, 1)
                    if free is None:
                        V.tensor_copy(slot_w[:, one], where[:, 1:2])
                    V.scalar_tensor_tensor(out=slot_empty[:, u:u + 1], in0=where[:, 0:1], scalar=0.0, in1=spare_id1,
                                           op0=ALU.is_equal, op1=ALU.mult).then_inc(E["empty", l], 1)
                    dve.wait_ge(E["empty", l], e + 1)
                    V.scalar_tensor_tensor(out=slot_u[:, one], in0=where[:, 0:1], scalar=-1.0,
                                           in1=slot_empty[:, u:u + 1], op0=ALU.add, op1=ALU.add).then_inc(slot_table, 1)
                    if free is not None:
                        V.tensor_copy(slot_w[:, one], where[:, 1:2]).then_inc(free, 1)

                def shared_act(t):
                    dve.wait_ge(sh_silu, before + t + 1)
                    if t >= 2:
                        ring.wait_full(dve, f"sh_t_{l}", t - 2)
                    V.tensor_tensor(act_chunks(act[:, t % 2, :]), pairs_of(bank(f"sh_gu_{l}", t)[:, ED:2 * ED]),
                                    pairs_of(gsil[:, t % 2, :]), ALU.mult).then_inc(ring.read(f"sh_gu_{l}", t), 1)

                shared_act(0)
                one_hot_of(0, 0)
                for e in range(TABLES_FIRST):
                    one_hot_of(e + 1, (e + 1) % 2)
                    ring.wait_full(dve, f"table_{l}", e)
                    slots_of(e, e % 2, bank(f"table_{l}", e), ring.read(f"table_{l}", e))
                    dve.wait_ge(slot_table, NE * l + e + 1)
                for k in range(tiles):
                    t = t0 + k
                    link(V.scalar_tensor_tensor(out=row_sum, in0=expert_no, scalar=float(P),
                                                in1=picked[:, t, :], op0=ALU.mult, op1=ALU.mult))
                    link(V.tensor_tensor(row_sum, row_sum, pos1[:, t, :], ALU.add))
                    for b in range(1, tiles):
                        link(V.tensor_scalar(choice, pos1[:, t, :], b * P + 0.5, float((NE - 1) * P), ALU.is_gt, ALU.mult))
                        link(V.tensor_tensor(row_sum, row_sum, choice, ALU.add))
                    link(V.max(row_best, row_sum))
                    link(V.tensor_scalar(combine_idx[:, t, :], row_best, 1.0, None, ALU.subtract))

                def shared_rows(t):
                    for half in range(2):
                        k = 2 * t + half
                        ring.wait_full(dve, f"sh_y_{l}", k)
                        cols = slice(half * 512, (half + 1) * 512)
                        tmp = one_hot[:, 0].rearrange("p t s -> p (t s)")
                        V.tensor_tensor(tmp, bank(f"sh_y_{l}", k), bc[:, (t0 + t) // 2, 2, cols], ALU.mult)\
                            .then_inc(ring.read(f"sh_y_{l}", k), 1)
                        ring.wait_read(dve, f"sh_y_{l}", k)
                        link(V.tensor_tensor(X[:, t0 + t, cols], X[:, t0 + t, cols], tmp, ALU.add))

                shared_act(1)
                for t in range(tiles):
                    if t >= 2:
                        shared_act(t)
                    shared_rows(t)

                def rows_out_half(e, u, stored):
                    dve.wait_ge(E["y_full", l], e + 1)
                    at_least(dve, E["stored", l, u], stored * 16)
                    V.tensor_copy(yb[:, u, 512:], ps[:, 6, :]).then_inc(E["y_read_d", l], 1)

                def step(e, i4, r):
                    i = r % 2
                    dve.wait_ge(E["sg_done", l], e + 1)
                    at_least(dve, E["aT_full", l], e - 1)
                    w = slot_w[:, e:e + 1] if isinstance(e, int) else slot_w[:, bass.ds(e, 1)]
                    V.scalar_tensor_tensor(out=act_chunks(act[:, i, :]), in0=pairs_of(ps[:, 2 + i, ED:2 * ED]), scalar=w,
                                           in1=pairs_of(gsil[:, i, :]), op0=ALU.mult,
                                           op1=ALU.mult).then_inc(E["act_done", l], 1)
                    if not isinstance(e, int) or e > 0:
                        rows_out_half(e - 1, (r - 1) % YB, i4)
                    x = e + TABLES_FIRST
                    if not isinstance(e, int) or x < NE:
                        dve.wait_ge(hot_used, e + (1 + (NE - TABLES_FIRST) * l))
                        u = (r + TABLES_FIRST) % 2
                        slots_of(x, u, ps[:, 7, 0:2])
                    if not isinstance(e, int) or x + 1 < NE:
                        one_hot_of(x + 1, (r + TABLES_FIRST + 1) % 2)

                step(0, -1, 4)
                for r in range(1, 5):
                    step(r, 0, r)
                with dve.Fori(1, NE // 4 - 2) as i4:
                    for r in range(1, 5):
                        step(i4 * 4 + r, i4, r)
                for e in range(NE - 7, NE):
                    step(e, (e - 1) // 4, (e - 1) % 4 + 1)
                rows_out_half(NE - 1, 3, NE // 4 - 1)
                overflow_dve(l)
                for k in range(2 * tiles):
                    t, g = t0 + k // 2, k % 2
                    dve.wait_ge(combine_in[g], 64 * ((0, NT)[l] + k // 2 + 1))
                    v = combined[:, g]
                    V.tensor_tensor(v[:, 0, :], v[:, 0, :], v[:, 1, :], ALU.add)
                    link(V.tensor_tensor(v[:, 2, :], v[:, 2, :], v[:, 3, :], ALU.add))
                    if g == 0:
                        V.tensor_tensor(combine_sum, v[:, 0, :], v[:, 2, :], ALU.add).then_inc(combine_used, 1)
                        continue
                    link(V.tensor_tensor(v[:, 0, :], v[:, 0, :], v[:, 2, :], ALU.add))
                    V.tensor_tensor(combine_sum, v[:, 0, :], combine_sum, ALU.add).then_inc(combine_used, 1)
                    dve.wait_ge(combine_used, 2 * ((0, NT)[l]) + k + 1)
                    link(V.tensor_tensor(combine_sum, combine_sum, bc[:, t // 2, 2, :], ALU.mult))
                    ins = V.tensor_tensor(X[:, t, :], X[:, t, :], combine_sum, ALU.add)
                    if k // 2 < tiles - 1:
                        ins.then_inc(residual, 1)
                    else:
                        ins.then_inc(moe_done, 1)

            mods("0b")
            norm_rows("0b", (0, 1))
            experts_phase(0)

            dve.wait_ge(residual, 2 * NT - 1)
            dve.wait_ge(moe_done, 1)
            mods("1a")
            norm_rows("1a", (0, 1))
            dve.wait_ge(da_in_sem, 16 * len(da_loads))
            for n, (c, t) in enumerate(DA_USES):
                ring.wait_full(dve, "da_qk", n)
                if n >= 2:
                    ring.wait_full(dve, "da_turn", n - 2)
                    ring.wait_read(dve, "da_qk", n - 2)
                dst, src = qk_da[:, n % 2, :], bank("da_qk", n)
                if t < 2:
                    V.tensor_copy(dst, src).then_inc(ring.read("da_qk", n), 1)
                else:
                    rotate(dst, src, rope_d, rope_dt[:, n % 2, :], t - 2, 8, DA_HD // 2, ring.read("da_qk", n))
            for i in range(2):
                ins = V.tensor_tensor_reduce(out=lamv[:, 2 * i, :], in0=lamv[:, 2 * i, :], in1=lamv[:, 2 * i + 1, :],
                                             scale=1.0, scalar=0.0, op0=ALU.mult, op1=ALU.add,
                                             accum_out=lamt[:, i:i + 1])
            ins.then_inc(lam_sums, 1)
            dve.wait_ge(lam_exp, 1)
            link(V.tensor_tensor(lamt[:, 2:3], lamt[:, 1:2], lamt[:, 0:1], ALU.subtract))
            link(V.tensor_scalar(lamt[:, 2:3], lamt[:, 2:3], LAMBDA_INIT, None, ALU.subtract))
            sc = DA_HD ** -0.5

            def mix(n):
                i = n % 2
                for c in range(2):
                    ring.wait_read(dve, "da_s", 2 * n + c)
                link(V.reciprocal(sinv[:, i, :], ssum[:, i, :]))
                link(V.tensor_tensor(sinv[:, i, 1:2], sinv[:, i, 1:2], lamt[:, 2:3], ALU.mult))
                if n >= 2:
                    ring.wait_full(dve, "da_at", n - 2)
                link(V.tensor_scalar(adiff[:, i, :], prob[:, i, 0, :], sinv[:, i, 0:1], None, ALU.mult))
                V.scalar_tensor_tensor(out=adiff[:, i, :], in0=prob[:, i, 1, :], scalar=sinv[:, i, 1:2],
                                       in1=adiff[:, i, :], op0=ALU.mult, op1=ALU.add).then_inc(probs_mixed, 1)

            for n in range(2 * DA_HEADS + 1):
                if n < 2 * DA_HEADS:
                    i = n % 2
                    if n >= 2:
                        for c in range(2):
                            ring.wait_read(dve, "da_s", 2 * (n - 2) + c)
                    for c in range(2):
                        ring.wait_full(dve, "da_s", 2 * n + c)
                        ins = V.tensor_reduce(smax[:, i, c:c + 1], bank("da_s", 2 * n + c), AX_X, ALU.max)
                    link(ins)
                    V.tensor_scalar(smax[:, i, :], smax[:, i, :], -sc, None, ALU.mult).then_inc(score_max, 1)
                if n:
                    mix(n - 1)
            for qt in range(2):
                for m in range(DA_HEADS):
                    ring.wait_read(dve, "da_o", qt * DA_HEADS + m)
                o3 = o_tok[:, qt, :].rearrange("p (h d) -> p h d", h=DA_HEADS)
                link(V.tensor_tensor(o_squares, o3, o3, ALU.mult))
                link(V.tensor_reduce(ohs[:, qt, :], o_squares, AX_X, ALU.add))
                V.tensor_scalar(ohs[:, qt, :], ohs[:, qt, :], 1.0 / P, 1e-5, ALU.mult, ALU.add).then_inc(o_var, 1)
            link(V.tensor_scalar(subln, subln, 1.0 - LAMBDA_INIT, None, ALU.mult))
            for qt in range(2):
                dve.wait_ge(o_dev, qt + 1)
                o3 = o_tok[:, qt, :].rearrange("p (h d) -> p h d", h=DA_HEADS)
                link(V.reciprocal(ohs[:, qt, :], ohs[:, qt, :]))
                link(V.tensor_tensor(o3, o3, ohs[:, qt, :].unsqueeze(2).broadcast_to([P, DA_HEADS, P]), ALU.mult))
                V.tensor_tensor(o3, o3, subln.unsqueeze(1).broadcast_to([P, DA_HEADS, P]), ALU.mult).then_inc(o_rows, 1)
            for k in range(4):
                ins = add_residual("out_1", k, 2 + k // 2, k % 2)
                if k % 2:
                    ins.then_inc(residual, 1)
                else:
                    link(ins)
            dve.wait_ge(residual, 2 * NT - 1 + 2)
            mods("1b")
            norm_rows("1b", (1,))
            experts_phase(1)
            dve.wait_ge(residual, 2 * NT - 1 + 3)
            dve.wait_ge(moe_done, 2)
            norm_inverse("final")
            dve.wait_ge(final_in, 16)
            for j in range(2):
                V.scalar_tensor_tensor(out=hrow_mix[:, j, :], in0=X[:, 2 + j, :], scalar=rstd[:, 2 + j:3 + j],
                                       in1=final_g, op0=ALU.mult, op1=ALU.mult).then_inc(result, 1)

        @block.gpsimd
        def _(pool):
            def overflow_pool(l):
                nb = LT[l][1] - 1
                last_row = pool.alloc_register(f"more_last_row_{l}")
                with pool.Fori(0, NE) as e:
                    for b in range(nb):
                        n = e * nb + b
                        pool.wait_ge(M["dve", l], n * 4 + 2)
                        pool.reg_add(last_row, pool.zero_reg, NTOK - 1)
                        pool.indirect_dma_start(xg[:, 0, :], None, h_rows,
                                                bass.IndirectOffsetOnAxis(gather_idx[:, 0, :], 0),
                                                bounds_check=last_row).then_inc(M["xg", l], 16)
                        pool.wait_ge(M["xg", l], n * 16 + 16)
                pool.wait_ge(M["out", l], NE * nb * 16)

            def experts_phase(l):
                t0, tiles = LT[l]
                last_row = pool.alloc_register(f"last_row_{l}")
                for j in range(tiles):
                    pool.wait_ge(rows, ROWS_BEFORE[f"{l}b"] + j + 1)
                    t = t0 + j
                    pool.dma_start(h_rows[t * P:(t + 1) * P, :], hrow_moe[:, j % 2, :]).then_inc(rows_out[j % 2], 16)
                for i in range(2):
                    pool.wait_ge(rows_out[i], (32, 48)[l])
                for j in range(2):
                    ring.wait_full(pool, f"norm_{l}b", 2 * (tiles - 1 - j) + 1)

                def gather(e, u):
                    pool.wait_ge(slot_table, e + (NE * l + 1))
                    at_least(pool, E["xT_full", l], e - (XG - 1))
                    pool.reg_add(last_row, pool.zero_reg, NTOK - 1)
                    col_ = slot_u[:, e:e + 1] if isinstance(e, int) else slot_u[:, bass.ds(e, 1)]
                    nc.gpsimd.tensor_copy(gather_idx[:, u, :], col_).then_inc(E["gidx", l], 1)
                    pool.wait_ge(E["gidx", l], e + 1)
                    pool.reg_add(last_row, pool.zero_reg, NTOK - 1)
                    pool.indirect_dma_start(xg[:, u, :], None, h_rows,
                                            bass.IndirectOffsetOnAxis(gather_idx[:, u, :], 0),
                                            bounds_check=last_row).then_inc(E["xg_in", l, u], 16)

                for e in range(XG):
                    gather(e, e)
                with pool.Fori(1, NE // XG) as i4:
                    for r in range(XG):
                        gather(i4 * XG + r, r)
                for i in range(YB):
                    pool.wait_ge(E["stored", l, i], NE // YB * 16)
                before = (0, 2 * NT)[l]

                def combine(blocks):
                    for k in range(2 * tiles):
                        if k >= 2:
                            pool.wait_ge(combine_used, before + k - 1)
                        for j in range(4):
                            n = (k % 2) * 4 + j
                            pool.indirect_dma_start(combined[:, k % 2, j, :], None, y_rows[0:blocks * NE * P, :],
                                                    bass.IndirectOffsetOnAxis(combine_idx[:, t0 + k // 2, n:n + 1], 0),
                                                    bounds_check=blocks * NE * P - 1).then_inc(combine_in[k % 2], 16)

                pool.wait_ge(flag_ready, l + 1)
                more = pool.value_load(flags[0:1, l:l + 1], min_val=0, max_val=1)
                with pool.If(more > 0):
                    overflow_pool(l)
                    combine(tiles)
                with pool.If(more < 1):
                    combine(1)

            experts_phase(0)
            experts_phase(1)


_INS = ['x', 'c', 'ctx', 'c_ctx', 'w_ada', 'b_ada', 'norm_mix', 'norm_ffn', 'ab_w_in', 'ab_w_out', 'ret_decay_logit',
        'hy_conv_w', 'hy_conv_b', 'hy_w1', 'hy_b1', 'hy_freq1', 'hy_w2', 'hy_b2', 'hy_freq2', 'hy_w3', 'hy_skip',
        'da_w_in', 'da_w_out', 'da_lambda', 'da_subln', 'router_w', 'router_b', 'exp_w_gate', 'exp_w_up', 'exp_w_down',
        'sh_w_gate', 'sh_w_up', 'sh_w_down', 'norm_final']


def kernel(**inputs):
    import numpy as _np
    import concourse.bacc as _bacc
    from concourse import mybir as _mybir
    from concourse.bass_utils import run_bass_kernel_spmd as _run

    nc = _bacc.Bacc("TRN2", target_bir_lowering=False, num_devices=1)
    arrays, A, K = {}, {}, {}
    for name in _INS:
        a = _np.ascontiguousarray(inputs[name])
        arrays[f"in_{name}"] = a
        A[name] = nc.dram_tensor(f"in_{name}", a.shape, _mybir.dt.from_np(a.dtype), kind="ExternalInput").ap()
    for name, a in shape_constants().items():
        a = _np.ascontiguousarray(a)
        arrays[f"const_{name}"] = a
        K[name] = nc.dram_tensor(f"const_{name}", a.shape, _mybir.dt.from_np(a.dtype), kind="ExternalInput").ap()
    out = nc.dram_tensor("out_0", (1, SEQ, D), F32, kind="ExternalOutput").ap()
    build(nc, A, K, out)
    r = _run(nc, [arrays], core_ids=[0])
    return r.results[0]["out_0"]
```

```python
import math
from contextlib import ExitStack, contextmanager

import numpy as np

import concourse.bass as bass
from concourse import mybir

F32 = mybir.dt.float32
I32 = mybir.dt.int32
U32 = mybir.dt.uint32
BF16 = mybir.dt.bfloat16
ALU = mybir.AluOpType
ACT = mybir.ActivationFunctionType
AX_X = mybir.AxisListType.X

P = 128
D = 1024
KC = D // P
SEQ = 256
CTX = 256
NTOK = CTX + SEQ
NT = NTOK // P
DEPTH = 2
EPS = 1e-6
GRID_W = 64
ROPE_BASE = 10000.0

RET_HEADS, RET_DK, RET_DV = 4, 128, 256
RET_V = RET_HEADS * RET_DV
HW = 512
HY_BANDS = 16
HY_EMB = 2 * HY_BANDS + 1
HY_FFN = 64
NFFT = 2 * SEQ

DA_HEADS, DA_HD = 8, 64
LAMBDA_INIT = 0.8 - 0.6 * math.exp(-0.3)

NE = 64
NG = 8
TOPG = 4
TOPK = 8
ED = 256
ROUTED_SCALE = 2.5

BANKS = 8
DENSE_SLOTS = 3
EXPERT_SLOTS = 4
XG = 4
YB = 4
TABLES_FIRST = 5
BIG = 1e30
TAB = 6

TWO_PI = 2.0 * math.pi
MAGIC = 12582912.0
PI_1 = 6.28125
PI_2 = float(np.float32(TWO_PI - PI_1))
PI_3 = float(np.float32(TWO_PI - PI_1 - PI_2))
PI_SAFE = 3.1415925


LAG = 2

HALF = {"0a": 0, "0b": 1, "1a": 2, "1b": 3}
BCAST = {"0a": (0, (2,), (0, 1)), "0b": (1, (0, 1), (0, 1)), "0bg": (1, (2,), (0, 1)),
         "1a": (2, (2,), (1,)), "1b": (3, (0, 1), (1,)), "1bg": (3, (2,), (1,))}


def bcast_uses(tag):
    _, vectors, streams = BCAST[tag]
    return [(v, s, half) for v in vectors for s in streams for half in range(2)]


ALL_BCASTS = [(f"bcast_{tag}", k) for tag in BCAST for k in range(len(bcast_uses(tag)))]


def bcasts_before(tag):
    names = list(BCAST)
    return sum(len(bcast_uses(x)) for x in names[:names.index(tag)])


MODS = [(tag, n) for tag in ("0a", "0b", "1a", "1b") for n in range(6)]
FILL_HYENA = ((1, 1), (1, 1))
FILL_RET = ((1, 1), (1, 1), (1, 1), (1, 1))
N_FILL_HYENA = sum(map(sum, FILL_HYENA))
LAST_MODS = (5, 17, 23)
assert 6 + N_FILL_HYENA + sum(map(sum, FILL_RET)) == 18


def mod_steps(first, count):
    steps = []
    for g in range(first, first + count):
        steps.append(("mod", g))
        if g and g - 1 not in LAST_MODS:
            steps.append(("modt", g - 1))
        if g in LAST_MODS:
            steps.append(("modt", g))
    return steps


FIRST_MODS = (mod_steps(0, 6)[0:3], mod_steps(0, 6)[3:7], mod_steps(0, 6)[7:])


def da_steps():
    steps, uses = [("norm", 0)], []
    for cols, m0 in (((2, 3), 0), ((0, 1), NT)):
        for t in range(NT):
            n = len(uses)
            pair = cols if m0 == 0 or t >= 2 else ()
            uses += [(c, t) for c in pair]
            if pair:
                steps += [("qk", n), ("qk", n + 1), ("turn", n)]
            steps.append(("v", m0 + t))
            if pair:
                steps.append(("turn", n + 1))
            if m0 == 0 and t + 1 < NT:
                steps.append(("norm", t + 1))
    return steps, uses


DA_STEPS, DA_USES = da_steps()


def shape_constants():
    f32 = np.float32
    k = {}
    k["ident"] = np.eye(P, dtype=f32)
    t = np.arange(SEQ, dtype=np.float64)
    tn = t / (SEQ - 1)
    bands = np.linspace(1e-4, HY_BANDS - 1, HY_BANDS)
    ang = (2.0 * math.pi / SEQ) * t[:, None] * bands[None, :]
    k["filter_features"] = np.concatenate([tn[:, None], np.cos(ang), -np.sin(ang)], axis=1).T.astype(f32)
    deltas = np.abs(np.linspace(math.log(1e-2) / 1.5, math.log(1e-2) / 0.3, HW))
    window = np.exp(-tn[:, None] * deltas[None, :])
    k["window"] = window.reshape(2, P, HW).transpose(1, 0, 2).astype(f32)
    f = np.arange(SEQ, dtype=np.float64)
    w = 2.0 * math.pi / NFFT
    re_f, im_f = np.cos(w * np.outer(t, f)), -np.sin(w * np.outer(t, f))
    nyquist = np.cos(math.pi * t)
    im_packed = im_f.copy()
    im_packed[:, 0] = nyquist
    re_nyq = re_f[:, 0:P].copy()
    re_nyq[:, 0] = nyquist
    fwd = np.concatenate([re_f, im_packed, im_f[:, 0:P], re_nyq], axis=1)
    k["dft_fwd"] = fwd.reshape(2, P, 6 * P).transpose(1, 0, 2).astype(f32)
    inv = np.zeros((NFFT, SEQ))
    inv[0:SEQ] = 2.0 * re_f.T
    inv[0] = 1.0
    inv[SEQ:] = 2.0 * im_f.T
    inv[SEQ] = nyquist
    inv /= NFFT
    k["dft_inv"] = inv.reshape(4, P, SEQ).transpose(1, 0, 2).astype(f32)
    for name, hd in (("rope_ret", RET_DK), ("rope_da", DA_HD)):
        nf = hd // 4
        fr = ROPE_BASE ** (-np.arange(nf, dtype=np.float64) / nf)
        row, col = np.repeat(np.arange(SEQ // GRID_W), GRID_W), np.tile(np.arange(GRID_W), SEQ // GRID_W)
        a = np.concatenate([row[:, None] * fr, col[:, None] * fr], axis=-1)
        cs = np.stack([np.cos(a), np.sin(a)], axis=0).reshape(2, 2, P, hd // 2)
        k[name] = cs.transpose(2, 0, 1, 3).reshape(P, 2 * 2 * (hd // 2)).astype(f32)
    i, j = np.arange(SEQ), np.arange(SEQ)
    k["distance"] = (i[None, :] - j[:, None]).reshape(2, P, SEQ).transpose(1, 0, 2).astype(f32)
    k["iota1"] = np.tile(np.arange(1, P + 1, dtype=f32), (P, 1))
    k["iota8"] = np.tile(np.arange(NG, dtype=f32), (P, TOPG)).reshape(P, TOPG * NG)
    k["earlier"] = (np.arange(P)[:, None] < np.arange(P)[None, :]).astype(f32)
    k["ones"] = np.ones((P, P), f32)
    k["place"] = np.arange(P)[:, None].astype(f32)
    k["expert_no"] = np.tile(np.arange(NE, dtype=f32), (P, 1))
    return k


class BankRing:

    def __init__(self, order, bank_full, bank_read):
        self.order, self.bank_full, self.bank_read = order, bank_full, bank_read
        self.at = {use: n for n, use in enumerate(order)}
        self.claimed = 0

    def bank(self, stage, k):
        return self.at[(stage, k)] % BANKS

    def claim(self, pe, stage, k):
        n = self.at[(stage, k)]
        assert n == self.claimed, (stage, k, self.order[self.claimed])
        self.claimed += 1
        if n >= BANKS:
            pe.wait_ge(self.bank_read[n % BANKS], n // BANKS)

    def full(self, stage, k):
        return self.bank_full[self.bank(stage, k)]

    def read(self, stage, k):
        return self.bank_read[self.bank(stage, k)]

    def wait_full(self, eng, stage, k):
        n = self.at[(stage, k)]
        eng.wait_ge(self.bank_full[n % BANKS], n // BANKS + 1)

    def wait_read(self, eng, stage, k):
        n = self.at[(stage, k)]
        eng.wait_ge(self.bank_read[n % BANKS], n // BANKS + 1)

    def fence(self, pe):
        for n in range(self.claimed - BANKS, self.claimed):
            pe.wait_ge(self.bank_read[n % BANKS], n // BANKS + 1)


class Chain:

    def __init__(self, eng, sem):
        self.eng, self.sem, self.n = eng, sem, 0

    def __call__(self, ins):
        self.n += 1
        ins.then_inc(self.sem, 1)
        self.eng.wait_ge(self.sem, self.n)


def psum_order():
    def norm(tag, t):
        return [(f"norm_{tag}", 2 * t), (f"norm_{tag}", 2 * t + 1)]

    def bcast(tag):
        return [(f"bcast_{tag}", k) for k in range(len(bcast_uses(tag)))]

    filled = [6]

    def fill(count):
        filled[0] += count
        return mod_steps(filled[0] - count, count)

    def moe(tag, tiles):
        def rows(t):
            return [(f"sh_t_{tag}", t), (f"sh_y_{tag}", 2 * t), (f"sh_y_{tag}", 2 * t + 1)]

        r = [(f"route_{tag}", k) for k in range(tiles)] + [(f"sh_gu_{tag}", 0), (f"sh_gu_{tag}", 1)]
        r += [(f"pos_{tag}", k) for k in range(tiles + 1)]
        for t in range(2):
            r += rows(t)
            if t + 2 < tiles:
                r.append((f"sh_gu_{tag}", t + 2))
        r += [(f"table_{tag}", e) for e in range(TABLES_FIRST)]
        for t in range(2, tiles):
            r += rows(t)
        return r

    a, b, c = FIRST_MODS
    o = a + [("filter_a", 0)] + b + [("filter_b", 0)] + c + [("mod_consts", 0)]
    o += norm("0a", 0) + norm("0a", 1)
    o += [("filter_c", k) for k in range(8)]
    o += norm("0a", 2) + norm("0a", 3)
    o += [("filter_dft", k) for k in range(10)]
    o += bcast("0a")
    for m in range(12):
        o.append(("u_proj", m))
        if 1 <= m <= 8:
            o.append(("u_turn", m - 1))
    for order in range(2):
        for s in range(2):
            o += [(f"dft_{order}", 4 * s + m) for m in range(4)]
            o += fill(FILL_HYENA[order][s])
            o += [(f"idft_{order}", (2, 4)[order] * s + m) for m in range((2, 4)[order])]
    for c in range(2):
        for t in range(NT):
            o.append(("qk_proj", c * NT + t))
            if c * NT + t:
                o.append(("qk_turn", c * NT + t - 1))
    o.append(("qk_turn", 2 * NT - 1))
    o += [("vg_proj", k) for k in range(4 * NT)]
    for h in range(RET_HEADS):
        o += [("ret_s", 4 * h + k) for k in range(4)]
        o += fill(FILL_RET[h][0])
        o += [("ret_o", NT * h + t) for t in range(NT)]
        o += fill(FILL_RET[h][1])
        o += [("ret_turn", NT * h + t) for t in range(NT)]
    o += bcast("0b")
    for t in range(NT):
        o += [("out_0", 2 * t), ("out_0", 2 * t + 1)]
        if t:
            o += norm("0b", t - 1)
    o += norm("0b", NT - 1) + bcast("0bg") + moe("0", NT)
    o += mod_steps(18, 6)
    for step in DA_STEPS:
        o += norm("1a", step[1]) if step[0] == "norm" else [("da_" + step[0], step[1])]
    o += bcast("1a") + bcast("1b")
    for n in range(2 * DA_HEADS + LAG):
        if n >= LAG:
            o.append(("da_at", n - LAG))
        if n < 2 * DA_HEADS:
            o += [("da_s", 2 * n), ("da_s", 2 * n + 1)]
        if n >= LAG:
            o.append(("da_o", n - LAG))
    o += [("da_ot", k) for k in range(4)]
    o += [("out_1", k) for k in range(4)]
    o += norm("1b", 0) + norm("1b", 1) + bcast("1bg") + moe("1", 2)
    return o


def build(nc, A, K, out):
    with ExitStack() as ctx:
        sems = {}

        def sem(name):
            if name not in sems:
                sems[name] = ctx.enter_context(nc.semaphore(name))
            return sems[name]

        order = psum_order()
        ring = BankRing(order, [sem(f"bank_full_{b}") for b in range(BANKS)],
                        [sem(f"bank_read_{b}") for b in range(BANKS)])
        ps = ctx.enter_context(nc.psum_tensor("ps", [P, BANKS, 512], F32))

        def bank(stage, k):
            return ps[:, ring.bank(stage, k), :]

        h_rows = nc.dram_tensor("h_rows", (NTOK, D), F32, kind="Internal").ap()
        y_rows = nc.dram_tensor("y_rows", (NE * NTOK, D), F32, kind="Internal").ap()

        WORDS = 53000
        arena = ctx.enter_context(nc.sbuf_tensor("arena", [P, WORDS], F32))

        class Region:
            def __init__(self, at, end=WORDS):
                self.at, self.end = at, end

            def take(self, *shape, parts=P, dt=F32):
                n = math.prod(shape)
                assert self.at + n <= self.end, (self.at, n, self.end)
                v = arena[0:parts, self.at:self.at + n]
                if dt != F32:
                    v = v.bitcast(dt)
                self.at += n
                names = ["a", "b", "c", "d"][:len(shape)]
                if len(shape) > 1:
                    v = v.rearrange(f"p ({' '.join(names)}) -> p {' '.join(names)}", **dict(zip(names, shape)))
                return v

        top = Region(0)
        WS = top.take(EXPERT_SLOTS, KC * 512)
        spare_at = top.at - KC * 512
        X = top.take(NT, D)
        bc = top.take(2, 3, D)
        hT = top.take(KC, NTOK)
        ident = top.take(P)
        cvec = top.take(2, KC)
        csilu = top.take(2, KC)
        ssq = top.take(NT)
        rstd = top.take(NT)
        flags = top.take(DEPTH, dt=I32)
        mod = top.take(4, 3, KC, 2)
        mod_consts = top.take(P)
        bias = mod_consts[:, 0:4 * 3 * KC].rearrange("p (h v c) -> p h v c", h=4, v=3)
        norm_g = mod_consts[:, 4 * 3 * KC:].rearrange("p (h c) -> p h c", h=4)
        iota1 = top.take(P)
        iota8 = top.take(TOPG, NG)
        earlier = top.take(P)
        ones = top.take(P)
        place = top.take(1)
        expert_no = top.take(NE)
        router_w2 = top.take(DEPTH, KC, NE)
        router_b2 = top.take(DEPTH, NE)
        diag = top.take(2, 4, P)
        mod_row = diag.rearrange("p a b c -> p a (b c)")
        scratch_at = top.at
        mod_rows_in = arena[:, scratch_at:scratch_at + P]
        top.take(1796)
        phase_at = top.at

        r = Region(scratch_at, phase_at)
        scores = r.take(NT, NE)
        lamv = scores.rearrange("p a b -> p (a b)").rearrange("p (a b) -> p a b", b=DA_HD)
        picked = r.take(NT, NE)
        pos1 = r.take(NT, NE)
        choice = r.take(NE)
        replaced = r.take(NE)
        best = r.take(NG, 8)
        gsum = r.take(NG)
        gtop = r.take(8)
        gidx = r.take(8, dt=U32)
        gidxf = r.take(8)
        geq = r.take(TOPG, NG)
        gmask = r.take(NG)
        gneg = r.take(NG)
        wsum = r.take(1)
        counts_max = r.take(1)
        slot_w = r.take(NE)
        slot_empty = r.take(2)
        row_sum = r.take(NE)
        row_best = r.take(8)
        combine_idx = r.take(NT, TOPK, dt=U32)
        slot_u = r.take(NE, dt=U32)
        gather_idx = r.take(XG, 1, dt=U32)
        r = Region(phase_at)
        DN = r.take(EXPERT_SLOTS, 2 * D)
        xg = r.take(XG, D)
        xgT = r.take(2, D)
        gsil = r.take(2, ED)
        act = r.take(2, ED)
        actT = r.take(2, 2 * P)
        one_hot = r.take(NT * P).bitcast(BF16).rearrange("p (a t s) -> p a t s", a=2, t=NT)
        idw = r.take(NT * NE * TAB // 2).bitcast(BF16).rearrange("p (t e c) -> p t e c", t=NT, e=NE)
        weight_left = r.take(NE)
        yb = hT.rearrange("p a n -> p (a n)").rearrange("p (a n) -> p a n", a=YB)

        r = Region(phase_at)
        H = r.take(2, 5, HW)
        dftf = r.take(2, 6 * P)
        dfti = r.take(4, SEQ)
        sub_at = r.at
        r = Region(WORDS - 4 * NTOK)
        catH = r.take(4, NTOK)
        r = Region(sub_at, WORDS - 4 * NTOK)
        window = r.take(2, HW)
        fdiff = r.take(2, 2, HW)
        fz = r.take(SEQ, parts=HY_EMB)
        fw1 = r.take(HY_FFN, parts=HY_EMB)
        fw2 = r.take(HY_FFN, parts=HY_FFN)
        fw3 = r.take(4 * HW, parts=HY_FFN)
        fcol = r.take(4, parts=HY_FFN)
        farg = r.take(SEQ, parts=HY_FFN)
        fturn = r.take(SEQ, parts=HY_FFN)
        fh = r.take(2, SEQ, parts=HY_FFN)
        skiprow = r.take(2, HW, parts=1)
        r = Region(spare_at, spare_at + KC * 512)
        filt = r.take(2, 4, HW)
        r = Region(sub_at, WORDS - 4 * NTOK)
        vtok = r.take(NT, HW)
        x1tok = r.take(NT, HW)
        uconv = r.take(2, NTOK)
        specY = r.take(4, HW)
        r = Region(WORDS - 4 * NTOK)
        cw = r.take(3, 12)
        cb = r.take(12)
        r = Region(spare_at, spare_at + KC * 512)
        x2T = r.take(4, NTOK)
        upad = r.take(2, 2, SEQ + 2)
        spec_t = r.take(HW)
        r = Region(phase_at, WORDS - 4 * NTOK)
        v_tok = r.take(NT, RET_V)
        g_tok = r.take(NT, RET_V)
        qT = r.take(RET_HEADS, NTOK)
        kT = r.take(RET_HEADS, NTOK)
        qk_tok = r.take(2, 512)
        rope_r = r.take(2, 2, RET_DK // 2)
        rope_t = r.take(2, 256)
        dist = r.take(2, SEQ)
        r = Region(spare_at, spare_at + KC * 512)
        dist_f = r.take(2, SEQ)
        dist_b = r.take(2, SEQ)
        decay = r.take(2, 2, SEQ)
        decay_e = r.take(2, 2 * SEQ)
        r = Region(r.at, r.end)
        ret_row = r.take(2, RET_DV)
        ret_stat = r.take(NT, 6)
        ret_mv = r.take(NT, 2)
        lg = r.take(2 * RET_HEADS)
        lgt = r.take(4, 2 * RET_HEADS)
        lg_ctx = r.take(2 * RET_HEADS)
        lg_neg = r.take(2 * RET_HEADS)
        r = Region(scratch_at, phase_at)
        sT0 = r.take(2, NTOK)
        sT2 = r.take(2, SEQ)
        catR = hT

        r = Region(phase_at)
        qTd = r.take(DA_HEADS, SEQ)
        kTd = r.take(DA_HEADS, NTOK)
        v_da = r.take(NT, D)
        qk_da = r.take(2, 512)
        rope_d = r.take(2, 2, DA_HD // 2)
        rope_dt = r.take(2, 256)
        o_tok = r.take(2, D)
        oT = r.take(DA_HEADS, SEQ)
        subln = r.take(P)
        lamt = r.take(8)
        combine_sum = r.take(D)
        hrow_da = oT.rearrange("p a n -> p (a n)").rearrange("p (a n) -> p a n", a=2)
        combined_more = o_tok
        r = Region(spare_at, spare_at + KC * 512)
        prob = r.take(2, 2, NTOK)
        adiff = r.take(2, NTOK)
        spare_rows = Region(spare_at, spare_at + KC * 512).take(4, D)
        combined = [spare_rows[:, 0:2], spare_rows[:, 2:4], combined_more]
        aT = r.take(1, NTOK)
        smax = r.take(2, 2)
        ssum = r.take(2, 2)
        sinv = r.take(2, 2)
        ohs = r.take(2, DA_HEADS)

        r = Region(phase_at + 4 * 2 * D)
        hrow_moe = r.take(2, D)
        final_g = Region(phase_at).take(D)

        col = lambda v: v.rearrange("(p a) -> p a", a=1)
        row = lambda v: v.rearrange("(a n) -> a n", a=1)
        every = lambda v, n=P: row(v).broadcast_to([n, v.shape[0]])
        start_loads = [
            (cvec[:, 0, :], A["c_ctx"].rearrange("(p c) -> p c", p=P)),
            (cvec[:, 1, :], A["c"].rearrange("a (p c) -> p (a c)", p=P)),
            (ident, K["ident"]),
        ]
        mod_loads = [(mod_rows_in[0:4 * 3 * KC, :], A["b_ada"].rearrange("l (r p) -> (l r) p", p=P))]
        mod_loads += [(mod_rows_in[KC * (12 + 2 * l + i):KC * (13 + 2 * l + i), :], A[g][l].rearrange("(c p) -> c p", p=P))
                      for l in range(DEPTH) for i, g in enumerate(("norm_mix", "norm_ffn"))]
        filter_loads = [
            (fz, K["filter_features"]),
            (fw1, A["hy_w1"][0]), (fw2, A["hy_w2"][0]), (fw3, A["hy_w3"][0]),
            (fcol[:, 0:1], col(A["hy_b1"][0])), (fcol[:, 1:2], col(A["hy_freq1"][0])),
            (fcol[:, 2:3], col(A["hy_b2"][0])), (fcol[:, 3:4], col(A["hy_freq2"][0])),
            (window, K["window"]), (dftf, K["dft_fwd"]), (dfti, K["dft_inv"]),
            (skiprow, A["hy_skip"][0:1]),
        ]
        token_loads = [(X[:, t, :], A["ctx"][0, t * P:(t + 1) * P, :]) for t in range(2)]
        token_loads += [(X[:, 2 + t, :], A["x"][0, t * P:(t + 1) * P, :]) for t in range(2)]
        conv_loads = [(cw[:, k, :].rearrange("p (i c) -> p i c", i=3), A["hy_conv_w"][0, k].rearrange("(i p c) -> p i c", p=P, c=4))
                      for k in range(3)]
        conv_loads += [(cb.rearrange("p (i c) -> p i c", i=3), A["hy_conv_b"][0].rearrange("(i p c) -> p i c", p=P, c=4))]
        ret_loads = [
            (rope_r, K["rope_ret"].rearrange("p (a b c) -> p a b c", a=2, b=2)),
            (dist, K["distance"]),
            (lgt[:, 0, :], every(A["ret_decay_logit"][0].rearrange("a h -> (a h)"))),
        ]
        da_loads = [
            (rope_d, K["rope_da"].rearrange("p (a b c) -> p a b c", a=2, b=2)),
            (subln, every(A["da_subln"][0])),
            (lamv, every(A["da_lambda"][0].rearrange("a h -> (a h)")).rearrange("p (a h) -> p a h", a=4)),
        ]

        moe_loads = [
            (iota1, K["iota1"]), (iota8, K["iota8"].rearrange("p (a b) -> p a b", a=TOPG)),
            (earlier, K["earlier"]), (ones, K["ones"]),
            (place, K["place"]), (expert_no, K["expert_no"]),
        ]
        for l in range(DEPTH):
            moe_loads += [(router_w2[:, l], A["router_w"][l].rearrange("(p c) n -> p c n", c=KC)),
                          (router_b2[:, l], every(A["router_b"][l]))]

        def columns(w, at):
            return w.rearrange("(c p) n -> p c n", p=P)[:, :, at:at + 512]

        def ada_columns(tag, n):
            w = A["w_ada"][HALF[tag] // 2].rearrange("(p c) n -> p c n", c=KC)
            at = (HALF[tag] % 2) * 3 * D + 512 * n
            return w[:, :, at:at + 512]

        def row_chunks(w, at):
            return w.rearrange("(c p) n -> p c n", p=P)[:, at:at + 4, :]

        dense = []
        first = {}

        def stream(name, items, last_use):
            first[name] = len(dense)
            dense.extend((src, last_use(n)) for n, src in enumerate(items))

        U_AT = 2 * RET_HEADS * RET_DK + 2 * RET_V
        ab_in, da_in = A["ab_w_in"][0], A["da_w_in"][0]
        mods = [ada_columns(tag, n) for tag, n in MODS]
        stream("ada_0a", mods[0:6], lambda n: ("mod", n))
        stream("u", [columns(ab_in, U_AT + 512 * n) for n in range(3)], lambda n: ("u_proj", 4 * n + 3))
        stream("fill_hyena", mods[6:6 + N_FILL_HYENA], lambda n: ("mod", 6 + n))
        stream("qk", [columns(ab_in, 512 * n) for n in range(2)], lambda n: ("qk_proj", NT * n + NT - 1))
        stream("vg", [columns(ab_in, 512 * (2 + n)) for n in range(4)], lambda n: ("vg_proj", NT * n + NT - 1))
        stream("fill_ret", mods[6 + N_FILL_HYENA:18], lambda n: ("mod", 6 + N_FILL_HYENA + n))
        stream("out_0", [row_chunks(A["ab_w_out"][0], 4 * n) for n in range(2)]
               + [A["ab_w_out"][0, RET_V:RET_V + HW, :].rearrange("(p c) n -> p c n", c=4)], lambda n: ("out_0", 2 * NT - 1))
        stream("ada_1b", mods[18:], lambda n: ("mod", 18 + n))
        stream("da", [columns(da_in, 512 * c) for c in (2, 3, 4, 5, 0, 1)],
               lambda n: (("da_qk", 6), ("da_qk", 7), ("da_v", 3), ("da_v", 7), ("da_qk", 10), ("da_qk", 11))[n])
        stream("out_1", [row_chunks(A["da_w_out"][0], 4 * n) for n in range(2)], lambda n: ("out_1", 3))
        DA_ITEM = {2: 0, 3: 1, 4: 2, 5: 3, 0: 4, 1: 5}

        def dense_slot(n, width):
            return WS[:, n % DENSE_SLOTS, :].rearrange("p (c n) -> p c n", n=width)

        dense_in = [sem(f"dense_in_{i}") for i in range(DENSE_SLOTS)]

        def wait_dense(pe, n):
            pe.wait_ge(dense_in[n % DENSE_SLOTS], 16 * (n // DENSE_SLOTS + 1))

        LT = {0: (0, NT), 1: (2, 2)}

        start_in, filter_in, token_in = sem("start_in"), sem("filter_in"), sem("token_in")
        conv_in, ret_in, da_in_sem, moe_in, mod_in = (sem(x) for x in ("conv_in", "ret_in", "da_in", "moe_in", "mod_in"))
        diag_ready = sem("diag_ready")
        final_in = sem("final_in")
        dve_step = sem("dve_step")
        c_silu, filt_arg, filt_sin, filt_taps = sem("c_silu"), sem("filt_arg"), sem("filt_sin"), sem("filt_taps")
        mod_rows = sem("mod_rows")
        squares, variance, deviation, rows = sem("squares"), sem("variance"), sem("deviation"), sem("rows")
        conv_done, conv_edges, spec_done = sem("conv_done"), sem("conv_edges"), sem("spec_done")
        decay_arg, decay_exp, decay_used = sem("decay_arg"), sem("decay_exp"), sem("decay_used")
        ret_var, ret_dev, ret_rows = sem("ret_var"), sem("ret_dev"), sem("ret_rows")
        residual = sem("residual")
        lam_sums, lam_exp = sem("lam_sums"), sem("lam_exp")
        score_max, probs_mixed = sem("score_max"), sem("probs_mixed")
        o_var, o_dev, o_rows = sem("o_var"), sem("o_dev"), sem("o_rows")
        rows_out = [sem(f"rows_out_{i}") for i in range(2)]
        picks, id_weights = sem("picks"), sem("id_weights")
        hot, hot_used, flag_ready, slot_table = sem("hot"), sem("hot_used"), sem("flag_ready"), sem("slot_table")
        sh_silu = sem("sh_silu")
        result_out = sem("result_out")
        combine_in = [sem(f"combine_in_{i}") for i in range(3)]
        combine_used = sem("combine_used")
        result = sem("result")
        E = {}
        for l in range(DEPTH):
            for nme in ("xT_full", "xT_read", "gu_full", "sg_done", "act_done", "aT_full",
                        "aT_read", "y_full", "y_read_a", "y_read_d", "gidx", "empty"):
                E[nme, l] = sem(f"{nme}_{l}")
            for i in range(XG):
                E["xg_in", l, i] = sem(f"xg_in_{i}_{l}")
            for i in range(YB):
                E["stored", l, i] = sem(f"stored_{i}_{l}")
            for i in range(EXPERT_SLOTS):
                E["gu_in", l, i] = sem(f"gu_in_{i}_{l}")
                E["dn_in", l, i] = sem(f"dn_in_{i}_{l}")

        def at_least(eng, s, v):
            if not isinstance(v, int) or v > 0:
                eng.wait_ge(s, v)

        block = ctx.enter_context(nc.Block())

        ROWS_BEFORE = {"0a": 0, "0b": NT, "1a": 2 * NT, "1b": 3 * NT, "final": 3 * NT + 2}
        RESIDUALS_BEFORE = {"0b": 0, "1a": NT, "1b": 2 * NT, "final": 2 * NT + 2}
        NORM_TILES = {"0a": (0, NT), "0b": (0, NT), "1a": (0, NT), "1b": (2, 2), "final": (2, 2)}
        hrow_first = catH.rearrange("p a n -> p (a n)").rearrange("p (a n) -> p a n", a=2)
        HROW = {"0a": hrow_first, "0b": hrow_moe, "1a": hrow_da, "1b": hrow_moe, "final": hrow_da}

        def y_block(e, b=0):
            v = y_rows.rearrange("(n p) d -> n p d", p=P)
            if isinstance(e, int):
                return v[b * NE + e]
            return v[bass.ds(e + b * NE, 1)].rearrange("a p d -> (a p) d")

        o_squares = qk_da.rearrange("p a (b c) -> p (a b) c", c=P)

        M = {}
        for l in range(DEPTH):
            for nme in ("step", "in", "pe", "act", "dve", "xg", "out"):
                M[nme, l] = sem(f"more_{nme}_{l}")

        @contextmanager
        def overflow(eng, l):
            eng.wait_ge(flag_ready, l + 1)
            more = eng.value_load(flags[0:1, l:l + 1], min_val=0, max_val=1)
            with eng.If(more > 0):
                yield

        @block.sync
        def _(sp):
            def load_dense(name):
                n0 = first[name]
                n1 = min([first[x] for x in first if first[x] > n0], default=len(dense))
                for n in range(n0, n1):
                    if n >= DENSE_SLOTS:
                        ring.wait_full(sp, *dense[n - DENSE_SLOTS][1])
                    src = dense[n][0]
                    sp.dma_start(dense_slot(n, src.shape[2]), src).then_inc(dense_in[n % DENSE_SLOTS], 16)

            def expert_rows(w, l, e):
                v = w[l, e] if isinstance(e, int) else w[l, bass.ds(e, 1)].rearrange("a d n -> (a d) n")
                return v.rearrange("(p c) n -> p (c n)", p=P)

            def load_expert(l, u, gate, up, down):
                dst = WS[:, u, :].rearrange("p (a n) -> p a n", a=2)
                sp.dma_start(dst[:, 0, :], gate).then_inc(E["gu_in", l, u], 16)
                sp.dma_start(dst[:, 1, :], up).then_inc(E["gu_in", l, u], 16)
                sp.dma_start(DN[:, u, :], down).then_inc(E["dn_in", l, u], 16)

            def routed(l, item, u):
                e = item - 1
                load_expert(l, u, expert_rows(A["exp_w_gate"], l, e), expert_rows(A["exp_w_up"], l, e),
                            expert_rows(A["exp_w_down"], l, e))

            def load_experts(l):
                whole = lambda w: w[l].rearrange("(p c) n -> p (c n)", p=P)
                load_expert(l, 0, whole(A["sh_w_gate"]), whole(A["sh_w_up"]), whole(A["sh_w_down"]))
                for item in range(1, EXPERT_SLOTS):
                    routed(l, item, item)
                ring.wait_full(sp, f"sh_y_{l}", 2 * LT[l][1] - 1)
                for u in range(EXPERT_SLOTS):
                    if u:
                        sp.wait_ge(E["y_full", l], u)
                    routed(l, EXPERT_SLOTS + u, u)
                with sp.Fori(2, NE // EXPERT_SLOTS) as i:
                    for u in range(EXPERT_SLOTS):
                        sp.wait_ge(E["y_full", l], i * EXPERT_SLOTS + (u - EXPERT_SLOTS))
                        routed(l, i * EXPERT_SLOTS + u, u)
                sp.wait_ge(E["y_full", l], NE - EXPERT_SLOTS)
                routed(l, NE, 0)

            def overflow_sp(l):
                def load_more(e):
                    dst = WS[:, 0, :].rearrange("p (a n) -> p a n", a=2)
                    sp.dma_start(dst[:, 0, :], expert_rows(A["exp_w_gate"], l, e)).then_inc(M["in", l], 16)
                    sp.dma_start(dst[:, 1, :], expert_rows(A["exp_w_up"], l, e)).then_inc(M["in", l], 16)
                    sp.dma_start(DN[:, 0, :], expert_rows(A["exp_w_down"], l, e)).then_inc(M["in", l], 16)

                with overflow(sp, l):
                    load_more(0)
                    with sp.Fori(1, NE) as e:
                        sp.wait_ge(M["pe", l], e * (5 * (LT[l][1] - 1)))
                        load_more(e)
                    sp.wait_ge(M["pe", l], NE * 5 * (LT[l][1] - 1))

            for dst, src in start_loads:
                sp.dma_start(dst, src).then_inc(start_in, 16)
            for name in ("ada_0a", "u", "fill_hyena", "qk", "vg", "fill_ret", "out_0"):
                load_dense(name)
            ring.wait_full(sp, "out_0", 2 * NT - 1)
            load_experts(0)
            sp.wait_ge(E["y_full", 0], NE)
            overflow_sp(0)
            for name in ("ada_1b", "da", "out_1"):
                load_dense(name)
            ring.wait_full(sp, "out_1", 3)
            load_experts(1)
            sp.wait_ge(E["y_full", 1], NE)
            overflow_sp(1)
            for t in range(2):
                sp.wait_ge(result, t + 1)
                sp.dma_start(out[0, t * P:(t + 1) * P, :], hrow_da[:, t, :]).then_inc(result_out, 16)
            sp.wait_ge(result_out, 32)

        @block.tensor
        def _(pe):
            def products(dst, pairs, signal):
                last = len(pairs) - 1
                for i, (l, r) in enumerate(pairs):
                    mm = nc.tensor.matmul(dst, l, r, start=(i == 0), stop=(i == last))
                if signal is not None:
                    mm.then_inc(signal, 1)

            def turns(dst, srcs, signal):
                for i, v in enumerate(srcs):
                    tr = nc.tensor.transpose(dst[:, i * P:(i + 1) * P], v, ident)
                tr.then_inc(signal, 1)

            def use(stage, k):
                ring.claim(pe, stage, k)
                return bank(stage, k), ring.full(stage, k)

            def mod_work(steps):
                for what, g in steps:
                    b, full = use(what, g)
                    if what == "mod":
                        groups = ((0, "ada_0a"), (6, "fill_hyena"), (6 + N_FILL_HYENA, "fill_ret"), (18, "ada_1b"))
                        at, name = max(x for x in groups if x[0] <= g)
                        item = first[name] + g - at
                        wait_dense(pe, item)
                        w = dense_slot(item, 512)
                        products(b[0:2, :], [(csilu[:, :, c], w[:, c, :]) for c in range(KC)], full)
                        continue
                    ring.wait_read(pe, "mod", g)
                    for q in range(4):
                        tr = nc.tensor.transpose(b[:, 2 * q:2 * q + 2], mod_row[0:2, g % 2, q * P:(q + 1) * P],
                                                 ident[0:2, 0:2])
                    tr.then_inc(full, 1)

            filled = [6]

            def fill(count):
                filled[0] += count
                mod_work(mod_steps(filled[0] - count, count))

            def bcast(tag):
                for k in range(len(bcast_uses(tag))):
                    pe.wait_ge(diag_ready, bcasts_before(tag) + k + 1)
                    b, full = use(f"bcast_{tag}", k)
                    products(b, [(ones, diag[:, k % 2].rearrange("p a b -> p (a b)"))], full)

            def norm(tag, j):
                pe.wait_ge(rows, ROWS_BEFORE[tag] + j + 1)
                for half in range(2):
                    b, full = use(f"norm_{tag}", 2 * j + half)
                    turns(b, [HROW[tag][:, j % 2, (4 * half + i) * P:(4 * half + i + 1) * P] for i in range(4)], full)

            def all_norm_read(tag):
                for k in range(2 * NORM_TILES[tag][1]):
                    ring.wait_read(pe, f"norm_{tag}", k)

            def tile_cols(t):
                return slice(t * P, (t + 1) * P)

            def project(stage, k, n, t):
                w = dense_slot(n, 512)
                b, full = use(stage, k)
                products(b, [(hT[:, c, tile_cols(t)], w[:, c, :]) for c in range(KC)], full)

            def filter_layer(stage, weights, x):
                b, full = use(stage, 0)
                products(b[0:HY_FFN, 0:SEQ], [(weights, x)], full)

            def first_mods_and_filters():
                a, b, c = FIRST_MODS
                mod_work(a)
                pe.wait_ge(filter_in, 16 * len(filter_loads))
                filter_layer("filter_a", fw1, fz)
                mod_work(b)
                pe.wait_ge(filt_sin, 1)
                filter_layer("filter_b", fw2, fh[:, 0, :])
                mod_work(c)
                pe.wait_ge(mod_in, 16 * len(mod_loads))
                b, full = use("mod_consts", 0)
                turns(b, [mod_rows_in], full)
                norm("0a", 0)
                norm("0a", 1)
                pe.wait_ge(filt_sin, 2)
                for t in range(2):
                    for n in range(4):
                        b, full = use("filter_c", 4 * t + n)
                        products(b, [(fh[:, 1, tile_cols(t)], fw3[:, n * HW:(n + 1) * HW])], full)

            def filter_transforms():
                pe.wait_ge(filt_taps, 1)
                for o in range(2):
                    for m in range(5):
                        g = (0, 1, 4, 3, 5)[m]
                        b, full = use("filter_dft", 5 * o + m)
                        taps = fdiff[:, :, o] if m in (2, 3) else filt[:, :, 2 * o]
                        products(b, [(dftf[:, t, g * P:(g + 1) * P], taps[:, t]) for t in range(2)], full)

            def u_turn(m):
                pe.wait_ge(conv_done, m + 1)
                b, full = use("u_turn", m)
                turns(b, [uconv[:, m % 2, tile_cols(t)] for t in range(NT)], full)

            def hyena():
                for m in range(12):
                    n = first["u"] + m // 4
                    wait_dense(pe, n)
                    w = dense_slot(n, 512)
                    b, full = use("u_proj", m)
                    w = w.rearrange("p c (q m) -> p c q m", m=4)[:, :, :, m % 4]
                    products(b, [(w[:, c, :], hT[:, c, :]) for c in range(KC)], full)
                    if 1 <= m <= 8:
                        u_turn(m - 1)
                for k in range(8):
                    ring.wait_read(pe, "u_turn", k)
                for o in range(2):
                    for s in range(2):
                        if o:
                            for m in range(2):
                                ring.wait_read(pe, "idft_0", 2 * s + m)
                        for m in range(4):
                            b, full = use(f"dft_{o}", 4 * s + m)
                            products(b, [(dftf[:, t, m * P:(m + 1) * P], vtok[:, 2 * s + t, :])
                                         for t in range(2)], full)
                        fill(FILL_HYENA[o][s])
                        pe.wait_ge(spec_done, 2 * o + s + 1)
                        for m in range((2, 4)[o]):
                            b, full = use(f"idft_{o}", (2, 4)[o] * s + m)
                            if o == 0:
                                products(b, [(dfti[:, f, m * P:(m + 1) * P], specY[:, f, :])
                                             for f in range(4)], full)
                            else:
                                by_chunk = specY.rearrange("p f (q m) -> p f q m", m=4)[:, :, :, m]
                                products(b[:, 0:SEQ], [(by_chunk[:, f, :], dfti[:, f, :])
                                                       for f in range(4)], full)

            def qk_turn(stage, source, n):
                ring.wait_read(pe, "qk_proj" if stage == "qk_turn" else "da_qk", n)
                b, full = use(stage, n)
                turns(b, [source[:, n % 2, i * P:(i + 1) * P] for i in range(4)], full)

            def retention():
                for n in range(2 * NT):
                    wait_dense(pe, first["qk"] + n // NT)
                    project("qk_proj", n, first["qk"] + n // NT, n % NT)
                    if n:
                        qk_turn("qk_turn", qk_tok, n - 1)
                qk_turn("qk_turn", qk_tok, 2 * NT - 1)
                for n in range(4 * NT):
                    wait_dense(pe, first["vg"] + n // NT)
                    project("vg_proj", n, first["vg"] + n // NT, n % NT)
                for n in range(2 * NT):
                    ring.wait_read(pe, "qk_turn", n)
                for n in range(4 * NT):
                    ring.wait_read(pe, "vg_proj", n)
                for h in range(RET_HEADS):
                    for kt in range(4):
                        b, full = use("ret_s", 4 * h + kt)
                        if kt < 2:
                            products(b, [(kT[:, h, tile_cols(kt)], qT[:, h, :])], full)
                        else:
                            products(b[:, 0:SEQ], [(kT[:, h, tile_cols(kt)], qT[:, h, CTX:])], full)
                    fill(FILL_RET[h][0])
                    for kt in range(4):
                        ring.wait_read(pe, "ret_s", 4 * h + kt)
                    for t in range(NT):
                        b, full = use("ret_o", NT * h + t)
                        pairs = [(sT0[:, kt, tile_cols(t)], v_tok[:, kt, h * RET_DV:(h + 1) * RET_DV])
                                 for kt in range(2)]
                        if t >= 2:
                            pairs += [(sT2[:, kt, tile_cols(t - 2)], v_tok[:, 2 + kt, h * RET_DV:(h + 1) * RET_DV])
                                      for kt in range(2)]
                        products(b[:, 0:RET_DV], pairs, full)
                    fill(FILL_RET[h][1])
                    for t in range(NT):
                        pe.wait_ge(ret_rows, NT * h + t + 1)
                        b, full = use("ret_turn", NT * h + t)
                        turns(b, [ret_row[:, t % 2, i * P:(i + 1) * P] for i in range(2)], full)

            def out_projection(layer):
                stage, n0 = f"out_{layer}", first[f"out_{layer}"]
                chunks = 12 if layer == 0 else KC
                for n in range(chunks // 4):
                    wait_dense(pe, n0 + n)
                for t in range(NT if layer == 0 else 2):
                    for half in range(2):
                        b, full = use(stage, 2 * t + half)
                        pairs = []
                        for c in range(chunks):
                            if layer == 0:
                                left = catR[:, c, tile_cols(t)] if c < 8 else catH[:, c - 8, tile_cols(t)]
                            else:
                                left = oT[:, c, tile_cols(t)]
                            w = dense_slot(n0 + c // 4, D)[:, c % 4, half * 512:(half + 1) * 512]
                            pairs.append((left, w))
                        products(b, pairs, full)
                    if layer == 0 and t:
                        norm("0b", t - 1)

            def attention():
                for what, n in DA_STEPS:
                    if what == "norm":
                        norm("1a", n)
                        continue
                    if what == "turn":
                        qk_turn("da_turn", qk_da, n)
                        continue
                    c, t = DA_USES[n] if what == "qk" else (4 + n // NT, n % NT)
                    for half in range(2):
                        ring.wait_read(pe, "norm_1a", 2 * t + half)
                    item = first["da"] + DA_ITEM[c]
                    wait_dense(pe, item)
                    project("da_" + what, n, item, t)
                bcast("1a")
                bcast("1b")
                for n in range(len(DA_USES)):
                    ring.wait_read(pe, "da_turn", n)
                for n in range(2 * NT):
                    ring.wait_read(pe, "da_v", n)
                for n in range(2 * DA_HEADS + LAG):
                    m = n - LAG
                    if m >= 0:
                        pe.wait_ge(probs_mixed, m + 1)
                        b, full = use("da_at", m)
                        turns(b, [adiff[:, m % 2, tile_cols(kt)] for kt in range(NT)], full)
                    if n < 2 * DA_HEADS:
                        qt, h = n // DA_HEADS, n % DA_HEADS
                        for c in range(2):
                            b, full = use("da_s", 2 * n + c)
                            half = slice(c * DA_HD, (c + 1) * DA_HD)
                            products(b, [(qTd[half, h, tile_cols(qt)], kTd[half, h, :])], full)
                    if m >= 0:
                        ring.wait_read(pe, "da_at", m)
                        b, full = use("da_o", m)
                        h = m % DA_HEADS
                        products(b[:, 0:P], [(aT[:, 0, tile_cols(kt)], v_da[:, kt, h * P:(h + 1) * P])
                                             for kt in range(NT)], full)
                for qt in range(2):
                    pe.wait_ge(o_rows, qt + 1)
                    for half in range(2):
                        b, full = use("da_ot", 2 * qt + half)
                        turns(b, [o_tok[:, qt, (4 * half + i) * P:(4 * half + i + 1) * P] for i in range(4)], full)
                for k in range(4):
                    ring.wait_read(pe, "da_ot", k)

            def gate_up(dst, left, u, signal):
                w = WS[:, u, :].rearrange("p (a c n) -> p a c n", a=2, c=KC)
                products(dst, [(left(c), w[:, :, c, :]) for c in range(KC)], signal)

            def turn_act(dst, i, signal):
                turns(dst, [act[:, i, c * P:(c + 1) * P] for c in range(2)], signal)

            def down(dst, half, i, u, signal):
                w = DN[:, u, :].rearrange("p (c n) -> p c n", c=2)
                products(dst, [(actT[:, i, c * P:(c + 1) * P], w[:, c, half * 512:(half + 1) * 512])
                               for c in range(2)], signal)

            def route(l):
                t0, tiles = LT[l]
                router_w = router_w2[:, l]
                for k in range(tiles):
                    b, full = use(f"route_{l}", k)
                    products(b[:, 0:NE], [(hT[:, c, tile_cols(t0 + k)], router_w[:, c, :]) for c in range(KC)], full)
                shared(l, [("gu", 0), ("gu", 1)])
                pe.wait_ge(picks, (0, NT)[l] + tiles)
                for k in range(tiles + 1):
                    b, full = use(f"pos_{l}", k)
                    pairs = [(ones, picked[:, t0 + t, :]) for t in range(k)]
                    if k < tiles:
                        pairs.append((earlier, picked[:, t0 + k, :]))
                    products(b[:, 0:NE], pairs, full)

            def shared(l, steps):
                t0 = LT[l][0]
                for what, t in steps:
                    if what == "gu":
                        if t == 0:
                            pe.wait_ge(E["gu_in", l, 0], 32)
                        b, full = use(f"sh_gu_{l}", t)
                        gate_up(b, lambda c: hT[:, c, tile_cols(t0 + t)], 0, full)
                        continue
                    if t == 0:
                        pe.wait_ge(E["dn_in", l, 0], 16)
                    ring.wait_read(pe, f"sh_gu_{l}", t)
                    b, full = use(f"sh_t_{l}", t)
                    turn_act(b, t % 2, full)
                    ring.wait_read(pe, f"sh_t_{l}", t)
                    for half in range(2):
                        b, full = use(f"sh_y_{l}", 2 * t + half)
                        down(b, half, t % 2, 0, full)

            def slot_table_of(l, e, u, dst, signal):
                t0, tiles = LT[l]
                pe.wait_ge(hot, e + (1 + NE * l))
                for t in range(tiles):
                    one = slice(e, e + 1) if isinstance(e, int) else bass.ds(e, 1)
                    mm = nc.tensor.matmul(dst, one_hot[:, u, t, :],
                                          idw[:, t0 + t, one, :].rearrange("p a b -> p (a b)"),
                                          start=(t == 0), stop=(t == tiles - 1))
                mm.then_inc(signal, 1)

            def first_tables(l):
                t0, tiles = LT[l]
                pe.wait_ge(id_weights, (0, NT)[l] + tiles)
                for e in range(TABLES_FIRST):
                    b, full = use(f"table_{l}", e)
                    slot_table_of(l, e, e % 2, b[:, 0:TAB], full)

            def experts(l):
                def turn_tokens(e, u, gathered):
                    pe.wait_ge(E["xg_in", l, u], gathered * 16)
                    at_least(pe, E["xT_read", l], e)
                    for c in range(KC):
                        tr = nc.tensor.transpose(ps[:, c // 4, (c % 4) * P:(c % 4 + 1) * P],
                                                 xg[:, u, c * P:(c + 1) * P], ident)
                    tr.then_inc(E["xT_full", l], 1)

                def down_of(e, i, u, item_count):
                    pe.wait_ge(E["aT_read", l], e + 1)
                    at_least(pe, E["y_read_a", l], e)
                    at_least(pe, E["y_read_d", l], e)
                    pe.wait_ge(E["dn_in", l, u], item_count * 16)
                    for half in range(2):
                        down(ps[:, 5 + half, :], half, i, u, E["y_full", l] if half else None)

                def step(e, r, i4, has_next=True):
                    u, i = r % 4, (r - 1) % 2
                    count = i4 + 1 + (1 if r == 4 else 0)
                    pe.wait_ge(E["xT_read", l], e + 1)
                    pe.wait_ge(E["gu_in", l, u], count * 32)
                    at_least(pe, E["act_done", l], e - 1)
                    gate_up(ps[:, 2 + i, :], lambda c: xgT[:, i, c * P:(c + 1) * P], u, E["gu_full", l])
                    if has_next:
                        turn_tokens(e + 1, r % XG, i4 + (1 + r // XG))
                    if not isinstance(e, int) or e < NE - TABLES_FIRST:
                        x = e + TABLES_FIRST
                        pe.wait_ge(slot_table, x + NE * l)
                        slot_table_of(l, x, (r - 1 + TABLES_FIRST) % 2, ps[:, 7, 0:TAB], hot_used)
                    if not isinstance(e, int) or e > 0:
                        down_of(e - 1, 1 - i, (r - 1) % 4, i4 + 1)
                    pe.wait_ge(E["act_done", l], e + 1)
                    turn_act(ps[:, 4, :], i, E["aT_full", l])

                turn_tokens(0, 0, 1)
                for r in range(1, 5):
                    step(r - 1, r, 0)
                with pe.Fori(1, NE // 4 - 2) as i4:
                    for r in range(1, 5):
                        step(i4 * 4 + (r - 1), r, i4)
                for i4 in range(NE // 4 - 2, NE // 4):
                    for r in range(1, 5):
                        step(i4 * 4 + r - 1, r, i4, has_next=(i4 * 4 + r < NE))
                down_of(NE - 1, 1, 0, NE // 4 + 1)
                pe.wait_ge(E["y_read_a", l], NE)
                pe.wait_ge(E["y_read_d", l], NE)

            def overflow_pe(l):
                t0, tiles = LT[l]
                nb = tiles - 1
                with overflow(pe, l), pe.Fori(0, NE) as e:
                    for b in range(nb):
                        n = e * nb + b
                        pe.wait_ge(M["dve", l], n * 4 + 1)
                        for t in range(tiles):
                            mm = nc.tensor.matmul(ps[:, 7, 0:TAB], one_hot[:, 0, t, :],
                                                  idw[:, t0 + t, bass.ds(e, 1), :].rearrange("p a b -> p (a b)"),
                                                  start=(t == 0), stop=(t == tiles - 1))
                        mm.then_inc(M["pe", l], 1)
                        pe.wait_ge(M["xg", l], n * 16 + 16)
                        for c in range(KC):
                            tr = nc.tensor.transpose(ps[:, c // 4, (c % 4) * P:(c % 4 + 1) * P],
                                                     xg[:, 0, c * P:(c + 1) * P], ident)
                        tr.then_inc(M["pe", l], 1)
                        pe.wait_ge(M["act", l], n * 4 + 1)
                        pe.wait_ge(M["in", l], e * 48 + 48)
                        gate_up(ps[:, 2, :], lambda c: xgT[:, 0, c * P:(c + 1) * P], 0, M["pe", l])
                        pe.wait_ge(M["dve", l], n * 4 + 3)
                        turn_act(ps[:, 4, :], 0, M["pe", l])
                        pe.wait_ge(M["act", l], n * 4 + 3)
                        for half in range(2):
                            down(ps[:, 5 + half, :], half, 0, 0, M["pe", l] if half else None)
                with overflow(pe, l):
                    pe.wait_ge(M["act", l], NE * nb * 4)
                    pe.wait_ge(M["dve", l], NE * nb * 4)

            def layer_moe(l):
                route(l)
                tiles = LT[l][1]
                shared(l, [x for t in range(2) for x in (("y", t), ("gu", t + 2)) if x[1] < tiles])
                first_tables(l)
                shared(l, [("y", t) for t in range(2, tiles)])
                ring.fence(pe)
                experts(l)
                overflow_pe(l)

            pe.wait_ge(start_in, 16 * len(start_loads))
            pe.wait_ge(c_silu, 1)
            first_mods_and_filters()
            norm("0a", 2)
            norm("0a", 3)
            filter_transforms()
            pe.wait_ge(moe_in, 16 * len(moe_loads))
            bcast("0a")
            all_norm_read("0a")
            hyena()
            retention()
            bcast("0b")
            for n in range(4 * RET_HEADS):
                ring.wait_read(pe, "ret_turn", n)
            out_projection(0)
            norm("0b", NT - 1)
            bcast("0bg")
            all_norm_read("0b")
            layer_moe(0)
            mod_work(mod_steps(18, 6))
            attention()
            out_projection(1)
            for j in range(2):
                norm("1b", j)
            bcast("1bg")
            all_norm_read("1b")
            layer_moe(1)
            assert ring.claimed == len(ring.order)

        @block.scalar
        def _(act_e):
            A_ = nc.scalar.activation

            def load(items, s):
                for dst, src in items:
                    act_e.dma_start(dst, src).then_inc(s, 16)

            def norm_scale(tag, j):
                t = NORM_TILES[tag][0] + j
                if tag != "0a":
                    act_e.wait_ge(residual, RESIDUALS_BEFORE[tag] + j + 1)
                if j >= 2:
                    ring.wait_full(act_e, f"norm_{tag}", 2 * (j - 2) + 1)
                    if tag == "0b":
                        act_e.wait_ge(rows_out[j % 2], 16)
                A_(HROW[tag][:, j % 2, :], X[:, t, :], ACT.Square, accum_out=ssq[:, t:t + 1]).then_inc(squares, 1)
                act_e.wait_ge(variance, ROWS_BEFORE[tag] + j + 1)
                A_(rstd[:, t:t + 1], rstd[:, t:t + 1], ACT.Sqrt).then_inc(deviation, 1)

            def norm_turns(tag, j):
                t = NORM_TILES[tag][0] + j
                cols = slice(t * P, (t + 1) * P)
                if tag[1] == "a":
                    act_e.wait_ge(mod_rows, HALF[tag] + 1)
                    ring.wait_full(act_e, f"norm_{tag}", 2 * j)
                    b = bank(f"norm_{tag}", 2 * j)
                    for c in range(4):
                        m = [mod[:, HALF[tag], v, c, t // 2:t // 2 + 1] for v in range(2)]
                        ins = A_(hT[:, c, cols], b[:, c * P:(c + 1) * P], ACT.Identity, scale=m[1], bias=m[0])
                    ins.then_inc(ring.read(f"norm_{tag}", 2 * j), 1)
                    return
                for half in range(2):
                    evacuate(f"norm_{tag}", 2 * j + half, hT[:, 4 * half:4 * half + 4, cols], shape=4)

            def spread(tag):
                for k, (v, s, half) in enumerate(bcast_uses(tag)):
                    evacuate(f"bcast_{tag}", k, bc[:, s, v, half * 512:(half + 1) * 512])

            def mod_out(steps):
                for what, g in steps:
                    if what == "mod":
                        if g >= 2:
                            ring.wait_full(act_e, "modt", g - 2)
                        ring.wait_full(act_e, "mod", g)
                        A_(mod_row[0:2, g % 2, :], bank("mod", g)[0:2, :], ACT.Copy).then_inc(ring.read("mod", g), 1)
                        continue
                    tag, n = MODS[g]
                    evacuate("modt", g, mod[:, HALF[tag], n // 2, (n % 2) * 4:(n % 2) * 4 + 4, :], width=8, shape=4)

            filled = [6]

            def fill_out(count):
                filled[0] += count
                mod_out(mod_steps(filled[0] - count, count))

            def evacuate(stage, k, dst, width=512, func=ACT.Copy, shape=None, scale=1.0):
                ring.wait_full(act_e, stage, k)
                src = bank(stage, k)[:, 0:width]
                if shape:
                    src = src.rearrange("p (a b) -> p a b", a=shape)
                A_(dst, src, func, scale=scale).then_inc(ring.read(stage, k), 1)

            load(token_loads, token_in)
            act_e.wait_ge(start_in, 16 * len(start_loads))
            A_(csilu, cvec, ACT.Silu).then_inc(c_silu, 1)
            load(mod_loads, mod_in)
            act_e.wait_ge(token_in, 16 * len(token_loads))
            norm_scale("0a", 0)
            norm_scale("0a", 1)
            def filter_sine(n):
                act_e.wait_ge(filt_arg, n + 1)
                A_(fh[:, n, :], farg, ACT.Sin).then_inc(filt_sin, 1)

            steps = [x for part in FIRST_MODS for x in part]
            mod_out(steps[:5])
            filter_sine(0)
            mod_out(steps[5:9])
            filter_sine(1)
            mod_out(steps[9:])
            evacuate("mod_consts", 0, mod_consts, width=P)
            norm_turns("0a", 0)
            norm_scale("0a", 2)
            norm_turns("0a", 1)
            norm_scale("0a", 3)
            norm_turns("0a", 2)
            norm_turns("0a", 3)
            for k in range(10):
                evacuate("filter_dft", k, H[:, k // 5, k % 5, :])
            load(conv_loads, conv_in)
            spread("0a")

            act_e.wait_ge(conv_edges, 1)
            for m in range(12):
                if m >= 2:
                    act_e.wait_ge(conv_done, m - 1)
                evacuate("u_proj", m, upad[:, m % 2, :, 1:SEQ + 1], shape=2)
                if 1 <= m <= 8:
                    n = m - 1
                    dst = (vtok, x1tok)[n // 4].rearrange("p t (q m) -> p t q m", m=4)[:, :, :, n % 4]
                    evacuate("u_turn", n, dst, shape=NT)
            for o in range(2):
                for s in range(2):
                    fill_out(FILL_HYENA[o][s])
            for k in range(8):
                ring.wait_read(act_e, "idft_1", k)
            load(ret_loads, ret_in)
            for c in range(2):
                for t in range(NT):
                    n = c * NT + t
                    evacuate("qk_turn", n, (qT, kT)[c][:, :, t * P:(t + 1) * P], shape=RET_HEADS,
                             scale=(1.0, RET_DK ** -0.5)[c])
            for n in range(4 * NT):
                i, t = n // NT, n % NT
                dst = (v_tok, g_tok)[i // 2][:, t, (i % 2) * 512:(i % 2 + 1) * 512]
                evacuate("vg_proj", n, dst, func=ACT.Copy if i < 2 else ACT.Silu)
            act_e.wait_ge(decay_arg, 1)
            A_(lgt[:, 1, :], lgt[:, 1, :], ACT.Exp).then_inc(decay_exp, 1)
            act_e.wait_ge(decay_arg, 2)
            for h in range(RET_HEADS):
                f, b = slice(h, h + 1), slice(RET_HEADS + h, RET_HEADS + h + 1)
                at_least(act_e, decay_used, 2 * h)
                flat_ = lambda v: v.rearrange("p a n -> p (a n)")
                A_(decay_e[:, 0, :], flat_(dist_f), ACT.Exp, scale=lg[:, f])
                A_(decay_e[:, 1, :], flat_(dist_b), ACT.Exp, scale=lg[:, b]).then_inc(decay_exp, 1)
                act_e.wait_ge(decay_used, 2 * h + 1)
                A_(decay_e[:, 0, :], flat_(dist), ACT.Exp, scale=lg[:, f], bias=lg_ctx[:, f])
                A_(decay_e[:, 1, :], flat_(dist), ACT.Exp, scale=lg_neg[:, b], bias=lg_ctx[:, b]).then_inc(decay_exp, 1)
                fill_out(FILL_RET[h][0])
                for t in range(NT):
                    n = NT * h + t
                    act_e.wait_ge(ret_var, n + 1)
                    A_(ret_mv[:, t, 1:2], ret_mv[:, t, 1:2], ACT.Sqrt).then_inc(ret_dev, 1)
                fill_out(FILL_RET[h][1])
                for t in range(NT):
                    evacuate("ret_turn", NT * h + t, catR[:, 2 * h:2 * h + 2, t * P:(t + 1) * P], width=2 * P, shape=2)
            spread("0b")
            for j in range(NT):
                norm_scale("0b", j)
                if j:
                    norm_turns("0b", j - 1)
            norm_turns("0b", NT - 1)
            spread("0bg")

            def overflow_act(l):
                nb = LT[l][1] - 1
                with overflow(act_e, l):
                    for i in range(YB):
                        act_e.wait_ge(E["stored", l, i], NE // YB * 16)
                    with act_e.Fori(0, NE) as e:
                        for b in range(nb):
                            n = e * nb + b
                            act_e.wait_ge(M["pe", l], n * 5 + 2)
                            A_(xgT[:, 0, 0:512], ps[:, 0, :], ACT.Copy)
                            A_(xgT[:, 0, 512:], ps[:, 1, :], ACT.Copy).then_inc(M["act", l], 1)
                            act_e.wait_ge(M["pe", l], n * 5 + 3)
                            A_(gsil[:, 0, :], ps[:, 2, 0:ED], ACT.Silu).then_inc(M["act", l], 1)
                            act_e.wait_ge(M["pe", l], n * 5 + 4)
                            A_(actT[:, 0, :], ps[:, 4, 0:2 * P], ACT.Copy).then_inc(M["act", l], 1)
                            act_e.wait_ge(M["pe", l], n * 5 + 5)
                            A_(yb[:, 0, 0:512], ps[:, 5, :], ACT.Copy).then_inc(M["act", l], 1)
                            act_e.wait_ge(M["act", l], n * 4 + 4)
                            act_e.wait_ge(M["dve", l], n * 4 + 4)
                            act_e.dma_start(y_block(e, b + 1), yb[:, 0, :]).then_inc(M["out", l], 16)
                            act_e.wait_ge(M["out", l], n * 16 + 16)

            def experts_phase(l):
                t0, tiles = LT[l]
                for k in range(tiles):
                    evacuate(f"route_{l}", k, scores[:, t0 + k, :], width=NE, func=ACT.Sigmoid)

                def shared_silu(t):
                    ring.wait_full(act_e, f"sh_gu_{l}", t)
                    if t >= 2:
                        ring.wait_read(act_e, f"sh_gu_{l}", t - 2)
                    A_(gsil[:, t % 2, :], bank(f"sh_gu_{l}", t)[:, 0:ED], ACT.Silu).then_inc(sh_silu, 1)

                shared_silu(0)
                shared_silu(1)
                for t in range(tiles):
                    evacuate(f"sh_t_{l}", t, actT[:, t % 2, :], width=2 * P)
                    if t + 2 < tiles:
                        shared_silu(t + 2)

                def tokens_in(e, i):
                    act_e.wait_ge(E["xT_full", l], e + 1)
                    for half in range(2):
                        a = A_(xgT[:, i, half * 512:(half + 1) * 512], ps[:, half, :], ACT.Copy)
                    a.then_inc(E["xT_read", l], 1)

                def rows_out_half(e, u, stored):
                    act_e.wait_ge(E["y_full", l], e + 1)
                    at_least(act_e, E["stored", l, u], stored * 16)
                    A_(yb[:, u, 0:512], ps[:, 5, :], ACT.Copy).then_inc(E["y_read_a", l], 1)

                def store(e, u):
                    act_e.wait_ge(E["y_read_a", l], e + 1)
                    act_e.wait_ge(E["y_read_d", l], e + 1)
                    act_e.dma_start(y_block(e), yb[:, u, :]).then_inc(E["stored", l, u], 16)

                def step(e, i4, r, has_next=True):
                    i = r % 2
                    act_e.wait_ge(E["gu_full", l], e + 1)
                    at_least(act_e, E["act_done", l], e - 1)
                    A_(gsil[:, i, :], ps[:, 2 + i, 0:ED], ACT.Silu).then_inc(E["sg_done", l], 1)
                    if has_next:
                        tokens_in(e + 1, 1 - i)
                    behind = not isinstance(e, int) or e > 0
                    if behind:
                        rows_out_half(e - 1, (r - 1) % YB, i4)
                    act_e.wait_ge(E["aT_full", l], e + 1)
                    A_(actT[:, i, :], ps[:, 4, 0:2 * P], ACT.Copy).then_inc(E["aT_read", l], 1)
                    if behind:
                        store(e - 1, (r - 1) % YB)

                tokens_in(0, 0)
                step(0, -1, 4)
                for r in range(1, 5):
                    step(r, 0, r)
                with act_e.Fori(1, NE // 4 - 1) as i4:
                    for r in range(1, 5):
                        step(i4 * 4 + r, i4, r)
                for r in range(1, 4):
                    step(NE - 4 + r, NE // 4 - 1, r, has_next=(r < 3))
                rows_out_half(NE - 1, 3, NE // 4 - 1)
                store(NE - 1, 3)
                overflow_act(l)

            experts_phase(0)
            load(da_loads, da_in_sem)
            mod_out(mod_steps(18, 6))
            norm_scale("1a", 0)
            norm_turns("1a", 0)
            norm_scale("1a", 1)
            for what, n in DA_STEPS[1:]:
                if what == "norm":
                    norm_turns("1a", n)
                    if n + 1 < NT:
                        norm_scale("1a", n + 1)
                elif what == "turn":
                    c, t = DA_USES[n]
                    hs = slice((c % 2) * 4, (c % 2) * 4 + 4)
                    dst = qTd[:, hs, (t - 2) * P:(t - 1) * P] if c < 2 else kTd[:, hs, t * P:(t + 1) * P]
                    evacuate("da_turn", n, dst, shape=4)
                elif what == "v":
                    i, t = n // NT, n % NT
                    evacuate("da_v", n, v_da[:, t, i * 512:(i + 1) * 512])
            spread("1a")
            spread("1b")
            act_e.wait_ge(lam_sums, 1)
            A_(lamt[:, 0:2], lamt[:, 0:2], ACT.Exp).then_inc(lam_exp, 1)
            for n in range(2 * DA_HEADS + LAG):
                m = n - LAG
                if m >= 0:
                    if m:
                        ring.wait_full(act_e, "da_o", m - 1)
                    evacuate("da_at", m, aT[:, 0, :])
                if n < 2 * DA_HEADS:
                    act_e.wait_ge(score_max, n + 1)
                    if n >= 2:
                        act_e.wait_ge(probs_mixed, n - 1)
                    for c in range(2):
                        ring.wait_full(act_e, "da_s", 2 * n + c)
                        A_(prob[:, n % 2, c, :], bank("da_s", 2 * n + c), ACT.Exp, scale=DA_HD ** -0.5,
                           bias=smax[:, n % 2, c:c + 1], accum_out=ssum[:, n % 2, c:c + 1])\
                            .then_inc(ring.read("da_s", 2 * n + c), 1)
                if m >= 0:
                    evacuate("da_o", m, o_tok[:, m // DA_HEADS, (m % DA_HEADS) * P:(m % DA_HEADS + 1) * P], width=P)
            for qt in range(2):
                act_e.wait_ge(o_var, qt + 1)
                A_(ohs[:, qt, :], ohs[:, qt, :], ACT.Sqrt).then_inc(o_dev, 1)
            for k in range(4):
                qt, half = k // 2, k % 2
                evacuate("da_ot", k, oT[:, 4 * half:4 * half + 4, qt * P:(qt + 1) * P], shape=4)
            for j in range(2):
                norm_scale("1b", j)
            for j in range(2):
                norm_turns("1b", j)
            spread("1bg")
            experts_phase(1)
            act_e.dma_start(final_g, every(A["norm_final"])).then_inc(final_in, 16)
            for j in range(2):
                norm_scale("final", j)

        @block.vector
        def _(dve):
            V = nc.vector
            link = Chain(dve, dve_step)

            def filter_arg(stage, i):
                ring.wait_full(dve, stage, 0)
                V.tensor_scalar(farg, bank(stage, 0)[0:HY_FFN, 0:SEQ], fcol[:, 2 * i:2 * i + 1],
                                fcol[:, 2 * i + 1:2 * i + 2], ALU.add, ALU.mult).then_inc(ring.read(stage, 0), 1)
                ring.wait_read(dve, stage, 0)
                link(V.tensor_scalar(fturn, farg, 1.0 / TWO_PI, MAGIC, ALU.mult, ALU.add))
                link(V.tensor_scalar(fturn, fturn, MAGIC, None, ALU.subtract))
                for part in (PI_1, PI_2, PI_3):
                    link(V.scalar_tensor_tensor(out=farg, in0=fturn, scalar=-part, in1=farg, op0=ALU.mult, op1=ALU.add))
                V.tensor_scalar(farg, farg, PI_SAFE, -PI_SAFE, ALU.min, ALU.max).then_inc(filt_arg, 1)

            def finish_mods(tag):
                h = HALF[tag]
                for n in range(6):
                    ring.wait_read(dve, "modt", 6 * h + n)
                ring.wait_read(dve, "mod_consts", 0)
                v = mod[:, h].rearrange("p v c s -> p (v c) s")
                link(V.tensor_tensor(v, v, bias[:, h].rearrange("p v c -> p (v c)").unsqueeze(2)
                                     .broadcast_to([P, 3 * KC, 2]), ALU.add))
                V.scalar_tensor_tensor(out=mod[:, h, 1], in0=mod[:, h, 1], scalar=1.0,
                                       in1=norm_g[:, h, :].unsqueeze(2).broadcast_to([P, KC, 2]), op0=ALU.add,
                                       op1=ALU.mult).then_inc(mod_rows, 1)
                dve.wait_ge(mod_rows, h + 1)

            def diagonals(tag):
                h = BCAST[tag][0]
                for k, (v, s, half) in enumerate(bcast_uses(tag)):
                    at = bcasts_before(tag) + k
                    if at >= 2:
                        ring.wait_full(dve, *ALL_BCASTS[at - 2])
                    values = mod[:, h, v, 4 * half:4 * half + 4, s:s + 1].broadcast_to([P, 4, P])
                    V.tensor_tensor(diag[:, k % 2], ident.unsqueeze(1).broadcast_to([P, 4, P]), values,
                                    ALU.mult).then_inc(diag_ready, 1)

            def norm_inverse(tag, j):
                t = NORM_TILES[tag][0] + j
                dve.wait_ge(squares, ROWS_BEFORE[tag] + j + 1)
                V.tensor_scalar(rstd[:, t:t + 1], ssq[:, t:t + 1], 1.0 / D, EPS, ALU.mult,
                                ALU.add).then_inc(variance, 1)
                dve.wait_ge(deviation, ROWS_BEFORE[tag] + j + 1)
                link(V.reciprocal(rstd[:, t:t + 1], rstd[:, t:t + 1]))

            def norm_rows(tag, j):
                t = NORM_TILES[tag][0] + j
                norm_inverse(tag, j)
                h = HROW[tag][:, j % 2, :]
                if j >= 2:
                    ring.wait_full(dve, f"norm_{tag}", 2 * (j - 2) + 1)
                if tag[1] == "a":
                    V.tensor_scalar(h, X[:, t, :], rstd[:, t:t + 1], None, ALU.mult).then_inc(rows, 1)
                    return
                if j >= 2:
                    dve.wait_ge(rows_out[j % 2], 16)
                for k in range(len(bcast_uses(tag))):
                    ring.wait_read(dve, f"bcast_{tag}", k)
                h = h.rearrange("p (c q) -> p q c", c=KC)
                chunks = lambda v: v.rearrange("p (q c) -> p q c", c=KC)
                link(V.scalar_tensor_tensor(out=h, in0=chunks(X[:, t, :]), scalar=rstd[:, t:t + 1],
                                            in1=chunks(bc[:, t // 2, 1, :]), op0=ALU.mult, op1=ALU.mult))
                V.tensor_tensor(h, h, chunks(bc[:, t // 2, 0, :]), ALU.add).then_inc(rows, 1)

            def norm_turns(tag, j):
                ring.wait_full(dve, f"norm_{tag}", 2 * j + 1)
                b = bank(f"norm_{tag}", 2 * j + 1)
                for c in range(4):
                    m = [mod[:, HALF[tag], v, 4 + c, j // 2:j // 2 + 1] for v in range(2)]
                    ins = V.tensor_scalar(hT[:, 4 + c, j * P:(j + 1) * P], b[:, c * P:(c + 1) * P], m[1], m[0],
                                          ALU.mult, ALU.add)
                ins.then_inc(ring.read(f"norm_{tag}", 2 * j + 1), 1)

            def rotate(dst, src, tab, tmp, t, groups, half, signal):
                v = src.rearrange("p (g a d) -> p g a d", g=groups, a=2)
                w = dst.rearrange("p (g a d) -> p g a d", g=groups, a=2)
                tmp = tmp.rearrange("p (g d) -> p g d", g=groups)
                cos, sin = (tab[:, i, t, :].unsqueeze(1).broadcast_to([P, groups, half]) for i in range(2))
                V.tensor_tensor(w[:, :, 0, :], v[:, :, 0, :], cos, ALU.mult)
                link(V.tensor_tensor(tmp, v[:, :, 1, :], sin, ALU.mult))
                link(V.tensor_tensor(w[:, :, 0, :], w[:, :, 0, :], tmp, ALU.subtract))
                V.tensor_tensor(w[:, :, 1, :], v[:, :, 1, :], cos, ALU.mult)
                link(V.tensor_tensor(tmp, v[:, :, 0, :], sin, ALU.mult))
                V.tensor_tensor(w[:, :, 1, :], w[:, :, 1, :], tmp, ALU.add).then_inc(signal, 1)

            def add_residual(stage, k, t, half):
                ring.wait_full(dve, stage, k)
                cols = slice(half * 512, (half + 1) * 512)
                b = bank(stage, k)
                gated = (qk_tok if stage == "out_0" else qk_da)[:, k % 2, :]
                V.tensor_tensor(gated, b, bc[:, t // 2, 2, cols], ALU.mult).then_inc(ring.read(stage, k), 1)
                ring.wait_read(dve, stage, k)
                return V.tensor_tensor(X[:, t, cols], X[:, t, cols], gated, ALU.add)

            norm_rows("0a", 0)
            norm_rows("0a", 1)
            dve.wait_ge(filter_in, 16 * len(filter_loads))
            filter_arg("filter_a", 0)
            dve.wait_ge(filt_sin, 1)
            filter_arg("filter_b", 1)
            finish_mods("0a")
            norm_turns("0a", 0)
            norm_rows("0a", 2)
            norm_turns("0a", 1)
            norm_rows("0a", 3)
            for k in range(8):
                t, n = k // 4, k % 4
                ring.wait_full(dve, "filter_c", k)
                V.tensor_tensor(filt[:, t, n, :], bank("filter_c", k), window[:, t, :], ALU.mult)\
                    .then_inc(ring.read("filter_c", k), 1)
            norm_turns("0a", 2)
            norm_turns("0a", 3)
            for k in range(8):
                ring.wait_read(dve, "filter_c", k)
            for o in range(2):
                V.tensor_tensor(filt[0:1, 0, 2 * o, :], filt[0:1, 0, 2 * o, :], skiprow[:, o, :], ALU.add)
                ins = V.memset(filt[0:1, 0, 2 * o + 1, :], 0.0)
            link(ins)
            for t in range(2):
                v = filt[:, t].rearrange("p (o d) n -> p o d n", o=2)
                link(V.tensor_tensor(fdiff[:, t], v[:, :, 0, :], v[:, :, 1, :], ALU.subtract))
                ins = V.tensor_tensor(v[:, :, 0, :], v[:, :, 0, :], v[:, :, 1, :], ALU.add)
            ins.then_inc(filt_taps, 1)

            diagonals("0a")

            for k in range(10):
                ring.wait_full(dve, "filter_dft", k)
            V.memset(upad[:, :, :, 0:1], 0.0)
            V.memset(upad[:, :, :, SEQ + 1:SEQ + 2], 0.0).then_inc(conv_edges, 1)
            dve.wait_ge(conv_in, 16 * len(conv_loads))
            dve.wait_ge(conv_edges, 1)
            for m in range(12):
                ring.wait_read(dve, "u_proj", m)
                if 2 <= m < 8:
                    ring.wait_full(dve, "u_turn", m - 2)
                dst = (uconv[:, m % 2, :] if m < 8 else x2T[:, m - 8, :]).rearrange("p (a n) -> p a n", a=2)
                u = upad[:, m % 2]
                link(V.tensor_scalar(dst, u[:, :, 0:SEQ], cw[:, 0, m:m + 1], cb[:, m:m + 1], ALU.mult, ALU.add))
                link(V.scalar_tensor_tensor(out=dst, in0=u[:, :, 1:SEQ + 1], scalar=cw[:, 1, m:m + 1], in1=dst,
                                            op0=ALU.mult, op1=ALU.add))
                V.scalar_tensor_tensor(out=dst, in0=u[:, :, 2:SEQ + 2], scalar=cw[:, 2, m:m + 1], in1=dst,
                                       op0=ALU.mult, op1=ALU.add).then_inc(conv_done, 1)
            for k in range(8):
                ring.wait_read(dve, "u_turn", k)
            for k in range(10):
                ring.wait_read(dve, "filter_dft", k)
            dve.wait_ge(conv_done, 12)
            for o in range(2):
                for s in range(2):
                    if o or s:
                        for m in range((2, 4)[(2 * o + s - 1) // 2]):
                            oo, sp_ = (2 * o + s - 1) // 2, (2 * o + s - 1) % 2
                            ring.wait_full(dve, f"idft_{oo}", (2, 4)[oo] * sp_ + m)
                    st = f"dft_{o}"
                    for m in range(4):
                        ring.wait_full(dve, st, 4 * s + m)
                    for m in range(2):
                        ur, ui = bank(st, 4 * s + m), bank(st, 4 * s + 2 + m)
                        hr, hi = H[:, o, m, :], H[:, o, 2 + m, :]
                        hr_i = H[:, o, 4, :] if m == 0 else hr
                        V.tensor_tensor(specY[:, m, :], ur, hr, ALU.mult)
                        link(V.tensor_tensor(spec_t, ui, hi, ALU.mult))
                        link(V.tensor_tensor(specY[:, m, :], specY[:, m, :], spec_t, ALU.subtract))
                        V.tensor_tensor(specY[:, 2 + m, :], ur, hi, ALU.mult).then_inc(ring.read(st, 4 * s + m), 1)
                        V.tensor_tensor(spec_t, ui, hr_i, ALU.mult).then_inc(ring.read(st, 4 * s + 2 + m), 1)
                        ring.wait_read(dve, st, 4 * s + 2 + m)
                        ins = V.tensor_tensor(specY[:, 2 + m, :], specY[:, 2 + m, :], spec_t, ALU.add)
                        if m == 0:
                            link(ins)
                    ins.then_inc(spec_done, 1)
                    for m in range((2, 4)[o]):
                        k = (2, 4)[o] * s + m
                        ring.wait_full(dve, f"idft_{o}", k)
                        if o == 0:
                            V.tensor_tensor(vtok[:, 2 * s + m, :], bank("idft_0", k), x1tok[:, 2 * s + m, :],
                                            ALU.mult).then_inc(ring.read("idft_0", k), 1)
                        else:
                            cols = slice(s * SEQ, (s + 1) * SEQ)
                            V.tensor_tensor(catH[:, m, cols], bank("idft_1", k)[:, 0:SEQ], x2T[:, m, cols],
                                            ALU.mult).then_inc(ring.read("idft_1", k), 1)

            dve.wait_ge(ret_in, 16 * len(ret_loads))
            for n in range(2 * NT):
                t = n % NT
                ring.wait_full(dve, "qk_proj", n)
                if n >= 2:
                    ring.wait_full(dve, "qk_turn", n - 2)
                    ring.wait_read(dve, "qk_proj", n - 2)
                dst, src = qk_tok[:, n % 2, :], bank("qk_proj", n)
                if t < 2:
                    V.tensor_copy(dst, src).then_inc(ring.read("qk_proj", n), 1)
                else:
                    rotate(dst, src, rope_r, rope_t[:, n % 2, :], t - 2, RET_HEADS, RET_DK // 2, ring.read("qk_proj", n))
            x_, e_, z_, p_ = (lgt[:, i, :] for i in range(4))
            link(V.tensor_scalar(e_, x_, -1.0, None, ALU.mult))
            V.tensor_tensor(e_, e_, x_, ALU.min).then_inc(decay_arg, 1)
            dve.wait_ge(decay_exp, 1)
            link(V.tensor_scalar(z_, e_, 2.0, None, ALU.add))
            link(V.reciprocal(z_, z_))
            link(V.tensor_tensor(z_, z_, e_, ALU.mult))
            link(V.tensor_tensor(e_, z_, z_, ALU.mult))
            link(V.tensor_scalar(p_, e_, 1.0 / 17.0, 1.0 / 15.0, ALU.mult, ALU.add))
            for k in (13, 11, 9, 7, 5, 3, 1):
                link(V.tensor_tensor(p_, p_, e_, ALU.mult))
                link(V.tensor_scalar(p_, p_, 1.0 / k, None, ALU.add))
            link(V.tensor_tensor(p_, p_, z_, ALU.mult))
            link(V.tensor_scalar(lg, x_, 0.0, None, ALU.min))
            link(V.scalar_tensor_tensor(out=lg, in0=p_, scalar=-2.0, in1=lg, op0=ALU.mult, op1=ALU.add))
            link(V.tensor_scalar(lg_ctx, lg, float(CTX), None, ALU.mult))
            link(V.tensor_scalar(lg_neg, lg, -1.0, None, ALU.mult))
            link(V.tensor_scalar(dist_f, dist, 0.0, None, ALU.max))
            V.tensor_scalar(dist_b, dist, -1.0, 0.0, ALU.mult, ALU.max).then_inc(decay_arg, 1)
            flat2 = lambda v: v.rearrange("p a n -> p (a n)")
            for h in range(RET_HEADS):
                dve.wait_ge(decay_exp, 2 * h + 2)
                e0, e1 = (decay_e[:, i, :].rearrange("p (a n) -> p a n", a=2) for i in range(2))
                link(V.scalar_tensor_tensor(out=e0, in0=dist, scalar=0.0, in1=e0, op0=ALU.is_ge, op1=ALU.mult))
                link(V.scalar_tensor_tensor(out=e1, in0=dist, scalar=0.0, in1=e1, op0=ALU.is_le, op1=ALU.mult))
                V.tensor_tensor(decay[:, :, 0, :], e0, e1, ALU.add).then_inc(decay_used, 1)
                dve.wait_ge(decay_exp, 2 * h + 3)
                V.tensor_tensor(decay[:, :, 1, :], e0, e1, ALU.add).then_inc(decay_used, 1)
                dve.wait_ge(decay_used, 2 * h + 2)
                if h:
                    for t in range(NT):
                        ring.wait_full(dve, "ret_o", NT * (h - 1) + t)
                for kt in range(4):
                    ring.wait_full(dve, "ret_s", 4 * h + kt)
                    if kt < 2:
                        V.tensor_tensor(sT0[:, kt, :], bank("ret_s", 4 * h + kt),
                                        decay[:, kt].rearrange("p a n -> p (a n)"), ALU.mult)\
                            .then_inc(ring.read("ret_s", 4 * h + kt), 1)
                    else:
                        V.tensor_tensor(sT2[:, kt - 2, :], bank("ret_s", 4 * h + kt)[:, 0:SEQ], decay[:, kt - 2, 0, :],
                                        ALU.mult).then_inc(ring.read("ret_s", 4 * h + kt), 1)
                for t in range(NT):
                    n = NT * h + t
                    ring.wait_full(dve, "ret_o", n)
                    link(V.bn_stats(ret_stat[:, t, :], bank("ret_o", n)[:, 0:RET_DV]))
                    link(V.bn_aggr(ret_mv[:, t, :], ret_stat[:, t, :]))
                    V.tensor_scalar(ret_mv[:, t, 1:2], ret_mv[:, t, 1:2], EPS, None, ALU.add).then_inc(ret_var, 1)
                for t in range(NT):
                    n = NT * h + t
                    dve.wait_ge(ret_dev, n + 1)
                    link(V.reciprocal(ret_mv[:, t, 1:2], ret_mv[:, t, 1:2]))
                    if n >= 2:
                        ring.wait_full(dve, "ret_turn", n - 2)
                    r_ = ret_row[:, t % 2, :]
                    V.tensor_scalar(r_, bank("ret_o", n)[:, 0:RET_DV], ret_mv[:, t, 0:1], ret_mv[:, t, 1:2],
                                    ALU.subtract, ALU.mult).then_inc(ring.read("ret_o", n), 1)
                    ring.wait_read(dve, "ret_o", n)
                    V.tensor_tensor(r_, r_, g_tok[:, t, h * RET_DV:(h + 1) * RET_DV], ALU.mult).then_inc(ret_rows, 1)
            for tag in ("0b", "1a"):
                finish_mods(tag)
            diagonals("0b")
            for k in range(len(bcast_uses("0a"))):
                ring.wait_read(dve, "bcast_0a", k)
            for t in range(NT):
                for half in range(2):
                    ins = add_residual("out_0", 2 * t + half, t, half)
                ins.then_inc(residual, 1)
                norm_rows("0b", t)
            diagonals("0bg")

            def top8_mask(t, router_b):
                link(V.tensor_tensor(choice, scores[:, t, :], router_b, ALU.add))
                for g in range(NG):
                    ins = V.max(best[:, g, :], choice[:, g * 8:(g + 1) * 8])
                link(ins)
                link(V.tensor_tensor(gsum, best[:, :, 0], best[:, :, 1], ALU.add))
                link(V.max(gtop, gsum))
                link(V.max_index(gidx, gtop, gsum))
                link(V.tensor_copy(gidxf, gidx))
                link(V.tensor_tensor(geq, iota8, gidxf[:, 0:TOPG].unsqueeze(2).broadcast_to([P, TOPG, NG]), ALU.is_equal))
                link(V.tensor_reduce(gmask, geq.rearrange("p k g -> p g k"), AX_X, ALU.add))
                link(V.tensor_scalar(gneg, gmask, 1.0, BIG, ALU.subtract, ALU.mult))
                c3 = choice.rearrange("p (g n) -> p g n", g=NG)
                link(V.tensor_tensor(c3, c3, gmask.unsqueeze(2).broadcast_to([P, NG, NE // NG]), ALU.mult))
                link(V.tensor_tensor(c3, c3, gneg.unsqueeze(2).broadcast_to([P, NG, NE // NG]), ALU.add))
                link(V.max(gtop, choice))
                link(V.match_replace(replaced, gtop, choice, -3e38))
                return V.tensor_tensor(picked[:, t, :], replaced, choice, ALU.not_equal)

            def act_chunks(v):
                return v.rearrange("p (c q) -> p q c", c=2)

            def pairs_of(v):
                return v.rearrange("p (q c) -> p q c", c=2)

            def overflow_dve(l):
                t0, tiles = LT[l]
                nb = tiles - 1
                step = M["step", l]
                with overflow(dve, l):
                    with dve.Fori(0, NE) as e:
                        for b in range(nb):
                            n = e * nb + b
                            oh = one_hot[:, 0, 0:tiles, :]
                            pos = choice[:, 0:tiles].unsqueeze(2)
                            V.tensor_scalar(pos, pos1[:, t0:t0 + tiles, bass.ds(e, 1)], float(P * (b + 1)), None,
                                            ALU.subtract).then_inc(step, 1)
                            dve.wait_ge(step, n * 3 + 1)
                            V.tensor_tensor(oh, pos.broadcast_to([P, tiles, P]),
                                            iota1.unsqueeze(1).broadcast_to([P, tiles, P]),
                                            ALU.is_equal).then_inc(M["dve", l], 1)
                            dve.wait_ge(M["pe", l], n * 5 + 1)
                            V.tensor_reduce(slot_w[:, 0:1], ps[:, 7, 2:5], AX_X, ALU.add).then_inc(step, 1)
                            V.scalar_tensor_tensor(out=slot_empty[:, 0:1], in0=ps[:, 7, 5:6], scalar=0.0,
                                                   in1=place, op0=ALU.is_equal, op1=ALU.mult).then_inc(step, 1)
                            dve.wait_ge(step, n * 3 + 3)
                            V.scalar_tensor_tensor(out=gather_idx[:, 0, :], in0=ps[:, 7, 0:1], scalar=ps[:, 7, 1:2],
                                                   in1=slot_empty[:, 0:1], op0=ALU.add, op1=ALU.add)\
                                .then_inc(M["dve", l], 1)
                            dve.wait_ge(M["act", l], n * 4 + 2)
                            V.scalar_tensor_tensor(out=act_chunks(act[:, 0, :]), in0=pairs_of(ps[:, 2, ED:2 * ED]),
                                                   scalar=slot_w[:, 0:1], in1=pairs_of(gsil[:, 0, :]), op0=ALU.mult,
                                                   op1=ALU.mult).then_inc(M["dve", l], 1)
                            dve.wait_ge(M["pe", l], n * 5 + 5)
                            V.tensor_copy(yb[:, 0, 512:], ps[:, 6, :]).then_inc(M["dve", l], 1)
                            dve.wait_ge(M["out", l], n * 16 + 16)

            def experts_phase(l):
                t0, tiles = LT[l]
                before = (0, NT)[l]
                router_b = router_b2[:, l]

                def shared_act(t):
                    dve.wait_ge(sh_silu, before + t + 1)
                    if t >= 2:
                        ring.wait_full(dve, f"sh_t_{l}", t - 2)
                    V.tensor_tensor(act_chunks(act[:, t % 2, :]), pairs_of(bank(f"sh_gu_{l}", t)[:, ED:2 * ED]),
                                    pairs_of(gsil[:, t % 2, :]), ALU.mult).then_inc(ring.read(f"sh_gu_{l}", t), 1)

                def shared_rows(t):
                    for k in range(len(bcast_uses(f"{l}bg"))):
                        ring.wait_read(dve, f"bcast_{l}bg", k)
                    for half in range(2):
                        k = 2 * t + half
                        ring.wait_full(dve, f"sh_y_{l}", k)
                        cols = slice(half * 512, (half + 1) * 512)
                        tmp = mod_row[:, 0, :]
                        V.tensor_tensor(tmp, bank(f"sh_y_{l}", k), bc[:, (t0 + t) // 2, 2, cols], ALU.mult)\
                            .then_inc(ring.read(f"sh_y_{l}", k), 1)
                        ring.wait_read(dve, f"sh_y_{l}", k)
                        link(V.tensor_tensor(X[:, t0 + t, cols], X[:, t0 + t, cols], tmp, ALU.add))

                for k in range(tiles):
                    t = t0 + k
                    ring.wait_read(dve, f"route_{l}", k)
                    top8_mask(t, router_b).then_inc(picks, 1)
                    dve.wait_ge(picks, before + k + 1)
                shared_act(0)
                shared_act(1)
                for k in range(tiles + 1):
                    ring.wait_full(dve, f"pos_{l}", k)
                    b = bank(f"pos_{l}", k)[:, 0:NE]
                    if k < tiles:
                        V.scalar_tensor_tensor(out=pos1[:, t0 + k, :], in0=b, scalar=1.0, in1=picked[:, t0 + k, :],
                                               op0=ALU.add, op1=ALU.mult).then_inc(ring.read(f"pos_{l}", k), 1)
                        ring.wait_read(dve, f"pos_{l}", k)
                    else:
                        V.tensor_reduce(counts_max, b, AX_X, ALU.max).then_inc(ring.read(f"pos_{l}", k), 1)
                        ring.wait_read(dve, f"pos_{l}", k)
                        V.tensor_scalar(flags[:, l:l + 1], counts_max, P + 0.5, None, ALU.is_gt).then_inc(flag_ready, 1)

                def one_hot_of(e, u):
                    one = slice(e, e + 1) if isinstance(e, int) else bass.ds(e, 1)
                    V.tensor_tensor(one_hot[:, u, 0:tiles, :], pos1[:, t0:t0 + tiles, one].broadcast_to([P, tiles, P]),
                                    iota1.unsqueeze(1).broadcast_to([P, tiles, P]), ALU.is_equal).then_inc(hot, 1)

                def slots_of(e, u, where, free=None):
                    one = slice(e, e + 1) if isinstance(e, int) else bass.ds(e, 1)
                    if free is None:
                        V.tensor_reduce(slot_w[:, one], where[:, 2:5], AX_X, ALU.add)
                    V.scalar_tensor_tensor(out=slot_empty[:, u:u + 1], in0=where[:, 5:6], scalar=0.0, in1=place,
                                           op0=ALU.is_equal, op1=ALU.mult).then_inc(E["empty", l], 1)
                    dve.wait_ge(E["empty", l], e + 1)
                    V.scalar_tensor_tensor(out=slot_u[:, one], in0=where[:, 0:1], scalar=where[:, 1:2],
                                           in1=slot_empty[:, u:u + 1], op0=ALU.add, op1=ALU.add).then_inc(slot_table, 1)
                    if free is not None:
                        V.tensor_reduce(slot_w[:, one], where[:, 2:5], AX_X, ALU.add).then_inc(free, 1)

                for t in range(t0, t0 + tiles):
                    link(V.tensor_tensor_reduce(out=replaced, in0=scores[:, t, :], in1=picked[:, t, :], scale=1.0,
                                                scalar=0.0, op0=ALU.mult, op1=ALU.add, accum_out=wsum))
                    link(V.tensor_scalar(wsum, wsum, 1e-20, None, ALU.add))
                    link(V.reciprocal(wsum, wsum))
                    link(V.tensor_scalar(weight_left, replaced, wsum, ROUTED_SCALE, ALU.mult, ALU.mult))
                    for part in range(2, 5):
                        link(V.tensor_copy(idw[:, t, :, part], weight_left))
                        if part < 4:
                            link(V.tensor_tensor(weight_left, weight_left, idw[:, t, :, part], ALU.subtract))
                    V.memset(idw[:, t, :, 0], float(t * P))
                    V.memset(idw[:, t, :, 5], 1.0)
                    V.tensor_copy(idw[:, t, :, 1], place.broadcast_to([P, NE])).then_inc(id_weights, 1)
                one_hot_of(0, 0)
                for t in range(2):
                    shared_rows(t)
                    if t + 2 < tiles:
                        shared_act(t + 2)
                for e in range(TABLES_FIRST):
                    one_hot_of(e + 1, (e + 1) % 2)
                    ring.wait_full(dve, f"table_{l}", e)
                    slots_of(e, e % 2, bank(f"table_{l}", e), ring.read(f"table_{l}", e))
                    dve.wait_ge(slot_table, NE * l + e + 1)
                for t in range(2, tiles):
                    shared_rows(t)
                for k in range(tiles):
                    t = t0 + k
                    link(V.scalar_tensor_tensor(out=row_sum, in0=expert_no, scalar=float(P),
                                                in1=picked[:, t, :], op0=ALU.mult, op1=ALU.mult))
                    link(V.tensor_tensor(row_sum, row_sum, pos1[:, t, :], ALU.add))
                    for b in range(1, tiles):
                        link(V.tensor_scalar(choice, pos1[:, t, :], b * P + 0.5, float((NE - 1) * P), ALU.is_gt, ALU.mult))
                        link(V.tensor_tensor(row_sum, row_sum, choice, ALU.add))
                    link(V.max(row_best, row_sum))
                    link(V.tensor_scalar(combine_idx[:, t, :], row_best, 1.0, None, ALU.subtract))

                def rows_out_half(e, u, stored):
                    dve.wait_ge(E["y_full", l], e + 1)
                    at_least(dve, E["stored", l, u], stored * 16)
                    V.tensor_copy(yb[:, u, 512:], ps[:, 6, :]).then_inc(E["y_read_d", l], 1)

                def step(e, i4, r):
                    i = r % 2
                    dve.wait_ge(E["sg_done", l], e + 1)
                    at_least(dve, E["aT_full", l], e - 1)
                    w = slot_w[:, e:e + 1] if isinstance(e, int) else slot_w[:, bass.ds(e, 1)]
                    V.scalar_tensor_tensor(out=act_chunks(act[:, i, :]), in0=pairs_of(ps[:, 2 + i, ED:2 * ED]), scalar=w,
                                           in1=pairs_of(gsil[:, i, :]), op0=ALU.mult,
                                           op1=ALU.mult).then_inc(E["act_done", l], 1)
                    if not isinstance(e, int) or e > 0:
                        rows_out_half(e - 1, (r - 1) % YB, i4)
                    x = e + TABLES_FIRST
                    if not isinstance(e, int) or x < NE:
                        dve.wait_ge(hot_used, e + (1 + (NE - TABLES_FIRST) * l))
                        u = (r + TABLES_FIRST) % 2
                        slots_of(x, u, ps[:, 7, 0:TAB])
                    if not isinstance(e, int) or x + 1 < NE:
                        one_hot_of(x + 1, (r + TABLES_FIRST + 1) % 2)

                step(0, -1, 4)
                for r in range(1, 5):
                    step(r, 0, r)
                with dve.Fori(1, NE // 4 - 2) as i4:
                    for r in range(1, 5):
                        step(i4 * 4 + r, i4, r)
                for e in range(NE - 7, NE):
                    step(e, (e - 1) // 4, (e - 1) % 4 + 1)
                rows_out_half(NE - 1, 3, NE // 4 - 1)
                overflow_dve(l)

            def combine(l, k):
                t = LT[l][0] + k
                for g in range(4):
                    n = 4 * ((0, NT)[l] + k) + g
                    v = combined[n % 3]
                    dve.wait_ge(combine_in[n % 3], 32 * (n // 3 + 1))
                    if g == 0:
                        V.tensor_tensor(combine_sum, v[:, 0, :], v[:, 1, :], ALU.add).then_inc(combine_used, 1)
                    else:
                        link(V.tensor_tensor(v[:, 0, :], v[:, 0, :], v[:, 1, :], ALU.add))
                        V.tensor_tensor(combine_sum, v[:, 0, :], combine_sum, ALU.add).then_inc(combine_used, 1)
                    dve.wait_ge(combine_used, n + 1)
                link(V.tensor_tensor(combine_sum, combine_sum, bc[:, t // 2, 2, :], ALU.mult))
                V.tensor_tensor(X[:, t, :], X[:, t, :], combine_sum, ALU.add).then_inc(residual, 1)

            experts_phase(0)

            def qk_out(n):
                t = DA_USES[n][1]
                ring.wait_full(dve, "da_qk", n)
                if n >= 2:
                    ring.wait_full(dve, "da_turn", n - 2)
                    ring.wait_read(dve, "da_qk", n - 2)
                dst, src = qk_da[:, n % 2, :], bank("da_qk", n)
                if t < 2:
                    V.tensor_copy(dst, src).then_inc(ring.read("da_qk", n), 1)
                else:
                    rotate(dst, src, rope_d, rope_dt[:, n % 2, :], t - 2, 8, DA_HD // 2, ring.read("da_qk", n))

            combine(0, 0)
            norm_rows("1a", 0)
            norm_turns("1a", 0)
            dve.wait_ge(da_in_sem, 16 * len(da_loads))
            for k in range(1, NT):
                combine(0, k)
                norm_rows("1a", k)
                qk_out(2 * (k - 1))
                qk_out(2 * (k - 1) + 1)
                norm_turns("1a", k)
            for n in range(2 * (NT - 1), len(DA_USES)):
                qk_out(n)
            diagonals("1a")
            finish_mods("1b")
            diagonals("1b")
            for i in range(2):
                ins = V.tensor_tensor_reduce(out=lamv[:, 2 * i, :], in0=lamv[:, 2 * i, :], in1=lamv[:, 2 * i + 1, :],
                                             scale=1.0, scalar=0.0, op0=ALU.mult, op1=ALU.add,
                                             accum_out=lamt[:, i:i + 1])
            ins.then_inc(lam_sums, 1)
            dve.wait_ge(lam_exp, 1)
            link(V.tensor_tensor(lamt[:, 2:3], lamt[:, 1:2], lamt[:, 0:1], ALU.subtract))
            link(V.tensor_scalar(lamt[:, 2:3], lamt[:, 2:3], LAMBDA_INIT, None, ALU.subtract))
            sc = DA_HD ** -0.5

            def mix(n):
                i = n % 2
                for c in range(2):
                    ring.wait_read(dve, "da_s", 2 * n + c)
                link(V.reciprocal(sinv[:, i, :], ssum[:, i, :]))
                link(V.tensor_tensor(sinv[:, i, 1:2], sinv[:, i, 1:2], lamt[:, 2:3], ALU.mult))
                if n >= 2:
                    ring.wait_full(dve, "da_at", n - 2)
                link(V.tensor_scalar(adiff[:, i, :], prob[:, i, 0, :], sinv[:, i, 0:1], None, ALU.mult))
                V.scalar_tensor_tensor(out=adiff[:, i, :], in0=prob[:, i, 1, :], scalar=sinv[:, i, 1:2],
                                       in1=adiff[:, i, :], op0=ALU.mult, op1=ALU.add).then_inc(probs_mixed, 1)

            for n in range(2 * DA_HEADS + 1):
                if n < 2 * DA_HEADS:
                    i = n % 2
                    if n >= 2:
                        for c in range(2):
                            ring.wait_read(dve, "da_s", 2 * (n - 2) + c)
                    for c in range(2):
                        ring.wait_full(dve, "da_s", 2 * n + c)
                        ins = V.tensor_reduce(smax[:, i, c:c + 1], bank("da_s", 2 * n + c), AX_X, ALU.max)
                    link(ins)
                    V.tensor_scalar(smax[:, i, :], smax[:, i, :], -sc, None, ALU.mult).then_inc(score_max, 1)
                if n:
                    mix(n - 1)
            for qt in range(2):
                for m in range(DA_HEADS):
                    ring.wait_read(dve, "da_o", qt * DA_HEADS + m)
                o3 = o_tok[:, qt, :].rearrange("p (h d) -> p h d", h=DA_HEADS)
                link(V.tensor_tensor(o_squares, o3, o3, ALU.mult))
                link(V.tensor_reduce(ohs[:, qt, :], o_squares, AX_X, ALU.add))
                V.tensor_scalar(ohs[:, qt, :], ohs[:, qt, :], 1.0 / P, 1e-5, ALU.mult, ALU.add).then_inc(o_var, 1)
            link(V.tensor_scalar(subln, subln, 1.0 - LAMBDA_INIT, None, ALU.mult))
            for qt in range(2):
                dve.wait_ge(o_dev, qt + 1)
                o3 = o_tok[:, qt, :].rearrange("p (h d) -> p h d", h=DA_HEADS)
                link(V.reciprocal(ohs[:, qt, :], ohs[:, qt, :]))
                link(V.tensor_tensor(o3, o3, ohs[:, qt, :].unsqueeze(2).broadcast_to([P, DA_HEADS, P]), ALU.mult))
                V.tensor_tensor(o3, o3, subln.unsqueeze(1).broadcast_to([P, DA_HEADS, P]), ALU.mult).then_inc(o_rows, 1)
            for k in range(len(bcast_uses("1a"))):
                ring.wait_read(dve, "bcast_1a", k)
            for j in range(2):
                for half in range(2):
                    ins = add_residual("out_1", 2 * j + half, 2 + j, half)
                ins.then_inc(residual, 1)
                norm_rows("1b", j)
            diagonals("1bg")
            experts_phase(1)
            for j in range(2):
                combine(1, j)
                norm_inverse("final", j)
            dve.wait_ge(final_in, 16)
            for j in range(2):
                V.scalar_tensor_tensor(out=hrow_da[:, j, :], in0=X[:, 2 + j, :], scalar=rstd[:, 2 + j:3 + j],
                                       in1=final_g, op0=ALU.mult, op1=ALU.mult).then_inc(result, 1)

        @block.gpsimd
        def _(pool):
            def overflow_pool(l):
                nb = LT[l][1] - 1
                last_row = pool.alloc_register(f"more_last_row_{l}")
                with pool.Fori(0, NE) as e:
                    for b in range(nb):
                        n = e * nb + b
                        pool.wait_ge(M["dve", l], n * 4 + 2)
                        pool.reg_add(last_row, pool.zero_reg, NTOK - 1)
                        pool.indirect_dma_start(xg[:, 0, :], None, h_rows,
                                                bass.IndirectOffsetOnAxis(gather_idx[:, 0, :], 0),
                                                bounds_check=last_row).then_inc(M["xg", l], 16)
                        pool.wait_ge(M["xg", l], n * 16 + 16)
                pool.wait_ge(M["out", l], NE * nb * 16)

            def experts_phase(l):
                t0, tiles = LT[l]
                last_row = pool.alloc_register(f"last_row_{l}")
                for j in range(tiles):
                    pool.wait_ge(rows, ROWS_BEFORE[f"{l}b"] + j + 1)
                    t = t0 + j
                    pool.dma_start(h_rows[t * P:(t + 1) * P, :], hrow_moe[:, j % 2, :]).then_inc(rows_out[j % 2], 16)
                for i in range(2):
                    pool.wait_ge(rows_out[i], (32, 48)[l])
                for j in range(2):
                    ring.wait_full(pool, f"norm_{l}b", 2 * (tiles - 1 - j) + 1)

                def gather(e, u):
                    pool.wait_ge(slot_table, e + (NE * l + 1))
                    at_least(pool, E["xT_full", l], e - (XG - 1))
                    pool.reg_add(last_row, pool.zero_reg, NTOK - 1)
                    col_ = slot_u[:, e:e + 1] if isinstance(e, int) else slot_u[:, bass.ds(e, 1)]
                    nc.gpsimd.tensor_copy(gather_idx[:, u, :], col_).then_inc(E["gidx", l], 1)
                    pool.wait_ge(E["gidx", l], e + 1)
                    pool.reg_add(last_row, pool.zero_reg, NTOK - 1)
                    pool.indirect_dma_start(xg[:, u, :], None, h_rows,
                                            bass.IndirectOffsetOnAxis(gather_idx[:, u, :], 0),
                                            bounds_check=last_row).then_inc(E["xg_in", l, u], 16)

                for e in range(XG):
                    gather(e, e)
                with pool.Fori(1, NE // XG) as i4:
                    for r in range(XG):
                        gather(i4 * XG + r, r)
                for i in range(YB):
                    pool.wait_ge(E["stored", l, i], NE // YB * 16)

                def combine(blocks):
                    for k in range(4 * tiles):
                        n = (0, 4 * NT)[l] + k
                        if k >= 3 or l:
                            pool.wait_ge(combine_used, n - 2)
                        for j in range(2):
                            i = 2 * (k % 4) + j
                            pool.indirect_dma_start(combined[n % 3][:, j, :], None, y_rows[0:blocks * NE * P, :],
                                                    bass.IndirectOffsetOnAxis(combine_idx[:, t0 + k // 4, i:i + 1], 0),
                                                    bounds_check=blocks * NE * P - 1).then_inc(combine_in[n % 3], 16)

                pool.wait_ge(flag_ready, l + 1)
                more = pool.value_load(flags[0:1, l:l + 1], min_val=0, max_val=1)
                with pool.If(more > 0):
                    overflow_pool(l)
                    combine(tiles)
                with pool.If(more < 1):
                    combine(1)

            for items, s in ((filter_loads, filter_in), (moe_loads, moe_in)):
                for dst, src in items:
                    pool.dma_start(dst, src).then_inc(s, 16)
            experts_phase(0)
            experts_phase(1)


_INS = ['x', 'c', 'ctx', 'c_ctx', 'w_ada', 'b_ada', 'norm_mix', 'norm_ffn', 'ab_w_in', 'ab_w_out', 'ret_decay_logit',
        'hy_conv_w', 'hy_conv_b', 'hy_w1', 'hy_b1', 'hy_freq1', 'hy_w2', 'hy_b2', 'hy_freq2', 'hy_w3', 'hy_skip',
        'da_w_in', 'da_w_out', 'da_lambda', 'da_subln', 'router_w', 'router_b', 'exp_w_gate', 'exp_w_up', 'exp_w_down',
        'sh_w_gate', 'sh_w_up', 'sh_w_down', 'norm_final']


def kernel(**inputs):
    import numpy as _np
    import concourse.bacc as _bacc
    from concourse import mybir as _mybir
    from concourse.bass_utils import run_bass_kernel_spmd as _run

    nc = _bacc.Bacc("TRN2", target_bir_lowering=False, num_devices=1)
    arrays, A, K = {}, {}, {}
    for name in _INS:
        a = _np.ascontiguousarray(inputs[name])
        arrays[f"in_{name}"] = a
        A[name] = nc.dram_tensor(f"in_{name}", a.shape, _mybir.dt.from_np(a.dtype), kind="ExternalInput").ap()
    for name, a in shape_constants().items():
        a = _np.ascontiguousarray(a)
        arrays[f"const_{name}"] = a
        K[name] = nc.dram_tensor(f"const_{name}", a.shape, _mybir.dt.from_np(a.dtype), kind="ExternalInput").ap()
    out = nc.dram_tensor("out_0", (1, SEQ, D), F32, kind="ExternalOutput").ap()
    build(nc, A, K, out)
    r = _run(nc, [arrays], core_ids=[0])
    return r.results[0]["out_0"]
```
